# Optimizing a Trainium2 kernel written in Bass

```python
import jax
import jax.numpy as jnp
from jax import lax
import numpy as np

D_MODEL = 1024
BATCH = 1
SEQ = 512
DEPTH = 2

CHUNK = 64
NORM_EPS = 1e-6
MASK_VALUE = -1e30
MIN_FORGET = 1e-30

A_HEADS = 4
A_DK = 64
A_DV = 64
A_WIDTH = A_HEADS * A_DV

B_HEADS = 4
B_DK = 48
B_DV = 96
B_WIDTH = B_HEADS * B_DV
ROPE_BASE = 10000.0

C_HEADS = 6
C_DH = 64
C_WIDTH = C_HEADS * C_DH
N_PREV_CHUNKS = 8
MAX_REL = 128

D_MIX = A_WIDTH + B_WIDTH + C_WIDTH
IN_SIZES = (A_HEADS * A_DK, A_HEADS * A_DK, A_WIDTH, A_WIDTH,
            B_HEADS * B_DK, B_HEADS * B_DK, B_WIDTH, B_WIDTH,
            C_WIDTH, C_WIDTH, C_WIDTH)
D_IN = sum(IN_SIZES)

N_GROUPS = 4
EXPERTS_PER_GROUP = 8
N_EXPERTS = N_GROUPS * EXPERTS_PER_GROUP
TOP_K = 2
D_EXPERT = 512
MOE_BLOCK = 128

kernel_name = 'hybrid_hgrn2_retention_chunkattn_hiermoe'

def rmsnorm(x, w):
    xf = x.astype(jnp.float32)
    y = xf * lax.rsqrt(jnp.mean(xf * xf, axis=-1, keepdims=True) + NORM_EPS)
    return (y * w.astype(jnp.float32)).astype(x.dtype)

def hgrn2_mixer(q, f_logit, i, g, lb, norm_w):
    f32 = jnp.float32
    Bsz, S = q.shape[0], q.shape[1]
    nc = S // CHUNK
    lbh = lb.astype(f32).reshape(A_HEADS, A_DK)
    zf = f_logit.astype(f32)
    f = lbh + (1.0 - lbh) * jax.nn.sigmoid(zf)
    log_f = jnp.log(jnp.maximum(f, MIN_FORGET))
    k = (1.0 - lbh) * jax.nn.sigmoid(-zf)
    qf = jax.nn.silu(q.astype(f32)) * (A_DK ** -0.5)
    v = i.astype(f32)

    def to_chunks(t):
        return t.reshape(Bsz, nc, CHUNK, A_HEADS, t.shape[-1]).transpose(1, 0, 3, 2, 4)

    qc, kc, vc, lfc = to_chunks(qf), to_chunks(k), to_chunks(v), to_chunks(log_f)
    G = jnp.cumsum(lfc, axis=3)
    causal = jnp.tril(jnp.ones((CHUNK, CHUNK), dtype=bool))[None, None, :, :, None]

    def step(state, inp):
        qb, kb, vb, Gb = inp
        G_last = Gb[:, :, -1]
        inter = jnp.einsum('bhik,bhkv->bhiv', qb * jnp.exp(Gb), state)
        diff = Gb[:, :, :, None, :] - Gb[:, :, None, :, :]
        decay = jnp.where(causal, jnp.exp(jnp.minimum(diff, 0.0)), 0.0)
        scores = jnp.einsum('bhik,bhjk,bhijk->bhij', qb, kb, decay)
        intra = jnp.einsum('bhij,bhjv->bhiv', scores, vb)
        new_state = (jnp.exp(G_last)[..., None] * state
                     + jnp.einsum('bhjk,bhjv->bhkv', kb * jnp.exp(G_last[:, :, None] - Gb), vb))
        return new_state, inter + intra

    s0 = jnp.zeros((Bsz, A_HEADS, A_DK, A_DV), f32)
    _, o = lax.scan(step, s0, (qc, kc, vc, G))
    o = o.transpose(1, 0, 3, 2, 4).reshape(Bsz, S, A_WIDTH)
    o = rmsnorm(o, norm_w) * jax.nn.silu(g.astype(f32))
    return o.astype(g.dtype)

def rotary(t, pos):
    half = t.shape[-1] // 2
    inv_freq = ROPE_BASE ** (-jnp.arange(half, dtype=jnp.float32) / half)
    ang = pos.astype(jnp.float32)[:, None] * inv_freq[None, :]
    cos = jnp.cos(ang)[None, :, None, :]
    sin = jnp.sin(ang)[None, :, None, :]
    t1, t2 = t[..., :half], t[..., half:]
    return jnp.concatenate([t1 * cos - t2 * sin, t1 * sin + t2 * cos], axis=-1)

def retention_mixer(q, k, v, g, norm_w):
    f32 = jnp.float32
    Bsz, S = q.shape[0], q.shape[1]
    nc = S // CHUNK
    pos = jnp.arange(S)
    qf = rotary(q.astype(f32), pos)
    kf = rotary(k.astype(f32), pos) * (B_DK ** -0.5)
    vf = v.astype(f32)
    log_gamma = jnp.log1p(-jnp.exp2(-5.0 - jnp.arange(B_HEADS, dtype=f32)))

    def to_chunks(t):
        return t.reshape(Bsz, nc, CHUNK, B_HEADS, t.shape[-1]).transpose(0, 3, 1, 2, 4)

    qc, kc, vc = to_chunks(qf), to_chunks(kf), to_chunks(vf)
    idx = jnp.arange(CHUNK, dtype=f32)
    rel = idx[:, None] - idx[None, :]
    decay = jnp.where(rel >= 0, jnp.exp(log_gamma[:, None, None] * jnp.maximum(rel, 0.0)), 0.0)
    scores = jnp.einsum('bhnid,bhnjd->bhnij', qc, kc) * decay[None, :, None]
    intra = jnp.einsum('bhnij,bhnjv->bhniv', scores, vc)
    k_decay = jnp.exp(log_gamma[:, None] * (CHUNK - 1.0 - idx)[None, :])
    q_decay = jnp.exp(log_gamma[:, None] * (idx + 1.0)[None, :])
    chunk_gamma = jnp.exp(log_gamma * CHUNK)
    U = jnp.einsum('bhnjd,hj,bhnjv->nbhdv', kc, k_decay, vc)

    def step(state, u):
        return chunk_gamma[None, :, None, None] * state + u, state

    s0 = jnp.zeros((Bsz, B_HEADS, B_DK, B_DV), f32)
    _, s_prev = lax.scan(step, s0, U)
    inter = jnp.einsum('bhnid,hi,nbhdv->bhniv', qc, q_decay, s_prev)
    o = (intra + inter).transpose(0, 2, 3, 1, 4).reshape(Bsz, S, B_HEADS, B_DV)
    mu = jnp.mean(o, axis=-1, keepdims=True)
    var = jnp.mean(jnp.square(o - mu), axis=-1, keepdims=True)
    o = ((o - mu) * lax.rsqrt(var + NORM_EPS)).reshape(Bsz, S, B_WIDTH)
    o = o * norm_w.astype(f32) * jax.nn.silu(g.astype(f32))
    return o.astype(g.dtype)

def chunk_attention_mixer(q, k, v, rel_bias):
    f32 = jnp.float32
    Bsz, S = q.shape[0], q.shape[1]
    nc = S // CHUNK
    W = N_PREV_CHUNKS + 1
    qc = q.reshape(Bsz, nc, CHUNK, C_HEADS, C_DH)
    pad = ((0, 0), (N_PREV_CHUNKS, 0), (0, 0), (0, 0), (0, 0))
    kp = jnp.pad(k.reshape(Bsz, nc, CHUNK, C_HEADS, C_DH), pad)
    vp = jnp.pad(v.reshape(Bsz, nc, CHUNK, C_HEADS, C_DH), pad)
    kb = jnp.concatenate([kp[:, w:w + nc] for w in range(W)], axis=2)
    vb = jnp.concatenate([vp[:, w:w + nc] for w in range(W)], axis=2)
    qi = jnp.arange(CHUNK)[:, None]
    km = jnp.arange(W * CHUNK)[None, :]
    dist = N_PREV_CHUNKS * CHUNK + qi - km
    bias = rel_bias[:, jnp.clip(dist, -MAX_REL, MAX_REL) + MAX_REL]
    valid = (jnp.arange(nc)[:, None] - N_PREV_CHUNKS + km // CHUNK) >= 0
    s = (jnp.einsum('bnihd,bnjhd->bhnij', qc, kb).astype(f32) * (C_DH ** -0.5)
         + bias[None, :, None].astype(f32))
    s = jnp.where(valid[None, None, :, None, :], s, MASK_VALUE)
    p = jax.nn.softmax(s, axis=-1).astype(v.dtype)
    o = jnp.einsum('bhnij,bnjhd->bnihd', p, vb)
    return o.reshape(Bsz, S, C_WIDTH)

def hier_moe(h, w_group, w_expert, w_gate, w_up, w_down):
    f32 = jnp.float32
    Bsz, S, D = h.shape
    T = Bsz * S
    x = h.reshape(T, D)
    g_logits = (x @ w_group).astype(f32)
    grp = jnp.argmax(g_logits, axis=-1)
    p_grp = jnp.take_along_axis(jax.nn.softmax(g_logits, axis=-1), grp[:, None], axis=-1)
    e_logits = (x @ w_expert).astype(f32).reshape(T, N_GROUPS, EXPERTS_PER_GROUP)
    e_logits = jnp.take_along_axis(e_logits, grp[:, None, None], axis=1)[:, 0]
    top_v, top_i = lax.top_k(e_logits, TOP_K)
    gates = jax.nn.softmax(top_v, axis=-1) * p_grp
    eid = grp[:, None] * EXPERTS_PER_GROUP + top_i

    A = T * TOP_K
    flat_e = eid.reshape(A)
    flat_t = jnp.arange(A, dtype=jnp.int32) // TOP_K
    flat_w = gates.reshape(A)
    order = jnp.argsort(flat_e)
    se = flat_e[order]
    counts = jnp.bincount(flat_e, length=N_EXPERTS)
    padded = (counts + MOE_BLOCK - 1) // MOE_BLOCK * MOE_BLOCK
    pad_end = jnp.cumsum(padded)
    pad_start = pad_end - padded
    start = jnp.cumsum(counts) - counts
    dest = pad_start[se] + jnp.arange(A) - start[se]
    P = (-(-A // MOE_BLOCK) + N_EXPERTS) * MOE_BLOCK
    NB = P // MOE_BLOCK
    slot_tok = jnp.full((P,), T, dtype=jnp.int32).at[dest].set(flat_t[order])
    slot_w = jnp.zeros((P,), f32).at[dest].set(flat_w[order])
    blk_exp = jnp.minimum(jnp.searchsorted(pad_end, jnp.arange(NB) * MOE_BLOCK, side='right'),
                          N_EXPERTS - 1)
    xpad = jnp.concatenate([x, jnp.zeros((1, D), x.dtype)], axis=0)
    xs = xpad[slot_tok].reshape(NB, MOE_BLOCK, D)

    def expert_block(args):
        xb, e = args
        hb = jax.nn.silu(xb @ w_gate[e]) * (xb @ w_up[e])
        return hb @ w_down[e]

    ys = lax.map(expert_block, (xs, blk_exp)).reshape(P, D)
    ys = ys * slot_w[:, None].astype(ys.dtype)
    out = jnp.zeros((T + 1, D), ys.dtype).at[slot_tok].add(ys)[:T]
    return out.reshape(Bsz, S, D)

def setup_inputs(seed: int = 0) -> dict:
    key = jax.random.key(seed)
    ks = jax.random.split(key, 16)
    f32 = jnp.float32

    def nrm(k, shape, scale):
        return jax.random.normal(k, shape, f32) * scale

    return {
        'x': nrm(ks[0], (BATCH, SEQ, D_MODEL), 1.0),
        'w_in': nrm(ks[1], (DEPTH, D_MODEL, D_IN), D_MODEL ** -0.5),
        'w_out': nrm(ks[2], (DEPTH, D_MIX, D_MODEL), D_MIX ** -0.5),
        'norm_mix': 1.0 + nrm(ks[3], (DEPTH, D_MODEL), 0.02),
        'norm_ffn': 1.0 + nrm(ks[4], (DEPTH, D_MODEL), 0.02),
        'norm_final': 1.0 + nrm(ks[5], (D_MODEL,), 0.02),
        'hgrn_lb': nrm(ks[6], (DEPTH, A_HEADS * A_DK), 1.0),
        'hgrn_norm': 1.0 + nrm(ks[7], (DEPTH, A_WIDTH), 0.02),
        'ret_norm': 1.0 + nrm(ks[8], (DEPTH, B_WIDTH), 0.02),
        'rel_bias': nrm(ks[9], (C_HEADS, 2 * MAX_REL + 1), 0.2),
        'router_group': nrm(ks[10], (DEPTH, D_MODEL, N_GROUPS), D_MODEL ** -0.5),
        'router_expert': nrm(ks[11], (DEPTH, D_MODEL, N_EXPERTS), D_MODEL ** -0.5),
        'expert_w_gate': nrm(ks[12], (DEPTH, N_EXPERTS, D_MODEL, D_EXPERT), D_MODEL ** -0.5),
        'expert_w_up': nrm(ks[13], (DEPTH, N_EXPERTS, D_MODEL, D_EXPERT), D_MODEL ** -0.5),
        'expert_w_down': nrm(ks[14], (DEPTH, N_EXPERTS, D_EXPERT, D_MODEL), D_EXPERT ** -0.5),
    }

def reference(x, w_in, w_out, norm_mix, norm_ffn, norm_final, hgrn_lb, hgrn_norm, ret_norm,
              rel_bias, router_group, router_expert, expert_w_gate, expert_w_up, expert_w_down):
    f32 = jnp.float32
    Bsz, S = x.shape[0], x.shape[1]
    p = jax.nn.softmax(hgrn_lb.astype(f32), axis=0)
    lower_bounds = jnp.clip(jnp.cumsum(p, axis=0) - p[0], 0.0, 1.0)
    split_at = np.cumsum(IN_SIZES)[:-1].tolist()

    def heads(t, n):
        return t.reshape(Bsz, S, n, -1)

    for l in range(DEPTH):
        h = rmsnorm(x, norm_mix[l])
        z = h @ w_in[l]
        aq, af, ai, ag, bq, bk, bv, bg, cq, ck, cv = jnp.split(z, split_at, axis=-1)
        ya = hgrn2_mixer(heads(aq, A_HEADS), heads(af, A_HEADS), heads(ai, A_HEADS), ag,
                         lower_bounds[l], hgrn_norm[l])
        yb = retention_mixer(heads(bq, B_HEADS), heads(bk, B_HEADS), heads(bv, B_HEADS), bg, ret_norm[l])
        yc = chunk_attention_mixer(heads(cq, C_HEADS), heads(ck, C_HEADS), heads(cv, C_HEADS), rel_bias)
        x = x + jnp.concatenate([ya, yb, yc], axis=-1) @ w_out[l]
        h = rmsnorm(x, norm_ffn[l])
        x = x + hier_moe(h, router_group[l], router_expert[l], expert_w_gate[l],
                         expert_w_up[l], expert_w_down[l])
    return rmsnorm(x, norm_final)


_drawn_inputs = setup_inputs


def setup_inputs(seed=0):
    import zlib

    import numpy as np

    out = dict(_drawn_inputs(seed))
    spreads = {}
    factors = {}
    for name, (base, spread) in spreads.items():
        noise = np.random.default_rng([zlib.crc32(name.encode()), seed]).standard_normal(out[name].shape)
        drawn = base * np.exp(spread * noise) if base else spread * noise
        out[name] = jnp.asarray(drawn.astype(out[name].dtype))
    for name, factor in factors.items():
        out[name] = (out[name] * factor).astype(out[name].dtype)
    return out
```

```python
from contextlib import ExitStack

import numpy as np
import concourse.bass as bass
from concourse import mybir

F32 = mybir.dt.float32
F32R = mybir.dt.float32r
I32 = mybir.dt.int32
U32 = mybir.dt.uint32
U8 = mybir.dt.uint8
ALU = mybir.AluOpType
ACT = mybir.ActivationFunctionType
AX = mybir.AxisListType

P = 128
DEPTH, D, S = 2, 1024, 512
TT = S // P
KT = D // P
EPS = 1e-6
NEG = -1e30
MIN_FORGET = 1e-30

A_H, A_DK = 4, 64
AW = A_H * A_DK
B_H, B_DK, B_DV = 4, 48, 96
BW = B_H * B_DV
HALF = B_DK // 2
C_H, C_DH = 6, 64
CW = C_H * C_DH
CHUNK, MAX_REL = 64, 128
ROPE_BASE = 10000.0
D_IN = 4 * AW + 2 * B_H * B_DK + 2 * BW + 3 * CW

NG, EPG = 4, 8
NE = NG * EPG
DE = 512
FT = DE // P
CAP = 64
PAIRS = NE // 2
MAX_ROUNDS = S // CAP

LEVELS = 7

_o = np.cumsum([0, AW, AW, AW, AW, B_H * B_DK, B_H * B_DK, BW, BW, CW, CW, CW]).tolist()
GROUPS = [
    ("aq_af", _o[0], 2 * AW, True),
    ("ai_ag", _o[2], 2 * AW, False),
    ("cq", _o[8], CW, True),
    ("ck", _o[9], CW, True),
    ("cv", _o[10], CW, False),
    ("bq_bk", _o[4], 2 * B_H * B_DK, False),
    ("bv", _o[6], BW, False),
    ("bg", _o[7], BW, False),
    ("out_lo", 0, D // 2, False),
    ("out_hi", D // 2, D // 2, False),
]
N_IN = 8
RING = 4


def tiles_of(g):
    return GROUPS[g][2] // P if GROUPS[g][3] else TT


def bank_fills(g, i):
    return sum(1 for k in range(g) if tiles_of(k) > i)


CONST = {}
_n = 0
for _name, _w in [("ident", 128), ("stack", CAP), ("causal", 128), ("before", 128), ("ones", 128),
                  ("rows", 128), ("token", TT), ("experts", NE), ("groups", NG), ("limits", MAX_ROUNDS)]:
    CONST[_name] = (_n, _n + _w)
    _n += _w
N_CONST = _n


def constants():
    c = np.zeros((P, N_CONST), np.float32)

    def put(name, a):
        c[:, CONST[name][0]:CONST[name][1]] = a.reshape(P, -1)

    i = np.arange(P)
    put("ident", np.eye(P))
    put("stack", np.concatenate([np.eye(CAP)] * 2))
    put("causal", (i[None, :] >= i[:, None]))
    put("before", (i[:, None] < i[None, :]))
    put("ones", np.ones((P, P)))
    put("rows", np.tile(np.arange(CAP), (P, 2)))
    put("token", i[:, None] + P * np.arange(TT)[None, :])
    put("experts", np.tile(np.arange(NE), (P, 1)))
    put("groups", np.tile(np.arange(NG), (P, 1)))
    put("limits", np.tile(CAP * (1 + np.arange(MAX_ROUNDS)), (P, 1)))
    pos = np.arange(S, dtype=np.float32)
    inv = (np.float32(ROPE_BASE) ** (-np.arange(HALF, dtype=np.float32) / np.float32(HALF))).astype(np.float32)
    ang = (pos[:, None] * inv[None, :]).astype(np.float32).astype(np.float64)
    lg = np.log1p(-np.exp2(-5.0 - np.arange(B_H)))
    gq = np.exp(lg[None, :] * pos[:, None].astype(np.float64))
    gk = np.exp(-lg[None, :] * pos[:, None].astype(np.float64)) * B_DK ** -0.5
    f = np.concatenate([gq, gk], axis=1)[:, :, None]
    trig = [(f * tr[:, None, :]).reshape(TT, P, 8, HALF).transpose(1, 0, 2, 3).reshape(P, -1)
            for tr in (np.cos(ang), np.sin(ang))]
    masks = np.zeros((P, LEVELS + 1, P), np.float32)
    j, q = i[:, None], i[None, :]
    for n in range(LEVELS):
        h = 1 << n
        masks[:, n] = (j // (2 * h) == q // (2 * h)) & (q % (2 * h) >= h) & (j % (2 * h) < h)
    masks[:, LEVELS] = j == q
    return c, np.concatenate(trig, axis=1).astype(np.float32), masks.reshape(P, -1)


class Side:

    def __init__(self):
        self.at, self.fills, self.signals = {}, [0] * 4, [0] * 4

    def add(self, key, bank, signalled=True):
        self.fills[bank] += 1
        self.signals[bank] += signalled
        self.at[key] = (bank, self.fills[bank], self.signals[bank])


N_SLOT = 8 * (N_IN - 1)
N_TAIL = 8


def slot(g, kt):
    return (g - 1) * KT + kt


LV0 = 5
A_LEVEL = LV0 + 2
A_KEYS, A_STATE, A_OUT = LV0 + 10, LV0 + 12, LV0 + 14
C0 = slot(5, 1)
C_ITEMS = [(t, h) for t in range(TT) for h in range(C_H)]
B_ROT = slot(6, 3)
B_QKT, B_SC, B_STATE, B_OUT = slot(6, 5), slot(6, 7), slot(7, 3), slot(7, 5)


def side_plan():
    s = Side()
    n = 0
    first = [("hT", i) for i in range(2 * TT)]
    first += [("level", lv, c) for lv in range(LEVELS + 1) for c in range(TT)]
    first += [("kdT", c) for c in range(TT - 1)] + [("aU", c) for c in range(TT - 1)]
    first += [("ao", c) for c in range(TT)]
    for n, key in enumerate(first):
        s.add(key, n % 4)
    n = 0
    for sl in range(C0, N_SLOT + N_TAIL):
        i = sl - C0
        keys = [("cT", i - 1)] if 0 <= i - 1 < len(C_ITEMS) else []
        keys += [("cs", i)] if 0 <= i < len(C_ITEMS) else []
        keys += [("bT", k) for k in range(4)] if sl == B_QKT else []
        keys += [("bs", c) for c in range(TT)] if sl == B_SC else []
        keys += [("bU", c) for c in range(TT - 1)] if sl == B_STATE else []
        keys += [("bo", c) for c in range(TT)] if sl == B_OUT else []
        for k in keys:
            s.add(k, n % 3)
            n += 1
        if 0 <= i - 2 < len(C_ITEMS) and C_ITEMS[i - 2][1] == 0:
            s.add(("co", C_ITEMS[i - 2][0]), 3, signalled=False)
    for i in range(2 * TT):
        s.add(("yT", i), i % 4)
    return s.at


def norm_square(act, x, squares, ssq, squares_done):
    for t in range(TT):
        act.activation(squares[:, t, :], x[:, t, :], ACT.Square,
                       accum_out=ssq[:, t:t + 1]).then_inc(squares_done, 1)


def norm_root(act, ssq, sem):
    act.wait_ge(sem["mean_ready"], 1)
    act.activation(ssq[:], ssq[:], ACT.Sqrt).then_inc(sem["root_ready"], 1)


def norm_scale(dve, link, x, xn, weight, ssq, sem):
    dve.wait_ge(sem["squares_done"], TT)
    dve.tensor_scalar(ssq[:], ssq[:], 1.0 / D, EPS, ALU.mult, ALU.add).then_inc(sem["mean_ready"], 1)
    dve.wait_ge(sem["root_ready"], 1)
    link(dve.reciprocal(ssq[:], ssq[:]))
    for t in range(TT):
        dve.scalar_tensor_tensor(xn[:, t, :], x[:, t, :], ssq[:, t:t + 1], weight, ALU.mult,
                                 ALU.mult).then_inc(sem["xn_ready"], 1)


def chain(eng, sem):
    n = [0]

    def link(ins):
        n[0] += 1
        ins.then_inc(sem, 1)
        eng.wait_ge(sem, n[0])
    return link


def spread(ap, n):
    return ap.rearrange("p (o a) -> p o a", o=1).broadcast_to([P, n, ap.shape[1]])


def each(ap, n):
    return ap.rearrange("p (a o) -> p a o", o=1).broadcast_to([P, ap.shape[1], n])


def head_rows(h, n=64):
    return slice(64 * (h % 2), 64 * (h % 2) + n)


def tile_cols(t, f=0):
    return slice(S * f + P * t, S * f + P * t + P)


def score_place(h, c):
    return 2 * (c // 2) + h % 2, slice(P * (2 * (c % 2) + h // 2), P * (2 * (c % 2) + h // 2) + P)


def mixer_block(nc, l, T, args, cst, sem):
    x, bias, pz, side = T["x"], T["bias"], T["pz"], T["side"]
    plan = side_plan()
    win = args["w_in"].rearrange("l (p k) n -> l p k n", k=KT)
    wout = args["w_out"].rearrange("l (p k) n -> l p k n", k=KT)
    with ExitStack() as ctx:
        def sb(name, shape, dt=F32):
            return ctx.enter_context(nc.sbuf_tensor(name, [P] + shape, dt))

        raw = sb("raw", [2, KT, 512])
        w_hi = sb("w_hi", [RING, 512], F32R)
        w_lo = sb("w_lo", [RING, 512], F32R)
        a_hi = sb("a_hi", [KT, S], F32R)
        a_lo = sb("a_lo", [KT, S], F32R)
        y = sb("y", [TT, D])
        junk = sb("junk", [AW])
        ssq = sb("ssq", [TT])
        norm_a = sb("norm_a", [AW])
        norm_b = sb("norm_b", [BW])
        lb = sb("lb", [2])
        omlb = sb("omlb", [2])
        glast = sb("glast", [2, TT])
        a_ms = sb("a_ms", [TT])
        b_mu = sb("b_mu", [TT * B_H])
        b_ms = sb("b_ms", [TT * B_H])
        nmax = sb("nmax", [len(C_ITEMS)])
        den = sb("den", [len(C_ITEMS)])
        rden = sb("rden", [len(C_ITEMS)])
        sa = sb("sa", [TT, 4 * P])

        arena = sb("arena", [16512])
        used = [0]

        def early(n):
            used[0] += n
            return arena[:, used[0] - n:used[0]]

        fa = early(2 * S)
        cum = early(2 * S)
        diff = [early(2 * S), early(2 * S)]
        qf = [early(2 * S), early(2 * S)]
        kf = [early(2 * S), early(2 * S)]
        qa = early(2 * S)
        ka = early(2 * S)
        aig = early(TT * 2 * AW).rearrange("p (t c) -> p t c", t=TT)
        kd = early(3 * AW).rearrange("p (t c) -> p t c", t=3)
        st_a = early(3 * AW).rearrange("p (t c) -> p t c", t=3)
        norm_w = arena[:, 15360:15360 + D]
        used[0] = 0
        cq = early(3 * S).rearrange("p (f t) -> p f t", f=3)
        ck = early(3 * S).rearrange("p (f t) -> p f t", f=3)
        cv = early(TT * CW).rearrange("p (t c) -> p t c", t=TT)
        pr = [early(S), early(S)]
        prT = [early(S), early(S)]
        zqk = early(TT * 8 * B_DK)
        rqk = early(TT * 8 * 64).rearrange("p (t h d) -> p t h d", t=TT, h=8)
        qkT = early(4 * S).rearrange("p (f t) -> p f t", f=4)
        bv = early(TT * BW).rearrange("p (t c) -> p t c", t=TT)
        trig = early(2 * TT * 8 * HALF)
        bg = trig.rearrange("p (t c) -> p t c", t=TT)
        st_b = early(3 * BW).rearrange("p (t c) -> p t c", t=3)

        block = ctx.enter_context(nc.Block())

        def evacuated(eng, g):
            for i in range(tiles_of(g)):
                eng.wait_ge(sem[f"pz_free{i}"], bank_fills(g, i) + 1)

        def was_read(eng, key):
            bank, nth, _ = plan[key]
            eng.wait_ge(sem[f"side_free{bank}"], nth)

        def filled(eng, key):
            bank, _, nth = plan[key]
            eng.wait_ge(sem[f"side_full{bank}"], nth)
            return side[bank], sem[f"side_free{bank}"]

        def add_out(dve, g):
            dve.wait_ge(sem["unit_done"], KT * (g + 1))
            col = GROUPS[g][1]
            for i in range(TT):
                xs = x[:, i, col:col + 512]
                dve.tensor_tensor(xs, xs, pz[i][:], ALU.add).then_inc(sem[f"pz_free{i}"], 1)

        @block.sync
        def _(sp):
            sp.dma_start(norm_w, args["norm_mix"][l].partition_broadcast(P)).then_inc(sem["small"], 16)
            sp.dma_start(norm_a[:], args["hgrn_norm"][l].partition_broadcast(P)).then_inc(sem["small"], 16)
            sp.dma_start(norm_b[:], args["ret_norm"][l].partition_broadcast(P)).then_inc(sem["small"], 16)
            sp.dma_start(lb[:], T["lb_dram"][l]).then_inc(sem["small"], 16)
            for g, (_, col, width, _) in enumerate(GROUPS):
                if g >= 2:
                    sp.wait_ge(sem["lo_split"], KT * (g - 1))
                src = win[l, :, :, col:col + width] if g < N_IN else wout[l, :, :, col:col + width]
                sp.dma_start(raw[:, g % 2, :, 0:width], src).then_inc(sem[f"raw{g % 2}"], 16)
                if g == 2:
                    sp.dma_start(trig, args["trig"]).then_inc(sem["trig"], 16)

        @block.gpsimd
        def _(pool):
            pool.memset(st_a, 0.0)
            pool.memset(sa[:], 0.0).then_inc(sem["zeroed"], 1)
            for c in range(TT):
                pool.wait_ge(sem[f"side_full{plan[('ao', c)][0]}"], plan[("ao", c)][2])
            pool.memset(st_b, 0.0)
            pool.memset(rqk, 0.0).then_inc(sem["zeroed"], 1)

        @block.tensor
        def _(pe):
            ident = cst("ident")

            def fill(key):
                bank, nth, _ = plan[key]
                if nth > 1:
                    pe.wait_ge(sem[f"side_free{bank}"], nth - 1)
                return side[bank], sem[f"side_full{bank}"]

            def turn_rows(name, i):
                t, half = i // 2, i % 2
                out, full = fill((name, i))
                for k in range(4):
                    last = pe.transpose(out[:, P * k:P * k + P],
                                        y[:, t, :].rearrange("p (f k) -> p k f", k=KT)[:, 4 * half + k, :], ident)
                last.then_inc(full, 1)

            def unit(g, kt):
                u = g * KT + kt
                _, _, width, feature_major = GROUPS[g]
                pe.wait_ge(sem["lo_split"], u + 1)
                wh, wl = w_hi[:, u % RING, :], w_lo[:, u % RING, :]
                ah, al = a_hi[:, kt, :], a_lo[:, kt, :]
                for i in range(tiles_of(g)):
                    if kt == 0 and bank_fills(g, i):
                        pe.wait_ge(sem[f"pz_free{i}"], bank_fills(g, i))
                    c = slice(P * i, P * i + P)
                    if feature_major:
                        parts = [(wh[:, c], ah), (wh[:, c], al), (wl[:, c], ah)]
                        out = pz[i][:]
                    else:
                        parts = [(ah[:, c], wh[:, 0:width]), (ah[:, c], wl[:, 0:width]), (al[:, c], wh[:, 0:width])]
                        out = pz[i][:, 0:width]
                    for n, (a, b) in enumerate(parts):
                        last = pe.matmul(out, a, b, start=(kt == 0 and n == 0), stop=(kt == KT - 1 and n == 2))
                last.then_inc(sem["unit_done"], 1)

            def level(n):
                if n < LEVELS:
                    pe.wait_ge(sem["factors"], n + 1)
                k_, q_ = (kf[n % 2], qf[n % 2]) if n < LEVELS else (ka, qa)
                for k in range(4):
                    out, full = fill(("level", n, k))
                    for c in (2 * (k // 2), 2 * (k // 2) + 1):
                        for h in range(k % 2, A_H, 2):
                            r, cols = head_rows(h), tile_cols(c, h // 2)
                            last = pe.matmul(out[:, score_place(h, c)[1]], k_[r, cols], q_[r, cols],
                                             start=True, stop=True)
                    last.then_inc(full, 1)

            def turn_keys():
                pe.wait_ge(sem["factors"], LEVELS + 1)
                for c in range(TT - 1):
                    out, full = fill(("kdT", c))
                    for f in range(2):
                        last = pe.transpose(out[:, P * f:P * f + P], kf[1][:, tile_cols(c, f)], ident)
                    last.then_inc(full, 1)

            def update_a():
                evacuated(pe, 1)
                for c in range(TT - 1):
                    was_read(pe, ("kdT", c))
                    out, full = fill(("aU", c))
                    for f in range(2):
                        v = slice(P * f, P * f + P)
                        last = pe.matmul(out[:, v], kd[:, c, v], aig[:, c, v], start=True, stop=True)
                    last.then_inc(full, 1)

            def out_a():
                for c in range(TT):
                    for h in range(2):
                        was_read(pe, ("level", LEVELS, score_place(h, c)[0]))
                    if c:
                        was_read(pe, ("aU", c - 1))
                    out, full = fill(("ao", c))
                    for h in range(A_H):
                        if c and h % 2 == 0:
                            v = slice(64 * h, 64 * h + P)
                            pe.matmul(out[:, v], qf[1][:, tile_cols(c, h // 2)], st_a[:, c - 1, v],
                                      start=True, stop=False)
                        v = slice(64 * h, 64 * h + 64)
                        k, cols = score_place(h, c)
                        last = pe.matmul(out[:, v], sa[:, k, cols], aig[:, c, v], start=(c == 0),
                                         stop=(c == 0 or h % 2 == 1))
                    last.then_inc(full, 1)

            def turn_b():
                pe.wait_ge(sem["rotated"], 1)
                for k in range(4):
                    out, full = fill(("bT", k))
                    for t in range(TT):
                        last = pe.transpose(out[:, P * t:P * t + P],
                                            rqk[:, t, 2 * k:2 * k + 2, :].rearrange("p a b -> p (a b)"), ident)
                    last.then_inc(full, 1)

            def scores_b():
                for k in range(4):
                    was_read(pe, ("bT", k))
                for k in range(4):
                    out, full = fill(("bs", k))
                    for c in (2 * (k // 2), 2 * (k // 2) + 1):
                        for h in range(k % 2, B_H, 2):
                            r = head_rows(h, B_DK)
                            last = pe.matmul(out[:, score_place(h, c)[1]], qkT[r, 2 + h // 2, tile_cols(c)],
                                             qkT[r, h // 2, tile_cols(c)], start=True, stop=True)
                    last.then_inc(full, 1)

            def update_b():
                evacuated(pe, 6)
                for c in range(TT - 1):
                    out, full = fill(("bU", c))
                    for k in range(2):
                        v = slice(2 * B_DV * k, 2 * B_DV * (k + 1))
                        last = pe.matmul(out[:, v], rqk[:, c, 4 + 2 * k:6 + 2 * k, :].rearrange("p a b -> p (a b)"),
                                         bv[:, c, v], start=True, stop=True)
                    last.then_inc(full, 1)

            def out_b():
                for c in range(TT):
                    for h in range(2):
                        was_read(pe, ("bs", score_place(h, c)[0]))
                    if c:
                        was_read(pe, ("bU", c - 1))
                    out, full = fill(("bo", c))
                    for h in range(B_H):
                        if c and h % 2 == 0:
                            v = slice(B_DV * h, B_DV * (h + 2))
                            pe.matmul(out[:, v], qkT[:, h // 2, tile_cols(c)], st_b[:, c - 1, v],
                                      start=True, stop=False)
                        v = slice(B_DV * h, B_DV * (h + 1))
                        k, cols = score_place(h, c)
                        last = pe.matmul(out[:, v], sa[:, k, cols], bv[:, c, v], start=(c == 0),
                                         stop=(c == 0 or h % 2 == 1))
                    last.then_inc(full, 1)

            def attend_turn(i):
                t, h = C_ITEMS[i]
                pe.wait_ge(sem["exp_done"], i + 1)
                out, full = fill(("cT", i))
                for j in range(t + 1):
                    last = pe.transpose(out[:, P * j:P * j + P], pr[i % 2][:, P * j:P * j + P], ident)
                last.then_inc(full, 1)

            def attend_scores(i):
                t, h = C_ITEMS[i]
                if i == 0:
                    evacuated(pe, 2)
                    evacuated(pe, 3)
                r = head_rows(h)
                out, full = fill(("cs", i))
                pe.matmul(out[:, 0:P * (t + 1)], cq[r, h // 2, tile_cols(t)], ck[r, h // 2, 0:P * (t + 1)],
                          start=True, stop=True).then_inc(full, 1)

            def attend_values(i):
                t, h = C_ITEMS[i]
                if i == 0:
                    evacuated(pe, 4)
                was_read(pe, ("cT", i))
                if h == 0:
                    fill(("co", t))
                for j in range(t + 1):
                    last = pe.matmul(side[3][:, 64 * h:64 * h + 64], prT[i % 2][:, P * j:P * j + P],
                                     cv[:, j, 64 * h:64 * h + 64], start=(j == 0), stop=(j == t))
                last.then_inc(sem["pv_done"], 1)

            def side_work(sl):
                if 0 <= sl - A_LEVEL <= LEVELS:
                    level(sl - A_LEVEL)
                if sl == A_KEYS:
                    turn_keys()
                if sl == A_STATE:
                    update_a()
                if sl == A_OUT:
                    out_a()
                i = sl - C0
                if 0 <= i - 1 < len(C_ITEMS):
                    attend_turn(i - 1)
                if 0 <= i < len(C_ITEMS):
                    attend_scores(i)
                if sl == B_QKT:
                    turn_b()
                if sl == B_SC:
                    scores_b()
                if sl == B_STATE:
                    update_b()
                if sl == B_OUT:
                    out_b()
                if 0 <= i - 2 < len(C_ITEMS):
                    attend_values(i - 2)

            for i in range(2 * TT):
                pe.wait_ge(sem["xn_ready"], i // 2 + 1)
                turn_rows("hT", i)
            for i in range(2 * TT):
                was_read(pe, ("hT", i))
            for g in range(N_IN):
                for kt in range(KT):
                    unit(g, kt)
                    if g:
                        side_work(slot(g, kt))
            for sl in range(N_SLOT, N_SLOT + N_TAIL):
                side_work(sl)
            pe.wait_ge(sem["y_ready"], 2)
            was_read(pe, ("co", TT - 1))
            for i in range(2 * TT):
                turn_rows("yT", i)
            for i in range(2 * TT):
                was_read(pe, ("yT", i))
            for g in range(N_IN, len(GROUPS)):
                for kt in range(KT):
                    unit(g, kt)

        @block.scalar
        def _(act):
            link = chain(act, sem["act_chain"])

            def hi_rows(name, i):
                t, half = i // 2, i % 2
                src, _ = filled(act, (name, i))
                act.copy(a_hi[:, 4 * half:4 * half + 4, tile_cols(t)],
                         src[:].rearrange("p (k t) -> p k t", k=4)).then_inc(sem["aT_hi"], 1)

            def split(g, kt):
                u, width = g * KT + kt, GROUPS[g][2]
                if kt == 0:
                    act.wait_ge(sem[f"raw{g % 2}"], 16 * (g // 2 + 1))
                if u >= RING:
                    act.wait_ge(sem["unit_done"], u - RING + 1)
                act.copy(w_hi[:, u % RING, 0:width], raw[:, g % 2, kt, 0:width]).then_inc(sem["hi_split"], 1)

            def evacuate(g):
                name = GROUPS[g][0]
                act.wait_ge(sem["unit_done"], KT * (g + 1))
                free = [sem[f"pz_free{i}"] for i in range(4)]
                if name == "aq_af":
                    for i in range(2):
                        act.activation(qa[:, S * i:S * i + S], pz[i][:], ACT.Silu).then_inc(free[i], 1)
                    for i in range(2):
                        act.activation(ka[:, S * i:S * i + S], pz[2 + i][:], ACT.Sigmoid, scale=-1.0)
                        act.activation(fa[:, S * i:S * i + S], pz[2 + i][:], ACT.Sigmoid).then_inc(free[2 + i], 1)
                if name == "ai_ag":
                    for i in range(TT):
                        act.copy(aig[:, i, 0:AW], pz[i][:, 0:AW])
                        act.activation(aig[:, i, AW:2 * AW], pz[i][:, AW:2 * AW], ACT.Silu).then_inc(free[i], 1)
                if name == "cq":
                    act.wait_ge(sem["factors"], LEVELS + 1)
                    for i in range(3):
                        act.mul(cq[:, i, :], pz[i][:], -C_DH ** -0.5).then_inc(free[i], 1)
                if name == "ck":
                    for c in range(TT):
                        was_read(act, ("ao", c))
                    for i in range(3):
                        act.copy(ck[:, i, :], pz[i][:]).then_inc(free[i], 1)
                if name == "cv":
                    for i in range(TT):
                        act.copy(cv[:, i, :], pz[i][:, 0:CW]).then_inc(free[i], 1)
                if name == "bq_bk":
                    for i in range(TT):
                        act.copy(zqk[:, 384 * i:384 * i + 384], pz[i][:, 0:384]).then_inc(free[i], 1)
                if name == "bv":
                    for i in range(TT):
                        act.copy(bv[:, i, :], pz[i][:, 0:BW]).then_inc(free[i], 1)
                if name == "bg":
                    act.wait_ge(sem["rotated"], 1)
                    for i in range(TT):
                        act.activation(bg[:, i, :], pz[i][:, 0:BW], ACT.Silu).then_inc(free[i], 1)

            def side_work(sl):
                g, kt = sl // KT + 1, sl % KT
                if kt == 0 and g - 1 < N_IN:
                    evacuate(g - 1)
                if sl == 3:
                    act.wait_ge(sem["f_ready"], 1)
                    link(act.activation(fa, fa, ACT.Sqrt))
                    act.activation(fa, fa, ACT.Ln).then_inc(sem["log_ready"], 1)
                n = sl - LV0
                if 0 <= n <= LEVELS:
                    act.wait_ge(sem["diff_ready"], n + 1)
                    act.activation(diff[n % 2], diff[n % 2], ACT.Exp, scale=2.0).then_inc(sem["decay_ready"], 1)
                    if n == LEVELS:
                        act.wait_ge(sem["factors"], LEVELS)
                        act.activation(diff[0], cum, ACT.Exp, scale=2.0).then_inc(sem["decay_ready"], 1)
                        act.activation(glast[:], cum.rearrange("p (f c t) -> p f c t", f=2, c=TT)[:, :, :, P - 1],
                                       ACT.Exp, scale=2.0).then_inc(sem["decay_ready"], 1)
                if sl == A_KEYS + 1:
                    for c in range(TT - 1):
                        src, free = filled(act, ("kdT", c))
                        act.copy(kd[:, c, :], src[:, 0:AW]).then_inc(free, 1)
                if sl == A_OUT + 1:
                    for c in range(TT):
                        src, free = filled(act, ("ao", c))
                        act.copy(y[:, c, 0:AW], src[:, 0:AW]).then_inc(free, 1)
                    for c in range(TT):
                        was_read(act, ("ao", c))
                        link(act.activation(junk[:], y[:, c, 0:AW], ACT.Square, accum_out=a_ms[:, c:c + 1]))
                    act.sem_inc(sem["a_squares"], 1)
                if sl == A_OUT + 3:
                    act.wait_ge(sem["a_mean"], 1)
                    act.activation(a_ms[:], a_ms[:], ACT.Sqrt).then_inc(sem["a_root"], 1)
                i = sl - C0
                if 0 <= i - 1 < len(C_ITEMS):
                    n = P * (C_ITEMS[i - 1][0] + 1)
                    src, free = filled(act, ("cT", i - 1))
                    if i - 1 >= 2:
                        act.wait_ge(sem["pv_done"], i - 2)
                    act.copy(prT[(i - 1) % 2][:, 0:n], src[:, 0:n]).then_inc(free, 1)
                if 0 <= i < len(C_ITEMS):
                    n = P * (C_ITEMS[i][0] + 1)
                    was_read(act, ("cs", i))
                    act.activation(pr[i % 2][:, 0:n], pr[i % 2][:, 0:n], ACT.Exp, bias=nmax[:, i:i + 1],
                                   scale=-1.0, accum_out=den[:, i:i + 1]).then_inc(sem["exp_done"], 1)
                if sl == B_QKT:
                    act.wait_ge(sem["y_ready"], 1)
                    for k in range(4):
                        src, free = filled(act, ("bT", k))
                        act.copy(qkT[:, k, :], src[:]).then_inc(free, 1)
                if sl == B_OUT:
                    for c in range(TT):
                        src, free = filled(act, ("bo", c))
                        act.copy(y[:, c, AW:AW + BW], src[:, 0:BW]).then_inc(free, 1)
                if sl == N_SLOT + 1:
                    act.wait_ge(sem["b_mean"], 1)
                    act.activation(b_ms[:], b_ms[:], ACT.Sqrt).then_inc(sem["b_root"], 1)

            norm_square(act, x, y, ssq, sem["squares_done"])
            norm_root(act, ssq, sem)
            for i in range(2 * TT):
                hi_rows("hT", i)
            for g in range(N_IN):
                for kt in range(KT):
                    split(g, kt)
                    if g:
                        side_work(slot(g, kt))
            for sl in range(N_SLOT, N_SLOT + N_TAIL):
                side_work(sl)
            for i in range(2 * TT):
                hi_rows("yT", i)
            for g in range(N_IN, len(GROUPS)):
                for kt in range(KT):
                    split(g, kt)

        @block.vector
        def _(dve):
            link = chain(dve, sem["dve_chain"])
            ones = cst("ones")

            def lo_rows(name, i, n):
                t, half = i // 2, i % 2
                src, free = filled(dve, (name, i))
                dve.wait_ge(sem["aT_hi"], n + 1)
                cols = a_hi[:, 4 * half:4 * half + 4, tile_cols(t)]
                dve.tensor_tensor(a_lo[:, 4 * half:4 * half + 4, tile_cols(t)],
                                  src[:].rearrange("p (k t) -> p k t", k=4), cols, ALU.subtract).then_inc(free, 1)

            def split(g, kt):
                u, width = g * KT + kt, GROUPS[g][2]
                dve.wait_ge(sem["hi_split"], u + 1)
                dve.tensor_tensor(w_lo[:, u % RING, 0:width], raw[:, g % 2, kt, 0:width],
                                  w_hi[:, u % RING, 0:width], ALU.subtract).then_inc(sem["lo_split"], 1)

            def gates():
                evacuated(dve, 0)
                link(dve.tensor_scalar(qa, qa, A_DK ** -0.5, None, ALU.mult))
                for i in range(2):
                    c = slice(S * i, S * i + S)
                    link(dve.tensor_scalar(ka[:, c], ka[:, c], omlb[:, i:i + 1], None, ALU.mult))
                    link(dve.tensor_scalar(fa[:, c], fa[:, c], omlb[:, i:i + 1], lb[:, i:i + 1], ALU.mult, ALU.add))
                dve.tensor_scalar(fa, fa, MIN_FORGET, None, ALU.max).then_inc(sem["f_ready"], 1)

            def factors(n):
                dve.wait_ge(sem["decay_ready"], n + 1 if n < LEVELS else n + 3)
                if n >= 2:
                    filled(dve, ("level", n - 2, TT - 1))
                    dve.wait_ge(sem["factors"], n - 1)
                qd = diff[n % 2] if n < LEVELS else diff[0]
                link(dve.tensor_tensor(qf[n % 2], qa, qd, ALU.mult))
                dve.tensor_tensor(kf[n % 2], ka, diff[n % 2], ALU.mult).then_inc(sem["factors"], 1)

            def exponents(n):
                if n >= 2:
                    dve.wait_ge(sem["factors"], n - 1)
                out = diff[n % 2]
                if n == LEVELS:
                    src = cum.rearrange("p (b h) -> p b h", h=P)
                    dve.tensor_tensor(out.rearrange("p (b h) -> p b h", h=P),
                                      src[:, :, P - 1:P].broadcast_to([P, 2 * TT, P]), src,
                                      ALU.subtract).then_inc(sem["diff_ready"], 1)
                    return
                h = 1 << n
                src = cum.rearrange("p (b h) -> p b h", h=2 * h)
                out = out.rearrange("p (b h) -> p b h", h=2 * h)
                ref = src[:, :, h - 1:h].broadcast_to([P, S // h, h])
                link(dve.tensor_tensor(out[:, :, h:2 * h], src[:, :, h:2 * h], ref, ALU.subtract))
                dve.tensor_tensor(out[:, :, 0:h], ref, src[:, :, 0:h], ALU.subtract).then_inc(sem["diff_ready"], 1)

            def place(n):
                mask = T["masks"][:, P * n:P * n + P]
                for c in range(TT):
                    src, free = filled(dve, ("level", n, c))
                    if n:
                        was_read(dve, ("level", n - 1, c))
                    dve.copy_predicated(sa[:, c, :].rearrange("p (h q) -> p h q", h=A_H), spread(mask, A_H),
                                        src[:].rearrange("p (h q) -> p h q", h=A_H)).then_inc(free, 1)

            def states_a():
                for c in range(TT - 1):
                    src, free = filled(dve, ("aU", c))
                    if c:
                        was_read(dve, ("aU", c - 1))
                    for h in range(A_H):
                        r, v = head_rows(h), slice(64 * h, 64 * h + 64)
                        if c == 0:
                            last = dve.tensor_copy(st_a[r, 0, v], src[r, v])
                        else:
                            last = dve.scalar_tensor_tensor(st_a[r, c, v], st_a[r, c - 1, v],
                                                            glast[r, h // 2, c:c + 1], src[r, v], ALU.mult, ALU.add)
                    last.then_inc(free, 1)

            def finish_a():
                dve.wait_ge(sem["a_root"], 1)
                link(dve.reciprocal(a_ms[:], a_ms[:]))
                for c in range(TT):
                    last = dve.scalar_tensor_tensor(y[:, c, 0:AW], y[:, c, 0:AW], a_ms[:, c:c + 1], norm_a[:],
                                                    ALU.mult, ALU.mult)
                link(last)
                dve.tensor_tensor(y[:, :, 0:AW], y[:, :, 0:AW], aig[:, :, AW:2 * AW],
                                  ALU.mult).then_inc(sem["y_ready"], 1)

            def rotate():
                evacuated(dve, 5)
                dve.wait_ge(sem["trig"], 16)
                dve.wait_ge(sem["zeroed"], 2)
                z = zqk.rearrange("p (t h d) -> p t h d", t=TT, d=B_DK)
                z1, z2 = z[:, :, :, 0:HALF], z[:, :, :, HALF:B_DK]
                n = TT * 8 * HALF
                cos = trig[:, 0:n].rearrange("p (t h d) -> p t h d", t=TT, d=HALF)
                sin = trig[:, n:2 * n].rearrange("p (t h d) -> p t h d", t=TT, d=HALF)
                t1, t2 = (y[:, :, AW + k:AW + k + 8 * HALF].rearrange("p t (h d) -> p t h d", d=HALF)
                          for k in (0, 8 * HALF))
                link(dve.tensor_tensor(t1, z1, cos, ALU.mult))
                link(dve.tensor_tensor(t2, z2, sin, ALU.mult))
                link(dve.tensor_tensor(rqk[:, :, :, 0:HALF], t1, t2, ALU.subtract))
                link(dve.tensor_tensor(t1, z1, sin, ALU.mult))
                link(dve.tensor_tensor(t2, z2, cos, ALU.mult))
                dve.tensor_tensor(rqk[:, :, :, HALF:B_DK], t1, t2, ALU.add).then_inc(sem["rotated"], 1)

            def mask_b():
                filled(dve, ("ao", TT - 1))
                for c in range(TT):
                    src, free = filled(dve, ("bs", c))
                    dve.tensor_tensor(sa[:, c, :].rearrange("p (h q) -> p h q", h=B_H),
                                      src[:].rearrange("p (h q) -> p h q", h=B_H), spread(cst("causal"), B_H),
                                      ALU.mult).then_inc(free, 1)

            def states_b():
                for c in range(TT - 1):
                    src, free = filled(dve, ("bU", c))
                    if c:
                        was_read(dve, ("bU", c - 1))
                    for h in range(B_H):
                        r, v = head_rows(h), slice(B_DV * h, B_DV * (h + 1))
                        if c == 0:
                            last = dve.tensor_copy(st_b[r, 0, v], src[r, v])
                        else:
                            last = dve.tensor_tensor(st_b[r, c, v], st_b[r, c - 1, v], src[r, v], ALU.add)
                    last.then_inc(free, 1)

            def norm_heads_b():
                for c in range(TT):
                    was_read(dve, ("bo", c))
                yb = y[:, :, AW:AW + BW].rearrange("p t (h d) -> p t h d", h=B_H)
                mu = b_mu[:].rearrange("p (t h o) -> p t h o", t=TT, o=1)
                sq = zqk.rearrange("p (a d) -> p a d", d=B_DV)
                link(dve.tensor_reduce(b_mu[:].rearrange("p (t h) -> p t h", t=TT), yb, AX.X, ALU.add))
                link(dve.tensor_scalar(b_mu[:], b_mu[:], 1.0 / B_DV, None, ALU.mult))
                link(dve.tensor_tensor(yb, yb, mu.broadcast_to([P, TT, B_H, B_DV]), ALU.subtract))
                link(dve.tensor_tensor(sq.rearrange("p (t h) d -> p t h d", t=TT), yb, yb, ALU.mult))
                link(dve.tensor_reduce(b_ms[:], sq, AX.X, ALU.add))
                dve.tensor_scalar(b_ms[:], b_ms[:], 1.0 / B_DV, EPS, ALU.mult, ALU.add).then_inc(sem["b_mean"], 1)

            def finish_b():
                dve.wait_ge(sem["b_root"], 1)
                link(dve.reciprocal(b_ms[:], b_ms[:]))
                yb = y[:, :, AW:AW + BW]
                rs = b_ms[:].rearrange("p (t h o) -> p t h o", t=TT, o=1)
                yh = yb.rearrange("p t (h d) -> p t h d", h=B_H)
                link(dve.tensor_tensor(yh, yh, rs.broadcast_to([P, TT, B_H, B_DV]), ALU.mult))
                link(dve.tensor_tensor(yb, yb, spread(norm_b[:], TT), ALU.mult))
                evacuated(dve, 7)
                dve.tensor_tensor(yb, yb, bg, ALU.mult).then_inc(sem["y_ready"], 1)

            def attend_max(i):
                t, h = C_ITEMS[i]
                n = P * (t + 1)
                src, free = filled(dve, ("cs", i))
                if i >= 2:
                    filled(dve, ("cT", i - 2))
                dve.tensor_tensor_reduce(pr[i % 2][:, 0:n], src[:, 0:n], bias[:, h, 512 - n:512], 1.0, 3.0e38,
                                         ALU.add, ALU.min, nmax[:, i:i + 1]).then_inc(free, 1)

            def finish_c(t):
                dve.wait_ge(sem["pv_done"], C_H * (t + 1))
                d = slice(C_H * t, C_H * t + C_H)
                link(dve.reciprocal(rden[:, d], den[:, d]))
                dve.tensor_tensor(y[:, t, AW + BW:D].rearrange("p (h d) -> p h d", h=C_H),
                                  side[3][:, 0:CW].rearrange("p (h d) -> p h d", h=C_H),
                                  each(rden[:, d], C_DH), ALU.mult).then_inc(sem["side_free3"], 1)

            def side_work(sl):
                if sl == 2:
                    gates()
                if sl == 4:
                    dve.wait_ge(sem["log_ready"], 1)
                    for c in range(2 * TT):
                        v = slice(P * c, P * c + P)
                        last = dve.tensor_tensor_scan(cum[:, v], ones, fa[:, v], 0.0, ALU.mult, ALU.add)
                    link(last)
                n = sl - LV0
                if 0 <= n - 1 <= LEVELS:
                    factors(n - 1)
                if 0 <= n <= LEVELS:
                    exponents(n)
                if 0 <= sl - A_LEVEL - 1 <= LEVELS:
                    if sl == A_LEVEL + 1:
                        dve.wait_ge(sem["zeroed"], 1)
                    place(sl - A_LEVEL - 1)
                if sl == A_STATE + 1:
                    states_a()
                if sl == A_OUT + 2:
                    dve.wait_ge(sem["a_squares"], 1)
                    dve.tensor_scalar(a_ms[:], a_ms[:], 1.0 / AW, EPS, ALU.mult, ALU.add).then_inc(sem["a_mean"], 1)
                if sl == A_OUT + 4:
                    finish_a()
                i = sl - C0
                if 0 <= i < len(C_ITEMS):
                    attend_max(i)
                if 0 <= i - 3 < len(C_ITEMS) and C_ITEMS[i - 3][1] == C_H - 1:
                    finish_c(C_ITEMS[i - 3][0])
                if sl == B_ROT:
                    rotate()
                if sl == B_SC:
                    mask_b()
                if sl == B_STATE:
                    states_b()
                if sl == B_OUT + 1:
                    norm_heads_b()
                if sl == N_SLOT + 3:
                    finish_b()

            dve.wait_ge(sem["small"], 64)
            link(dve.tensor_scalar(omlb[:], lb[:], -1.0, 1.0, ALU.mult, ALU.add))
            norm_scale(dve, link, x, y, norm_w, ssq, sem)
            for i in range(2 * TT):
                lo_rows("hT", i, i)
            for g in range(N_IN):
                for kt in range(KT):
                    split(g, kt)
                    if g:
                        side_work(slot(g, kt))
            for sl in range(N_SLOT, N_SLOT + N_TAIL):
                side_work(sl)
            for i in range(2 * TT):
                lo_rows("yT", i, 2 * TT + i)
            for g in range(N_IN, len(GROUPS)):
                for kt in range(KT):
                    split(g, kt)
                    if g > N_IN and kt == 2:
                        add_out(dve, g - 1)
            add_out(dve, len(GROUPS) - 1)


MIXER_SEMS = (["small", "raw0", "raw1", "trig", "lo_split", "hi_split", "unit_done", "zeroed", "factors",
               "squares_done", "mean_ready", "root_ready", "xn_ready", "aT_hi", "act_chain", 
               "dve_chain", "f_ready", "log_ready", "diff_ready", "decay_ready", "a_squares", "a_mean",
               "a_root", "b_mean", "b_root", "rotated", "y_ready", "exp_done", "pv_done"]
              + [f"pz_free{i}" for i in range(4)] + [f"side_full{i}" for i in range(4)]
              + [f"side_free{i}" for i in range(4)])


def router_block(nc, l, T, args, cst, sem):
    x, pz, side = T["x"], T["pz"], T["side"]
    with ExitStack() as ctx:
        def sb(name, shape, dt=F32):
            return ctx.enter_context(nc.sbuf_tensor(name, [P] + shape, dt))

        h = sb("h", [TT, D])
        hT = sb("hT", [KT, S])
        w_router = sb("w_router", [KT, NG + NE])
        ffn_w = sb("ffn_w", [D])
        ssq = sb("r_ssq", [TT])
        lg = sb("lg", [TT, 8])
        gtop = sb("gtop", [TT, 8])
        gtop_i = sb("gtop_i", [TT, 8], U32)
        gidx = sb("gidx", [TT])
        pgrp = sb("pgrp", [TT, NG])
        psum_ = sb("psum_", [TT])
        picked = sb("picked", [TT, NG])
        penalty = sb("penalty", [TT, NG])
        le = sb("le", [TT, NE])
        etop = sb("etop", [TT, 8])
        etop_i = sb("etop_i", [TT, 8], U32)
        e2 = sb("e2", [TT])
        both = sb("both", [TT, NE])
        cumr = sb("cumr", [TT, NE])
        prod = sb("prod", [TT * 2, NE])
        over = sb("over", [MAX_ROUNDS])
        most = sb("most", [2])
        one, gate, rank = T["one"], T["gate"], T["rank"]
        e_f = T["expert"]
        block = ctx.enter_context(nc.Block())

        @block.sync
        def _(sp):
            sp.dma_start(ffn_w[:], args["norm_ffn"][l].partition_broadcast(P)).then_inc(sem["small"], 16)
            sp.dma_start(w_router[:, :, 0:NG],
                         args["router_group"].rearrange("l (p k) n -> l p k n", k=KT)[l]).then_inc(sem["small"], 16)
            sp.dma_start(w_router[:, :, NG:NG + NE],
                         args["router_expert"].rearrange("l (p k) n -> l p k n", k=KT)[l]).then_inc(sem["small"], 16)
            for t in range(TT):
                sp.wait_ge(sem["xn_ready"], t + 1)
                sp.dma_start(T["h_dram"][P * t:P * t + P, :], h[:, t, :]).then_inc(sem["h_stored"], 16)
            sp.wait_ge(sem["h_stored"], 16 * TT)

        @block.tensor
        def _(pe):
            ident = cst("ident")
            for i in range(2 * TT):
                t, half = i // 2, i % 2
                pe.wait_ge(sem["xn_ready"], t + 1)
                if i >= 4:
                    pe.wait_ge(sem["hT_ready"], i - 3)
                for k in range(4):
                    last = pe.transpose(side[i % 4][:, P * k:P * k + P],
                                        h[:, t, :].rearrange("p (f k) -> p k f", k=KT)[:, 4 * half + k, :], ident)
                last.then_inc(sem["hT_turned"], 1)
            pe.wait_ge(sem["small"], 48)
            for t in range(TT):
                pe.wait_ge(sem["hT_ready"], 2 * t + 2)
                for kt in range(KT):
                    last = pe.matmul(pz[t][:, 0:NG + NE], hT[:, kt, tile_cols(t)], w_router[:, kt, :],
                                     start=(kt == 0), stop=(kt == KT - 1))
                last.then_inc(sem["logits"], 1)
            pe.wait_ge(sem["both_ready"], 1)
            for t in range(TT):
                for n in range(t + 1):
                    last = pe.matmul(side[0][:, NE * t:NE * t + NE], cst("before") if n == 0 else cst("ones"),
                                     both[:, t if n == 0 else n - 1, :], start=(n == 0), stop=(n == t))
            for n in range(TT):
                last = pe.matmul(side[1][:, 0:NE], cst("ones"), both[:, n, :], start=(n == 0), stop=(n == TT - 1))
            last.then_inc(sem["counted"], 1)

        @block.scalar
        def _(act):
            norm_square(act, x, h, ssq, sem["squares_done"])
            norm_root(act, ssq, sem)
            for i in range(2 * TT):
                t, half = i // 2, i % 2
                act.wait_ge(sem["hT_turned"], i + 1)
                act.copy(hT[:, 4 * half:4 * half + 4, tile_cols(t)],
                         side[i % 4][:].rearrange("p (k t) -> p k t", k=4)).then_inc(sem["hT_ready"], 1)
            act.wait_ge(sem["exp_args"], 1)
            act.activation(pgrp[:], pgrp[:], ACT.Exp).then_inc(sem["exps"], 1)
            act.wait_ge(sem["exp_args"], 2)
            act.activation(e2[:], e2[:], ACT.Exp).then_inc(sem["exps"], 1)

        @block.vector
        def _(dve):
            link = chain(dve, sem["dve_chain"])
            dve.wait_ge(sem["small"], 48)
            link(dve.memset(lg[:], NEG))
            norm_scale(dve, link, x, h, ffn_w[:], ssq, sem)
            for t in range(TT):
                dve.wait_ge(sem["logits"], t + 1)
                dve.tensor_copy(lg[:, t, 0:NG], pz[t][:, 0:NG])
                last = dve.tensor_copy(le[:, t, :], pz[t][:, NG:NG + NE])
            link(last)
            for t in range(TT):
                link(dve.max(gtop[:, t, :], lg[:, t, :]))
                last = dve.max_index(gtop_i[:, t, :], gtop[:, t, :], lg[:, t, :])
            link(last)
            link(dve.tensor_copy(gidx[:], gtop_i[:, :, 0]))
            dve.tensor_tensor(pgrp[:], lg[:, :, 0:NG], gtop[:, :, 0:1].broadcast_to([P, TT, NG]),
                              ALU.subtract).then_inc(sem["exp_args"], 1)
            link(dve.tensor_tensor(picked[:], spread(cst("groups"), TT), each(gidx[:], NG), ALU.is_equal))
            link(dve.tensor_scalar(penalty[:], picked[:], -1.0, -NEG, ALU.add, ALU.mult))
            lev = le[:].rearrange("p t (g e) -> p (t g) e", g=NG)
            link(dve.tensor_tensor(lev, lev, each(picked[:].rearrange("p t g -> p (t g)"), EPG), ALU.mult))
            link(dve.tensor_tensor(lev, lev, each(penalty[:].rearrange("p t g -> p (t g)"), EPG), ALU.add))
            for t in range(TT):
                link(dve.max(etop[:, t, :], le[:, t, :]))
                last = dve.max_index(etop_i[:, t, :], etop[:, t, :], le[:, t, :])
            link(last)
            dve.tensor_tensor(e2[:], etop[:, :, 1], etop[:, :, 0], ALU.subtract).then_inc(sem["exp_args"], 1)
            link(dve.tensor_copy(e_f[:], etop_i[:, :, 0:2]))
            link(dve.tensor_tensor(one[:], spread(cst("experts"), 2 * TT),
                                   each(e_f[:].rearrange("p t k -> p (t k)"), NE), ALU.is_equal))
            ov = one[:].rearrange("p (t k) e -> p t k e", k=2)
            dve.tensor_tensor(both[:], ov[:, :, 0, :], ov[:, :, 1, :], ALU.add).then_inc(sem["both_ready"], 1)
            for t in range(TT):
                last = dve.tensor_scalar(T["token_at"][:, 2 * t:2 * t + 2, :], one[:, 2 * t:2 * t + 2, :],
                                         cst("token")[:, t:t + 1], None, ALU.mult)
            link(last)
            dve.wait_ge(sem["exps"], 2)
            link(dve.tensor_reduce(psum_[:], pgrp[:], AX.X, ALU.add))
            link(dve.tensor_scalar(gidx[:], e2[:], 1.0, None, ALU.add))
            link(dve.tensor_tensor(psum_[:], psum_[:], gidx[:], ALU.mult))
            link(dve.reciprocal(gate[:, :, 0], psum_[:]))
            link(dve.tensor_tensor(gate[:, :, 1], gate[:, :, 0], e2[:], ALU.mult))
            dve.wait_ge(sem["counted"], 1)
            link(dve.tensor_copy(cumr[:].rearrange("p t e -> p (t e)"), side[0][:, 0:TT * NE]))
            for k in range(2):
                last = dve.tensor_tensor(prod[:].rearrange("p (t k) e -> p t k e", k=2)[:, :, k, :], ov[:, :, k, :],
                                         cumr[:], ALU.mult)
            link(last)
            link(dve.tensor_reduce(rank[:].rearrange("p t k -> p (t k)"), prod[:], AX.X, ALU.add))
            link(dve.tensor_reduce(most[:, 0:1], side[1][:, 0:NE], AX.X, ALU.max))
            link(dve.tensor_scalar(over[:], cst("limits"), most[:, 0:1], None, ALU.is_lt))
            link(dve.tensor_reduce(most[:, 1:2], over[:], AX.X, ALU.add))
            link(dve.tensor_scalar(T["rounds"][:], most[:, 1:2], 1.0, None, ALU.add))


ROUTER_SEMS = ["small", "h_stored", "xn_ready", "hT_ready", "hT_turned", "logits", "both_ready", "counted",
               "squares_done", "mean_ready", "root_ready", "exp_args", "exps", "dve_chain"]

UNITS = 12
UW = 1024


def expert_block(nc, l, T, args, cst, sem):
    x, pz, side = T["x"], T["pz"], T["side"]
    weights = [args["expert_w_gate"].rearrange("l e (p k) n -> l e p (k n)", k=KT),
               args["expert_w_up"].rearrange("l e (p k) n -> l e p (k n)", k=KT),
               args["expert_w_down"].rearrange("l e (p k) n -> l e p (k n)", k=FT)]
    rank, gate, e_f = T["rank"], T["gate"], T["expert"]
    with ExitStack() as ctx:
        def sb(name, shape, dt=F32):
            return ctx.enter_context(nc.sbuf_tensor(name, [P] + shape, dt))

        raw = sb("e_raw", [2, UNITS, UW])
        w_hi = sb("e_hi", [RING, UW], F32R)
        w_lo = sb("e_lo", [RING, UW], F32R)
        xg = sb("xg", [D])
        xs = sb("xs", [2, KT, P], F32R)
        hit = sb("hit", [2 * TT, P])
        idx = sb("idx", [PAIRS], I32)
        g_sb = sb("g_sb", [DE])
        u_sb = sb("u_sb", [DE])
        act_g = sb("act_g", [FT, CAP])
        hid = sb("hid", [FT, CAP])
        hs = sb("hs", [FT, P], F32R)
        y_low = sb("y_low", [D])
        y_sb = sb("y_sb", [D])
        yg = sb("yg", [2, D])
        inr = sb("inr", [2 * TT])
        tmp = sb("tmp", [2 * TT])
        wgt = sb("wgt", [2 * TT])
        row = sb("row", [2 * TT], I32)
        block = ctx.enter_context(nc.Block())
        PU = 2 * UNITS
        pzf = T["pz_all"]

        @block.sync
        def _(sp):
            def load(e, q, w):
                src = weights[w][l, e]
                sp.dma_start(raw[:, q, 4 * w:4 * w + 4, :].rearrange("p a b -> p (a b)"), src).then_inc(sem[f"w{q}{w}"], 16)

            for q in range(2):
                for w in range(3):
                    load(q, q, w)
            with sp.Fori(1, PAIRS) as p:
                for q in range(2):
                    for w in range(3):
                        sp.wait_ge(sem["lo_split"], (p - 1) * PU + (q * UNITS + 4 * w + 4))
                        load(2 * p + q, q, w)

        @block.gpsimd
        def _(pool):
            pool.wait_ge(sem["idx_ready"], 1)
            for p in range(PAIRS):
                if p:
                    pool.wait_ge(sem["xg_turned"], 2 * p)
                pool.indirect_dma_start(xg[:], None, T["h_dram"],
                                        bass.IndirectOffsetOnAxis(ap=idx[:, p:p + 1], axis=0)
                                        ).then_inc(sem["gathered"], 16)
            pool.wait_ge(sem["y_stored"], 16 * (PAIRS + 1))
            for n in range(2 * TT):
                if n >= 2:
                    pool.wait_ge(sem["combined"], n - 1)
                pool.indirect_dma_start(yg[:, n % 2, :], None, T["y_dram"],
                                        bass.IndirectOffsetOnAxis(ap=row[:, n:n + 1], axis=0)
                                        ).then_inc(sem[f"fetched{n % 2}"], 16)
            pool.wait_ge(sem["combined"], 2 * TT)
            nums = sorted(sem[k].num for k in ("gathered", "fetched0", "fetched1"))
            pool.dma_reset(range(nums[0], nums[-1] + 1))

        @block.tensor
        def _(pe):
            ident = cst("ident")
            pe.sem_inc(sem["unit_done"], RING)
            pe.wait_ge(sem["hit_ready"], 1)
            for n in range(2 * TT):
                last = pe.matmul(side[3][:, 0:NE], hit[:, n, :], T["token_at"][:, n, :], start=(n == 0),
                                 stop=(n == 2 * TT - 1))
            last.then_inc(sem["tokens_found"], 1)
            with pe.Fori(0, PAIRS) as p:
                pe.wait_ge(sem["gathered"], 16 * p + 16)
                for half in range(2):
                    for k in range(4):
                        last = pe.transpose(side[half][:, P * k:P * k + P],
                                            xg[:].rearrange("p (f k) -> p k f", k=KT)[:, 4 * half + k, :], ident)
                    last.then_inc(sem["xg_turned"], 1)
                pe.wait_ge(sem["xs_ready"], 2 * p + 2)
                for q in range(2):
                    def unit(j):
                        pe.wait_ge(sem["lo_split"], p * PU + (q * UNITS + j + 1))
                        return w_hi[:, j % RING, :], w_lo[:, j % RING, :]

                    for j in range(8):
                        wh, wl = unit(j)
                        for k in range(2):
                            kt = 2 * (j % 4) + k
                            for n, w in enumerate((wh, wl)):
                                last = pe.matmul(pz[j // 4][:], xs[:, q, kt, :], w[:, 512 * k:512 * k + 512],
                                                 start=(kt == 0 and n == 0), stop=(kt == KT - 1 and n == 1))
                        last.then_inc(sem["unit_done"], 1)
                    pe.wait_ge(sem["g_copied"], 2 * p + (q + 1))
                    pe.wait_ge(sem["u_copied"], 2 * p + (q + 1))
                    for n, src in enumerate((g_sb, u_sb)):
                        for f in range(FT):
                            c = CAP * (FT * n + f)
                            last = pe.matmul(side[2][:, c:c + CAP],
                                             src[:].rearrange("p (f k) -> p k f", k=FT)[:, f, :], cst("stack"),
                                             start=True, stop=True)
                    last.then_inc(sem["gu_turned"], 1)
                    pe.wait_ge(sem["hs_ready"], 2 * p + (q + 1))
                    pe.wait_ge(sem["y_read"], 2 * p + (q + 1))
                    for f in range(FT):
                        wh, wl = unit(8 + f)
                        for n, w in enumerate((wh, wl)):
                            for c in range(2):
                                last = pe.matmul(pz[2 + c][:], hs[:, f, :], w[:, 512 * c:512 * c + 512],
                                                 start=(f == 0 and n == 0), stop=(f == FT - 1 and n == 1))
                        last.then_inc(sem["unit_done"], 1)

        @block.scalar
        def _(act):
            act.sem_inc(sem["y_stored"], 16)
            with act.Fori(0, PAIRS) as p:
                for q in range(2):
                    def split(j):
                        if j % 4 == 0:
                            act.wait_ge(sem[f"w{q}{j // 4}"], 16 * p + 16)
                        act.wait_ge(sem["unit_done"], p * PU + (q * UNITS + j + 1))
                        act.copy(w_hi[:, j % RING, :], raw[:, q, j, :]).then_inc(sem["hi_split"], 1)

                    for j in range(4):
                        split(j)
                    if q == 0:
                        for half in range(2):
                            act.wait_ge(sem["xg_turned"], 2 * p + (half + 1))
                            act.copy(xs[:, :, 4 * half:4 * half + 4, 0:CAP].rearrange("p q k s -> p k q s"),
                                     side[half][:].rearrange("p (k q s) -> p k q s", k=4, q=2)
                                     ).then_inc(sem["xs_hi"], 1)
                    for j in range(4, 8):
                        split(j)
                    act.wait_ge(sem["unit_done"], p * PU + (q * UNITS + RING + 4))
                    act.copy(g_sb[:], pz[0][:]).then_inc(sem["g_copied"], 1)
                    for j in range(8, UNITS):
                        split(j)
                    act.wait_ge(sem["gu_turned"], 2 * p + (q + 1))
                    act.activation(act_g[:].rearrange("p a b -> p (a b)"), side[2][:, 0:FT * CAP],
                                   ACT.Silu).then_inc(sem["silu_done"], 1)
                    act.wait_ge(sem["unit_done"], p * PU + (q * UNITS + RING + UNITS))
                    act.copy(y_low[0:CAP, :], pzf[CAP:P, 2:4, :].rearrange("p a b -> p (a b)")
                             ).then_inc(sem["low_copied"], 1)
                act.wait_ge(sem["y_read"], 2 * p + 3)
                act.dma_start(T["y_dram"].rearrange("(p s) d -> p s d", s=P)[p], y_sb[:]).then_inc(sem["y_stored"], 16)

        @block.vector
        def _(dve):
            link = chain(dve, sem["dve_chain"])
            dve.sem_inc(sem["y_read"], 1)
            rk = rank[:].rearrange("p t k -> p (t k)")
            dve.tensor_tensor(hit[:], spread(cst("rows"), 2 * TT), each(rk, P), ALU.is_equal).then_inc(sem["hit_ready"], 1)
            link(dve.tensor_scalar(inr[:], rk, 0.0, None, ALU.is_ge))
            link(dve.tensor_scalar(tmp[:], rk, float(CAP), None, ALU.is_lt))
            link(dve.tensor_tensor(inr[:], inr[:], tmp[:], ALU.mult))
            link(dve.tensor_tensor(wgt[:], gate[:].rearrange("p t k -> p (t k)"), inr[:], ALU.mult))
            link(dve.scalar_tensor_tensor(tmp[:], e_f[:].rearrange("p t k -> p (t k)"), float(CAP), rk,
                                          ALU.mult, ALU.add))
            link(dve.tensor_tensor(tmp[:], tmp[:], inr[:], ALU.mult))
            link(dve.tensor_copy(row[:], tmp[:]))
            link(dve.tensor_scalar(rk, rk, -float(CAP), None, ALU.add))
            dve.wait_ge(sem["tokens_found"], 1)
            pairs = side[3][:, 0:NE].rearrange("p (e two) -> p two e", two=2)
            dve.tensor_copy(idx[0:CAP, :], pairs[0:CAP, 0, :])
            dve.tensor_copy(idx[CAP:P, :], pairs[CAP:P, 1, :]).then_inc(sem["idx_ready"], 1)
            with dve.Fori(0, PAIRS) as p:
                for q in range(2):
                    def split(j):
                        dve.wait_ge(sem["hi_split"], p * PU + (q * UNITS + j + 1))
                        dve.tensor_tensor(w_lo[:, j % RING, :], raw[:, q, j, :], w_hi[:, j % RING, :],
                                          ALU.subtract).then_inc(sem["lo_split"], 1)

                    for j in range(4):
                        split(j)
                    if q == 0:
                        for half in range(2):
                            dve.wait_ge(sem["xs_hi"], 2 * p + (half + 1))
                            out = xs[:, :, 4 * half:4 * half + 4, :].rearrange("p q k s -> p k q s")
                            dve.tensor_tensor(out[:, :, :, CAP:P],
                                              side[half][:].rearrange("p (k q s) -> p k q s", k=4, q=2),
                                              out[:, :, :, 0:CAP], ALU.subtract).then_inc(sem["xs_ready"], 1)
                    for j in range(4, UNITS):
                        split(j)
                    dve.wait_ge(sem["unit_done"], p * PU + (q * UNITS + RING + 8))
                    dve.tensor_copy(u_sb[:], pz[1][:]).then_inc(sem["u_copied"], 1)
                    dve.wait_ge(sem["silu_done"], 2 * p + (q + 1))
                    dve.tensor_tensor(hid[:].rearrange("p a b -> p (a b)"), act_g[:].rearrange("p a b -> p (a b)"),
                                      side[2][:, FT * CAP:2 * FT * CAP], ALU.mult).then_inc(sem["hid_chain"], 1)
                    dve.wait_ge(sem["hid_chain"], 4 * p + (2 * q + 1))
                    dve.tensor_copy(hs[:, :, 0:CAP], hid[:]).then_inc(sem["hid_chain"], 1)
                    dve.wait_ge(sem["hid_chain"], 4 * p + (2 * q + 2))
                    dve.tensor_tensor(hs[:, :, CAP:P], hid[:], hs[:, :, 0:CAP], ALU.subtract).then_inc(sem["hs_ready"], 1)
                    if q == 0:
                        dve.wait_ge(sem["y_stored"], 16 * p + 16)
                    dve.wait_ge(sem["low_copied"], 2 * p + (q + 1))
                    dve.tensor_tensor(y_sb[CAP * q:CAP * q + CAP, :], pzf[0:CAP, 2:4, :].rearrange("p a b -> p (a b)"),
                                      y_low[0:CAP, :], ALU.add).then_inc(sem["y_read"], 1)
            for n in range(2 * TT):
                dve.wait_ge(sem[f"fetched{n % 2}"], 16 * (n // 2 + 1))
                if n % 2:
                    dve.wait_ge(sem["combined"], n)
                xt = x[:, n // 2, :]
                dve.scalar_tensor_tensor(xt, yg[:, n % 2, :], wgt[:, n:n + 1], xt, ALU.mult,
                                         ALU.add).then_inc(sem["combined"], 1)


EXPERT_SEMS = (["lo_split", "hi_split", "unit_done", "idx_ready", "xg_turned", "gathered", "y_stored", "combined",
                "fetched0", "fetched1", "hit_ready", "tokens_found", "xs_ready", "xs_hi", "g_copied", "u_copied",
                "gu_turned", "hs_ready", "y_read", "silu_done", "low_copied", "hid_chain", "dve_chain"]
               + [f"w{q}{w}" for q in range(2) for w in range(3)])


def trunk(nc, args, out):
    with ExitStack() as ctx:
        T = {}

        def sb(name, shape, dt=F32):
            T[name] = ctx.enter_context(nc.sbuf_tensor(name, [P] + shape, dt))
            return T[name]

        x = sb("x", [TT, D])
        bias = sb("bias", [C_H, S])
        const = sb("const", [N_CONST])
        sb("masks", [(LEVELS + 1) * P], U8)
        sb("one", [2 * TT, NE])
        sb("token_at", [2 * TT, NE])
        sb("expert", [TT, 2])
        sb("gate", [TT, 2])
        sb("rank", [TT, 2])
        sb("rounds", [1], I32)
        lbs = sb("lbs", [DEPTH, 2])
        lt = sb("lt", [3, 2])
        T["h_dram"] = nc.dram_tensor("h_rows", [S, D], F32, kind="Internal").ap()
        T["y_dram"] = nc.dram_tensor("expert_rows", [NE * CAP, D], F32, kind="Internal").ap()
        T["lb_dram"] = nc.dram_tensor("lower_bounds", [DEPTH, P, 2], F32, kind="Internal").ap()
        T["pz_all"] = ctx.enter_context(nc.psum_tensor("pz", [P, 4, 512], F32))
        side = ctx.enter_context(nc.psum_tensor("side", [P, 4, 512], F32))
        T["pz"] = [T["pz_all"][:, i, :] for i in range(4)]
        T["side"] = [side[:, i, :] for i in range(4)]

        def cst(name):
            a, b = CONST[name]
            return const[:, a:b]

        pool_sems = ["gathered", "fetched0", "fetched1"]
        names = pool_sems + sorted((set(MIXER_SEMS) | set(ROUTER_SEMS) | set(EXPERT_SEMS) | {"ready"})
                                   - set(pool_sems))
        sem = {n: ctx.enter_context(nc.semaphore(n)) for n in names}
        numbers = range(min(s.num for s in sem.values()), max(s.num for s in sem.values()) + 1)

        def restart():
            nc.all_engine_barrier(sems_to_clear=numbers)

        xv = args["x"].rearrange("b (t p) d -> p (b t) d", p=P)
        ov = out.rearrange("b (t p) d -> p (b t) d", p=P)

        with nc.sbuf_tensor("masks_in", [P, (LEVELS + 1) * P], F32) as masks_in, nc.Block() as block:
            @block.sync
            def _(sp):
                sp.dma_start(lbs[:], args["hgrn_lb"]).then_inc(sem["ready"], 16)
                sp.dma_start(x[:], xv).then_inc(sem["small"], 16)
                sp.dma_start(const[:], args["const"]).then_inc(sem["small"], 16)
                sp.dma_start(masks_in[:], args["masks"]).then_inc(sem["small"], 16)
                sp.dma_start(bias[:], args["rel_bias"]).then_inc(sem["raw0"], 16)
                sp.wait_ge(sem["f_ready"], 1)
                for n in range(DEPTH):
                    sp.dma_start(T["lb_dram"][n], lbs[:, n, :]).then_inc(sem["raw1"], 16)
                sp.wait_ge(sem["raw1"], 16 * DEPTH)
                sp.wait_ge(sem["small"], 48)

            @block.scalar
            def _(act):
                act.wait_ge(sem["exp_args"], 1)
                act.activation(lt[:, 0:2, :], lt[:, 0:2, :], ACT.Exp).then_inc(sem["exps"], 1)

            @block.vector
            def _(dve):
                link = chain(dve, sem["dve_chain"])
                dve.wait_ge(sem["ready"], 16)
                link(dve.tensor_tensor(lt[:, 2, :], lbs[:, 0, :], lbs[:, 1, :], ALU.max))
                dve.tensor_tensor(lt[:, 0, :], lbs[:, 0, :], lt[:, 2, :], ALU.subtract)
                dve.tensor_tensor(lt[:, 1, :], lbs[:, 1, :], lt[:, 2, :], ALU.subtract).then_inc(sem["exp_args"], 1)
                dve.wait_ge(sem["exps"], 1)
                link(dve.tensor_tensor(lt[:, 2, :], lt[:, 0, :], lt[:, 1, :], ALU.add))
                link(dve.reciprocal(lt[:, 2, :], lt[:, 2, :]))
                link(dve.memset(lbs[:, 0, :], 0.0))
                dve.tensor_tensor(lbs[:, 1, :], lt[:, 1, :], lt[:, 2, :], ALU.mult).then_inc(sem["f_ready"], 1)
                dve.wait_ge(sem["small"], 48)
                dve.tensor_copy(T["masks"][:], masks_in[:])
                dve.wait_ge(sem["raw0"], 16)
                link(dve.tensor_scalar(bias[:], bias[:], -1.0, None, ALU.mult))
                link(dve.memset(bias[0:CHUNK, :, S - CHUNK:S], -NEG))
        restart()
        with nc.Fori(0, DEPTH) as l:
            mixer_block(nc, l, T, args, cst, sem)
            restart()
            router_block(nc, l, T, args, cst, sem)
            restart()
            rounds = nc.values_load(T["rounds"][0:1, 0:1], min_val=1, max_val=MAX_ROUNDS)
            with nc.Fori(0, rounds):
                expert_block(nc, l, T, args, cst, sem)
                restart()

        with nc.sbuf_tensor("f_out", [P, TT, D], F32) as y, nc.sbuf_tensor("f_w", [P, D], F32) as fw, \
                nc.sbuf_tensor("f_ssq", [P, TT], F32) as ssq, nc.Block() as block:
            @block.sync
            def _(sp):
                sp.dma_start(fw[:], args["norm_final"].partition_broadcast(P)).then_inc(sem["small"], 16)
                for t in range(TT):
                    sp.wait_ge(sem["xn_ready"], t + 1)
                    sp.dma_start(ov[:, t, :], y[:, t, :]).then_inc(sem["y_stored"], 16)
                sp.wait_ge(sem["y_stored"], 16 * TT)

            @block.scalar
            def _(act):
                norm_square(act, x, y, ssq, sem["squares_done"])
                norm_root(act, ssq, sem)

            @block.vector
            def _(dve):
                link = chain(dve, sem["dve_chain"])
                dve.wait_ge(sem["small"], 16)
                norm_scale(dve, link, x, y, fw[:], ssq, sem)


_INPUTS = ["x", "w_in", "w_out", "norm_mix", "norm_ffn", "norm_final", "hgrn_lb", "hgrn_norm", "ret_norm",
           "rel_bias", "router_group", "router_expert", "expert_w_gate", "expert_w_up", "expert_w_down"]


def kernel(**inputs):
    import concourse.bacc as bacc
    from concourse.bass_utils import run_bass_kernel_spmd

    arrays = {n: np.ascontiguousarray(inputs[n]) for n in _INPUTS}
    arrays["hgrn_lb"] = np.ascontiguousarray(arrays["hgrn_lb"].reshape(DEPTH, 2, P).transpose(2, 0, 1))
    dist = (S - P) + np.arange(P)[:, None] - np.arange(S)[None, :]
    at = np.clip(dist, -MAX_REL, MAX_REL) + MAX_REL
    arrays["rel_bias"] = np.ascontiguousarray(arrays["rel_bias"][:, at].transpose(1, 0, 2))
    arrays["const"], arrays["trig"], arrays["masks"] = constants()

    nc = bacc.Bacc("TRN2", target_bir_lowering=False, num_devices=1)
    args = {n: nc.dram_tensor(f"in_{n}", a.shape, mybir.dt.from_np(a.dtype), kind="ExternalInput").ap()
            for n, a in arrays.items()}
    out = nc.dram_tensor("out", (1, S, D), F32, kind="ExternalOutput").ap()
    trunk(nc, args, out)
    r = run_bass_kernel_spmd(nc, [{f"in_{n}": a for n, a in arrays.items()}], core_ids=[0])
    return r.results[0]["out"]
```

```python
from contextlib import ExitStack

import numpy as np
import concourse.bass as bass
from concourse import mybir

F32 = mybir.dt.float32
F32R = mybir.dt.float32r
I32 = mybir.dt.int32
U32 = mybir.dt.uint32
U8 = mybir.dt.uint8
ALU = mybir.AluOpType
ACT = mybir.ActivationFunctionType
AX = mybir.AxisListType

P = 128
DEPTH, D, S = 2, 1024, 512
TT = S // P
KT = D // P
EPS = 1e-6
NEG = -1e30
MIN_FORGET = 1e-30

A_H, A_DK = 4, 64
AW = A_H * A_DK
B_H, B_DK, B_DV = 4, 48, 96
BW = B_H * B_DV
HALF = B_DK // 2
C_H, C_DH = 6, 64
CW = C_H * C_DH
CHUNK, MAX_REL = 64, 128
ROPE_BASE = 10000.0
D_IN = 4 * AW + 2 * B_H * B_DK + 2 * BW + 3 * CW

NG, EPG = 4, 8
NE = NG * EPG
DE = 512
FT = DE // P
CAP = 64
PAIRS = NE // 2
MAX_ROUNDS = S // CAP

LEVELS = 7

_o = np.cumsum([0, AW, AW, AW, AW, B_H * B_DK, B_H * B_DK, BW, BW, CW, CW, CW]).tolist()
GROUPS = [
    ("aq_af", _o[0], 2 * AW, True),
    ("ai_ag", _o[2], 2 * AW, False),
    ("cq", _o[8], CW, True),
    ("ck", _o[9], CW, True),
    ("cv", _o[10], CW, False),
    ("bq_bk", _o[4], 2 * B_H * B_DK, False),
    ("bv", _o[6], BW, False),
    ("bg", _o[7], BW, False),
    ("out_lo", 0, D // 2, False),
    ("out_hi", D // 2, D // 2, False),
]
N_IN = 8
RING = 4


def tiles_of(g):
    return GROUPS[g][2] // P if GROUPS[g][3] else TT


def bank_fills(g, i):
    return sum(1 for k in range(g) if tiles_of(k) > i)


CONST = {}
_n = 0
for _name, _w in [("ident", 128), ("stack", CAP), ("causal", 128), ("before", 128), ("ones", 128),
                  ("rows", 128), ("token", TT), ("experts", NE), ("groups", NG), ("limits", MAX_ROUNDS)]:
    CONST[_name] = (_n, _n + _w)
    _n += _w
N_CONST = _n


def constants():
    c = np.zeros((P, N_CONST), np.float32)

    def put(name, a):
        c[:, CONST[name][0]:CONST[name][1]] = a.reshape(P, -1)

    i = np.arange(P)
    put("ident", np.eye(P))
    put("stack", np.concatenate([np.eye(CAP)] * 2))
    put("causal", (i[None, :] >= i[:, None]))
    put("before", (i[:, None] < i[None, :]))
    put("ones", np.ones((P, P)))
    put("rows", np.tile(np.arange(CAP), (P, 2)))
    put("token", i[:, None] + P * np.arange(TT)[None, :])
    put("experts", np.tile(np.arange(NE), (P, 1)))
    put("groups", np.tile(np.arange(NG), (P, 1)))
    put("limits", np.tile(CAP * (1 + np.arange(MAX_ROUNDS)), (P, 1)))
    pos = np.arange(S, dtype=np.float32)
    inv = (np.float32(ROPE_BASE) ** (-np.arange(HALF, dtype=np.float32) / np.float32(HALF))).astype(np.float32)
    ang = (pos[:, None] * inv[None, :]).astype(np.float32).astype(np.float64)
    lg = np.log1p(-np.exp2(-5.0 - np.arange(B_H)))
    gq = np.exp(lg[None, :] * pos[:, None].astype(np.float64))
    gk = np.exp(-lg[None, :] * pos[:, None].astype(np.float64)) * B_DK ** -0.5
    f = np.concatenate([gq, gk], axis=1)[:, :, None]
    trig = [(f * tr[:, None, :]).reshape(TT, P, 8, HALF).transpose(1, 0, 2, 3).reshape(P, -1)
            for tr in (np.cos(ang), np.sin(ang))]
    masks = np.zeros((P, LEVELS + 1, P), np.float32)
    j, q = i[:, None], i[None, :]
    for n in range(LEVELS):
        h = 1 << n
        masks[:, n] = (j // (2 * h) == q // (2 * h)) & (q % (2 * h) >= h) & (j % (2 * h) < h)
    masks[:, LEVELS] = j == q
    return c, np.concatenate(trig, axis=1).astype(np.float32), masks.reshape(P, -1)


class Side:

    def __init__(self):
        self.at, self.fills, self.signals = {}, [0] * 4, [0] * 4

    def add(self, key, bank, signalled=True):
        self.fills[bank] += 1
        self.signals[bank] += signalled
        self.at[key] = (bank, self.fills[bank], self.signals[bank])


N_SLOT = 8 * (N_IN - 1)
N_TAIL = 8


def slot(g, kt):
    return (g - 1) * KT + kt


LV0 = 5
A_LEVEL = LV0 + 2
A_KEYS, A_STATE, A_OUT = LV0 + 10, LV0 + 12, LV0 + 14
C0 = slot(5, 1)
C_ITEMS = [(t, h) for t in range(TT) for h in range(C_H)]
B_ROT = slot(6, 3)
B_QKT, B_SC, B_STATE, B_OUT = slot(6, 5), slot(6, 7), slot(7, 3), slot(7, 5)


def side_plan():
    s = Side()
    n = 0
    first = [("hT", i) for i in range(2 * TT)]
    first += [("level", lv, c) for lv in range(LEVELS + 1) for c in range(TT)]
    first += [("kdT", c) for c in range(TT - 1)] + [("aU", c) for c in range(TT - 1)]
    first += [("ao", c) for c in range(TT)]
    for n, key in enumerate(first):
        s.add(key, n % 4)
    n = 0
    for sl in range(C0, N_SLOT + N_TAIL):
        i = sl - C0
        keys = [("cT", i - 1)] if 0 <= i - 1 < len(C_ITEMS) else []
        keys += [("cs", i)] if 0 <= i < len(C_ITEMS) else []
        keys += [("bT", k) for k in range(4)] if sl == B_QKT else []
        keys += [("bs", c) for c in range(TT)] if sl == B_SC else []
        keys += [("bU", c) for c in range(TT - 1)] if sl == B_STATE else []
        keys += [("bo", c) for c in range(TT)] if sl == B_OUT else []
        for k in keys:
            s.add(k, n % 3)
            n += 1
        if 0 <= i - 2 < len(C_ITEMS) and C_ITEMS[i - 2][1] == 0:
            s.add(("co", C_ITEMS[i - 2][0]), 3, signalled=False)
    for i in range(2 * TT):
        s.add(("yT", i), i % 4)
    return s.at


def norm_square(act, x, squares, ssq, squares_done):
    for t in range(TT):
        act.activation(squares[:, t, :], x[:, t, :], ACT.Square,
                       accum_out=ssq[:, t:t + 1]).then_inc(squares_done, 1)


def norm_root(act, ssq, sem):
    act.wait_ge(sem["mean_ready"], 1)
    act.activation(ssq[:], ssq[:], ACT.Sqrt).then_inc(sem["root_ready"], 1)


def norm_scale(dve, link, x, xn, weight, ssq, sem):
    dve.wait_ge(sem["squares_done"], TT)
    dve.tensor_scalar(ssq[:], ssq[:], 1.0 / D, EPS, ALU.mult, ALU.add).then_inc(sem["mean_ready"], 1)
    dve.wait_ge(sem["root_ready"], 1)
    link(dve.reciprocal(ssq[:], ssq[:]))
    for t in range(TT):
        dve.scalar_tensor_tensor(xn[:, t, :], x[:, t, :], ssq[:, t:t + 1], weight, ALU.mult,
                                 ALU.mult).then_inc(sem["xn_ready"], 1)


def chain(eng, sem):
    n = [0]

    def link(ins):
        n[0] += 1
        ins.then_inc(sem, 1)
        eng.wait_ge(sem, n[0])
    return link


def spread(ap, n):
    return ap.rearrange("p (o a) -> p o a", o=1).broadcast_to([P, n, ap.shape[1]])


def each(ap, n):
    return ap.rearrange("p (a o) -> p a o", o=1).broadcast_to([P, ap.shape[1], n])


def head_rows(h, n=64):
    return slice(64 * (h % 2), 64 * (h % 2) + n)


def tile_cols(t, f=0):
    return slice(S * f + P * t, S * f + P * t + P)


def score_place(h, c):
    return 2 * (c // 2) + h % 2, slice(P * (2 * (c % 2) + h // 2), P * (2 * (c % 2) + h // 2) + P)


def mixer_block(nc, l, T, args, cst, sem):
    x, bias, pz, side = T["x"], T["bias"], T["pz"], T["side"]
    plan = side_plan()
    win = args["w_in"].rearrange("l (p k) n -> l p k n", k=KT)
    wout = args["w_out"].rearrange("l (p k) n -> l p k n", k=KT)
    with ExitStack() as ctx:
        def sb(name, shape, dt=F32):
            return ctx.enter_context(nc.sbuf_tensor(name, [P] + shape, dt))

        raw = sb("raw", [2, KT, 512])
        w_hi = sb("w_hi", [RING, 512], F32R)
        w_lo = sb("w_lo", [RING, 512], F32R)
        a_hi = sb("a_hi", [KT, S], F32R)
        a_lo = sb("a_lo", [KT, S], F32R)
        y = sb("y", [TT, D])
        junk = sb("junk", [AW])
        ssq = sb("ssq", [TT])
        norm_a = sb("norm_a", [AW])
        norm_b = sb("norm_b", [BW])
        lb = sb("lb", [2])
        omlb = sb("omlb", [2])
        glast = sb("glast", [2, TT])
        a_ms = sb("a_ms", [TT])
        b_mu = sb("b_mu", [TT * B_H])
        b_ms = sb("b_ms", [TT * B_H])
        nmax = sb("nmax", [len(C_ITEMS)])
        den = sb("den", [len(C_ITEMS)])
        rden = sb("rden", [len(C_ITEMS)])
        sa = sb("sa", [TT, 4 * P])

        arena = sb("arena", [16512])
        used = [0]

        def early(n):
            used[0] += n
            return arena[:, used[0] - n:used[0]]

        fa = early(2 * S)
        cum = early(2 * S)
        diff = [early(2 * S), early(2 * S)]
        qf = [early(2 * S), early(2 * S)]
        kf = [early(2 * S), early(2 * S)]
        qa = early(2 * S)
        ka = early(2 * S)
        aig = early(TT * 2 * AW).rearrange("p (t c) -> p t c", t=TT)
        kd = early(3 * AW).rearrange("p (t c) -> p t c", t=3)
        st_a = early(3 * AW).rearrange("p (t c) -> p t c", t=3)
        norm_w = arena[:, 15360:15360 + D]
        used[0] = 0
        cq = early(3 * S).rearrange("p (f t) -> p f t", f=3)
        ck = early(3 * S).rearrange("p (f t) -> p f t", f=3)
        cv = early(TT * CW).rearrange("p (t c) -> p t c", t=TT)
        pr = [early(S), early(S)]
        prT = [early(S), early(S)]
        zqk = early(TT * 8 * B_DK)
        rqk = early(TT * 8 * 64).rearrange("p (t h d) -> p t h d", t=TT, h=8)
        qkT = early(4 * S).rearrange("p (f t) -> p f t", f=4)
        bv = early(TT * BW).rearrange("p (t c) -> p t c", t=TT)
        trig = early(2 * TT * 8 * HALF)
        bg = trig.rearrange("p (t c) -> p t c", t=TT)
        st_b = early(3 * BW).rearrange("p (t c) -> p t c", t=3)

        block = ctx.enter_context(nc.Block())

        def evacuated(eng, g):
            for i in range(tiles_of(g)):
                eng.wait_ge(sem[f"pz_free{i}"], bank_fills(g, i) + 1)

        def was_read(eng, key):
            bank, nth, _ = plan[key]
            eng.wait_ge(sem[f"side_free{bank}"], nth)

        def filled(eng, key):
            bank, _, nth = plan[key]
            eng.wait_ge(sem[f"side_full{bank}"], nth)
            return side[bank], sem[f"side_free{bank}"]

        def add_out(dve, g):
            dve.wait_ge(sem["unit_done"], KT * (g + 1))
            col = GROUPS[g][1]
            for i in range(TT):
                xs = x[:, i, col:col + 512]
                dve.tensor_tensor(xs, xs, pz[i][:], ALU.add).then_inc(sem[f"pz_free{i}"], 1)

        @block.sync
        def _(sp):
            sp.dma_start(norm_w, args["norm_mix"][l].partition_broadcast(P)).then_inc(sem["small"], 16)
            sp.dma_start(norm_a[:], args["hgrn_norm"][l].partition_broadcast(P)).then_inc(sem["small"], 16)
            sp.dma_start(norm_b[:], args["ret_norm"][l].partition_broadcast(P)).then_inc(sem["small"], 16)
            sp.dma_start(lb[:], T["lb_dram"][l]).then_inc(sem["small"], 16)
            for g, (_, col, width, _) in enumerate(GROUPS):
                if g >= 2:
                    sp.wait_ge(sem["lo_split"], KT * (g - 1))
                src = win[l, :, :, col:col + width] if g < N_IN else wout[l, :, :, col:col + width]
                sp.dma_start(raw[:, g % 2, :, 0:width], src).then_inc(sem[f"raw{g % 2}"], 16)
                if g == 2:
                    sp.dma_start(trig, args["trig"]).then_inc(sem["trig"], 16)

        @block.gpsimd
        def _(pool):
            pool.memset(st_a, 0.0)
            pool.memset(sa[:], 0.0).then_inc(sem["zeroed"], 1)
            for c in range(TT):
                pool.wait_ge(sem[f"side_full{plan[('ao', c)][0]}"], plan[("ao", c)][2])
            pool.memset(st_b, 0.0)
            pool.memset(rqk, 0.0).then_inc(sem["zeroed"], 1)

        @block.tensor
        def _(pe):
            ident = cst("ident")

            def fill(key):
                bank, nth, _ = plan[key]
                if nth > 1:
                    pe.wait_ge(sem[f"side_free{bank}"], nth - 1)
                return side[bank], sem[f"side_full{bank}"]

            def turn_rows(name, i):
                t, half = i // 2, i % 2
                out, full = fill((name, i))
                for k in range(4):
                    last = pe.transpose(out[:, P * k:P * k + P],
                                        y[:, t, :].rearrange("p (f k) -> p k f", k=KT)[:, 4 * half + k, :], ident)
                last.then_inc(full, 1)

            def unit(g, kt):
                u = g * KT + kt
                _, _, width, feature_major = GROUPS[g]
                pe.wait_ge(sem["lo_split"], u + 1)
                wh, wl = w_hi[:, u % RING, :], w_lo[:, u % RING, :]
                ah, al = a_hi[:, kt, :], a_lo[:, kt, :]
                for i in range(tiles_of(g)):
                    if kt == 0 and bank_fills(g, i):
                        pe.wait_ge(sem[f"pz_free{i}"], bank_fills(g, i))
                    c = slice(P * i, P * i + P)
                    if feature_major:
                        parts = [(wh[:, c], ah), (wh[:, c], al), (wl[:, c], ah)]
                        out = pz[i][:]
                    else:
                        parts = [(ah[:, c], wh[:, 0:width]), (ah[:, c], wl[:, 0:width]), (al[:, c], wh[:, 0:width])]
                        out = pz[i][:, 0:width]
                    for n, (a, b) in enumerate(parts):
                        last = pe.matmul(out, a, b, start=(kt == 0 and n == 0), stop=(kt == KT - 1 and n == 2))
                last.then_inc(sem["unit_done"], 1)

            def level(n):
                if n < LEVELS:
                    pe.wait_ge(sem["factors"], n + 1)
                k_, q_ = (kf[n % 2], qf[n % 2]) if n < LEVELS else (ka, qa)
                for k in range(4):
                    out, full = fill(("level", n, k))
                    for c in (2 * (k // 2), 2 * (k // 2) + 1):
                        for h in range(k % 2, A_H, 2):
                            r, cols = head_rows(h), tile_cols(c, h // 2)
                            last = pe.matmul(out[:, score_place(h, c)[1]], k_[r, cols], q_[r, cols],
                                             start=True, stop=True)
                    last.then_inc(full, 1)

            def turn_keys():
                pe.wait_ge(sem["factors"], LEVELS + 1)
                for c in range(TT - 1):
                    out, full = fill(("kdT", c))
                    for f in range(2):
                        last = pe.transpose(out[:, P * f:P * f + P], kf[1][:, tile_cols(c, f)], ident)
                    last.then_inc(full, 1)

            def update_a():
                evacuated(pe, 1)
                for c in range(TT - 1):
                    was_read(pe, ("kdT", c))
                    out, full = fill(("aU", c))
                    for f in range(2):
                        v = slice(P * f, P * f + P)
                        last = pe.matmul(out[:, v], kd[:, c, v], aig[:, c, v], start=True, stop=True)
                    last.then_inc(full, 1)

            def out_a():
                for c in range(TT):
                    for h in range(2):
                        was_read(pe, ("level", LEVELS, score_place(h, c)[0]))
                    if c:
                        was_read(pe, ("aU", c - 1))
                    out, full = fill(("ao", c))
                    for h in range(A_H):
                        if c and h % 2 == 0:
                            v = slice(64 * h, 64 * h + P)
                            pe.matmul(out[:, v], qf[1][:, tile_cols(c, h // 2)], st_a[:, c - 1, v],
                                      start=True, stop=False)
                        v = slice(64 * h, 64 * h + 64)
                        k, cols = score_place(h, c)
                        last = pe.matmul(out[:, v], sa[:, k, cols], aig[:, c, v], start=(c == 0),
                                         stop=(c == 0 or h % 2 == 1))
                    last.then_inc(full, 1)

            def turn_b():
                pe.wait_ge(sem["rotated"], 1)
                for k in range(4):
                    out, full = fill(("bT", k))
                    for t in range(TT):
                        last = pe.transpose(out[:, P * t:P * t + P],
                                            rqk[:, t, 2 * k:2 * k + 2, :].rearrange("p a b -> p (a b)"), ident)
                    last.then_inc(full, 1)

            def scores_b():
                for k in range(4):
                    was_read(pe, ("bT", k))
                for k in range(4):
                    out, full = fill(("bs", k))
                    for c in (2 * (k // 2), 2 * (k // 2) + 1):
                        for h in range(k % 2, B_H, 2):
                            r = head_rows(h, B_DK)
                            last = pe.matmul(out[:, score_place(h, c)[1]], qkT[r, 2 + h // 2, tile_cols(c)],
                                             qkT[r, h // 2, tile_cols(c)], start=True, stop=True)
                    last.then_inc(full, 1)

            def update_b():
                evacuated(pe, 6)
                for c in range(TT - 1):
                    out, full = fill(("bU", c))
                    for k in range(2):
                        v = slice(2 * B_DV * k, 2 * B_DV * (k + 1))
                        last = pe.matmul(out[:, v], rqk[:, c, 4 + 2 * k:6 + 2 * k, :].rearrange("p a b -> p (a b)"),
                                         bv[:, c, v], start=True, stop=True)
                    last.then_inc(full, 1)

            def out_b():
                for c in range(TT):
                    for h in range(2):
                        was_read(pe, ("bs", score_place(h, c)[0]))
                    if c:
                        was_read(pe, ("bU", c - 1))
                    out, full = fill(("bo", c))
                    for h in range(B_H):
                        if c and h % 2 == 0:
                            v = slice(B_DV * h, B_DV * (h + 2))
                            pe.matmul(out[:, v], qkT[:, h // 2, tile_cols(c)], st_b[:, c - 1, v],
                                      start=True, stop=False)
                        v = slice(B_DV * h, B_DV * (h + 1))
                        k, cols = score_place(h, c)
                        last = pe.matmul(out[:, v], sa[:, k, cols], bv[:, c, v], start=(c == 0),
                                         stop=(c == 0 or h % 2 == 1))
                    last.then_inc(full, 1)

            def attend_turn(i):
                t, h = C_ITEMS[i]
                pe.wait_ge(sem["exp_done"], i + 1)
                out, full = fill(("cT", i))
                for j in range(t + 1):
                    last = pe.transpose(out[:, P * j:P * j + P], pr[i % 2][:, P * j:P * j + P], ident)
                last.then_inc(full, 1)

            def attend_scores(i):
                t, h = C_ITEMS[i]
                if i == 0:
                    evacuated(pe, 2)
                    evacuated(pe, 3)
                r = head_rows(h)
                out, full = fill(("cs", i))
                pe.matmul(out[:, 0:P * (t + 1)], cq[r, h // 2, tile_cols(t)], ck[r, h // 2, 0:P * (t + 1)],
                          start=True, stop=True).then_inc(full, 1)

            def attend_values(i):
                t, h = C_ITEMS[i]
                if i == 0:
                    evacuated(pe, 4)
                was_read(pe, ("cT", i))
                if h == 0:
                    fill(("co", t))
                for j in range(t + 1):
                    last = pe.matmul(side[3][:, 64 * h:64 * h + 64], prT[i % 2][:, P * j:P * j + P],
                                     cv[:, j, 64 * h:64 * h + 64], start=(j == 0), stop=(j == t))
                last.then_inc(sem["pv_done"], 1)

            def side_work(sl):
                if 0 <= sl - A_LEVEL <= LEVELS:
                    level(sl - A_LEVEL)
                if sl == A_KEYS:
                    turn_keys()
                if sl == A_STATE:
                    update_a()
                if sl == A_OUT:
                    out_a()
                i = sl - C0
                if 0 <= i - 1 < len(C_ITEMS):
                    attend_turn(i - 1)
                if 0 <= i < len(C_ITEMS):
                    attend_scores(i)
                if sl == B_QKT:
                    turn_b()
                if sl == B_SC:
                    scores_b()
                if sl == B_STATE:
                    update_b()
                if sl == B_OUT:
                    out_b()
                if 0 <= i - 2 < len(C_ITEMS):
                    attend_values(i - 2)

            for i in range(2 * TT):
                pe.wait_ge(sem["xn_ready"], i // 2 + 1)
                turn_rows("hT", i)
            for i in range(2 * TT):
                was_read(pe, ("hT", i))
            for g in range(N_IN):
                for kt in range(KT):
                    unit(g, kt)
                    if g:
                        side_work(slot(g, kt))
            for sl in range(N_SLOT, N_SLOT + N_TAIL):
                side_work(sl)
            pe.wait_ge(sem["y_ready"], 2)
            was_read(pe, ("co", TT - 1))
            for i in range(2 * TT):
                turn_rows("yT", i)
            for i in range(2 * TT):
                was_read(pe, ("yT", i))
            for g in range(N_IN, len(GROUPS)):
                for kt in range(KT):
                    unit(g, kt)

        @block.scalar
        def _(act):
            link = chain(act, sem["act_chain"])

            def hi_rows(name, i):
                t, half = i // 2, i % 2
                src, _ = filled(act, (name, i))
                act.copy(a_hi[:, 4 * half:4 * half + 4, tile_cols(t)],
                         src[:].rearrange("p (k t) -> p k t", k=4)).then_inc(sem["aT_hi"], 1)

            def split(g, kt):
                u, width = g * KT + kt, GROUPS[g][2]
                if kt == 0:
                    act.wait_ge(sem[f"raw{g % 2}"], 16 * (g // 2 + 1))
                if u >= RING:
                    act.wait_ge(sem["unit_done"], u - RING + 1)
                act.copy(w_hi[:, u % RING, 0:width], raw[:, g % 2, kt, 0:width]).then_inc(sem["hi_split"], 1)

            def evacuate(g):
                name = GROUPS[g][0]
                act.wait_ge(sem["unit_done"], KT * (g + 1))
                free = [sem[f"pz_free{i}"] for i in range(4)]
                if name == "aq_af":
                    for i in range(2):
                        act.activation(qa[:, S * i:S * i + S], pz[i][:], ACT.Silu).then_inc(free[i], 1)
                    for i in range(2):
                        act.activation(ka[:, S * i:S * i + S], pz[2 + i][:], ACT.Sigmoid, scale=-1.0)
                        act.activation(fa[:, S * i:S * i + S], pz[2 + i][:], ACT.Sigmoid).then_inc(free[2 + i], 1)
                if name == "ai_ag":
                    for i in range(TT):
                        act.copy(aig[:, i, 0:AW], pz[i][:, 0:AW])
                        act.activation(aig[:, i, AW:2 * AW], pz[i][:, AW:2 * AW], ACT.Silu).then_inc(free[i], 1)
                if name == "cq":
                    act.wait_ge(sem["factors"], LEVELS + 1)
                    for i in range(3):
                        act.mul(cq[:, i, :], pz[i][:], -C_DH ** -0.5).then_inc(free[i], 1)
                if name == "ck":
                    for c in range(TT):
                        was_read(act, ("ao", c))
                    for i in range(3):
                        act.copy(ck[:, i, :], pz[i][:]).then_inc(free[i], 1)
                if name == "cv":
                    for i in range(TT):
                        act.copy(cv[:, i, :], pz[i][:, 0:CW]).then_inc(free[i], 1)
                if name == "bq_bk":
                    for i in range(TT):
                        act.copy(zqk[:, 384 * i:384 * i + 384], pz[i][:, 0:384]).then_inc(free[i], 1)
                if name == "bv":
                    for i in range(TT):
                        act.copy(bv[:, i, :], pz[i][:, 0:BW]).then_inc(free[i], 1)
                if name == "bg":
                    act.wait_ge(sem["rotated"], 1)
                    for i in range(TT):
                        act.activation(bg[:, i, :], pz[i][:, 0:BW], ACT.Silu).then_inc(free[i], 1)

            def side_work(sl):
                g, kt = sl // KT + 1, sl % KT
                if kt == 0 and g - 1 < N_IN:
                    evacuate(g - 1)
                if sl == 3:
                    act.wait_ge(sem["f_ready"], 1)
                    link(act.activation(fa, fa, ACT.Sqrt))
                    act.activation(fa, fa, ACT.Ln).then_inc(sem["log_ready"], 1)
                n = sl - LV0
                if 0 <= n <= LEVELS:
                    act.wait_ge(sem["diff_ready"], n + 1)
                    act.activation(diff[n % 2], diff[n % 2], ACT.Exp, scale=2.0).then_inc(sem["decay_ready"], 1)
                    if n == LEVELS:
                        act.wait_ge(sem["factors"], LEVELS)
                        act.activation(diff[0], cum, ACT.Exp, scale=2.0).then_inc(sem["decay_ready"], 1)
                        act.activation(glast[:], cum.rearrange("p (f c t) -> p f c t", f=2, c=TT)[:, :, :, P - 1],
                                       ACT.Exp, scale=2.0).then_inc(sem["decay_ready"], 1)
                if sl == A_KEYS + 1:
                    for c in range(TT - 1):
                        src, free = filled(act, ("kdT", c))
                        act.copy(kd[:, c, :], src[:, 0:AW]).then_inc(free, 1)
                if sl == A_OUT + 1:
                    for c in range(TT):
                        src, free = filled(act, ("ao", c))
                        act.copy(y[:, c, 0:AW], src[:, 0:AW]).then_inc(free, 1)
                    for c in range(TT):
                        was_read(act, ("ao", c))
                        link(act.activation(junk[:], y[:, c, 0:AW], ACT.Square, accum_out=a_ms[:, c:c + 1]))
                    act.sem_inc(sem["a_squares"], 1)
                if sl == A_OUT + 3:
                    act.wait_ge(sem["a_mean"], 1)
                    act.activation(a_ms[:], a_ms[:], ACT.Sqrt).then_inc(sem["a_root"], 1)
                i = sl - C0
                if 0 <= i - 1 < len(C_ITEMS):
                    n = P * (C_ITEMS[i - 1][0] + 1)
                    src, free = filled(act, ("cT", i - 1))
                    if i - 1 >= 2:
                        act.wait_ge(sem["pv_done"], i - 2)
                    act.copy(prT[(i - 1) % 2][:, 0:n], src[:, 0:n]).then_inc(free, 1)
                if 0 <= i < len(C_ITEMS):
                    n = P * (C_ITEMS[i][0] + 1)
                    was_read(act, ("cs", i))
                    act.activation(pr[i % 2][:, 0:n], pr[i % 2][:, 0:n], ACT.Exp, bias=nmax[:, i:i + 1],
                                   scale=-1.0, accum_out=den[:, i:i + 1]).then_inc(sem["exp_done"], 1)
                if sl == B_QKT:
                    act.wait_ge(sem["y_ready"], 1)
                    for k in range(4):
                        src, free = filled(act, ("bT", k))
                        act.copy(qkT[:, k, :], src[:]).then_inc(free, 1)
                if sl == B_OUT:
                    for c in range(TT):
                        src, free = filled(act, ("bo", c))
                        act.copy(y[:, c, AW:AW + BW], src[:, 0:BW]).then_inc(free, 1)
                if sl == N_SLOT + 1:
                    act.wait_ge(sem["b_mean"], 1)
                    act.activation(b_ms[:], b_ms[:], ACT.Sqrt).then_inc(sem["b_root"], 1)

            norm_square(act, x, y, ssq, sem["squares_done"])
            norm_root(act, ssq, sem)
            for i in range(2 * TT):
                hi_rows("hT", i)
            for g in range(N_IN):
                for kt in range(KT):
                    split(g, kt)
                    if g:
                        side_work(slot(g, kt))
            for sl in range(N_SLOT, N_SLOT + N_TAIL):
                side_work(sl)
            for i in range(2 * TT):
                hi_rows("yT", i)
            for g in range(N_IN, len(GROUPS)):
                for kt in range(KT):
                    split(g, kt)

        @block.vector
        def _(dve):
            link = chain(dve, sem["dve_chain"])
            ones = cst("ones")

            def lo_rows(name, i, n):
                t, half = i // 2, i % 2
                src, free = filled(dve, (name, i))
                dve.wait_ge(sem["aT_hi"], n + 1)
                cols = a_hi[:, 4 * half:4 * half + 4, tile_cols(t)]
                dve.tensor_tensor(a_lo[:, 4 * half:4 * half + 4, tile_cols(t)],
                                  src[:].rearrange("p (k t) -> p k t", k=4), cols, ALU.subtract).then_inc(free, 1)

            def split(g, kt):
                u, width = g * KT + kt, GROUPS[g][2]
                dve.wait_ge(sem["hi_split"], u + 1)
                dve.tensor_tensor(w_lo[:, u % RING, 0:width], raw[:, g % 2, kt, 0:width],
                                  w_hi[:, u % RING, 0:width], ALU.subtract).then_inc(sem["lo_split"], 1)

            def gates():
                evacuated(dve, 0)
                link(dve.tensor_scalar(qa, qa, A_DK ** -0.5, None, ALU.mult))
                for i in range(2):
                    c = slice(S * i, S * i + S)
                    link(dve.tensor_scalar(ka[:, c], ka[:, c], omlb[:, i:i + 1], None, ALU.mult))
                    link(dve.tensor_scalar(fa[:, c], fa[:, c], omlb[:, i:i + 1], lb[:, i:i + 1], ALU.mult, ALU.add))
                dve.tensor_scalar(fa, fa, MIN_FORGET, None, ALU.max).then_inc(sem["f_ready"], 1)

            def factors(n):
                dve.wait_ge(sem["decay_ready"], n + 1 if n < LEVELS else n + 3)
                if n >= 2:
                    filled(dve, ("level", n - 2, TT - 1))
                    dve.wait_ge(sem["factors"], n - 1)
                qd = diff[n % 2] if n < LEVELS else diff[0]
                link(dve.tensor_tensor(qf[n % 2], qa, qd, ALU.mult))
                dve.tensor_tensor(kf[n % 2], ka, diff[n % 2], ALU.mult).then_inc(sem["factors"], 1)

            def exponents(n):
                if n >= 2:
                    dve.wait_ge(sem["factors"], n - 1)
                out = diff[n % 2]
                if n == LEVELS:
                    src = cum.rearrange("p (b h) -> p b h", h=P)
                    dve.tensor_tensor(out.rearrange("p (b h) -> p b h", h=P),
                                      src[:, :, P - 1:P].broadcast_to([P, 2 * TT, P]), src,
                                      ALU.subtract).then_inc(sem["diff_ready"], 1)
                    return
                h = 1 << n
                src = cum.rearrange("p (b h) -> p b h", h=2 * h)
                out = out.rearrange("p (b h) -> p b h", h=2 * h)
                ref = src[:, :, h - 1:h].broadcast_to([P, S // h, h])
                link(dve.tensor_tensor(out[:, :, h:2 * h], src[:, :, h:2 * h], ref, ALU.subtract))
                dve.tensor_tensor(out[:, :, 0:h], ref, src[:, :, 0:h], ALU.subtract).then_inc(sem["diff_ready"], 1)

            def place(n):
                mask = T["masks"][:, P * n:P * n + P]
                for c in range(TT):
                    src, free = filled(dve, ("level", n, c))
                    if n:
                        was_read(dve, ("level", n - 1, c))
                    dve.copy_predicated(sa[:, c, :].rearrange("p (h q) -> p h q", h=A_H), spread(mask, A_H),
                                        src[:].rearrange("p (h q) -> p h q", h=A_H)).then_inc(free, 1)

            def states_a():
                for c in range(TT - 1):
                    src, free = filled(dve, ("aU", c))
                    if c:
                        was_read(dve, ("aU", c - 1))
                    for h in range(A_H):
                        r, v = head_rows(h), slice(64 * h, 64 * h + 64)
                        if c == 0:
                            last = dve.tensor_copy(st_a[r, 0, v], src[r, v])
                        else:
                            last = dve.scalar_tensor_tensor(st_a[r, c, v], st_a[r, c - 1, v],
                                                            glast[r, h // 2, c:c + 1], src[r, v], ALU.mult, ALU.add)
                    last.then_inc(free, 1)

            def finish_a():
                dve.wait_ge(sem["a_root"], 1)
                link(dve.reciprocal(a_ms[:], a_ms[:]))
                for c in range(TT):
                    last = dve.scalar_tensor_tensor(y[:, c, 0:AW], y[:, c, 0:AW], a_ms[:, c:c + 1], norm_a[:],
                                                    ALU.mult, ALU.mult)
                link(last)
                dve.tensor_tensor(y[:, :, 0:AW], y[:, :, 0:AW], aig[:, :, AW:2 * AW],
                                  ALU.mult).then_inc(sem["y_ready"], 1)

            def rotate():
                evacuated(dve, 5)
                dve.wait_ge(sem["trig"], 16)
                dve.wait_ge(sem["zeroed"], 2)
                z = zqk.rearrange("p (t h d) -> p t h d", t=TT, d=B_DK)
                z1, z2 = z[:, :, :, 0:HALF], z[:, :, :, HALF:B_DK]
                n = TT * 8 * HALF
                cos = trig[:, 0:n].rearrange("p (t h d) -> p t h d", t=TT, d=HALF)
                sin = trig[:, n:2 * n].rearrange("p (t h d) -> p t h d", t=TT, d=HALF)
                t1, t2 = (y[:, :, AW + k:AW + k + 8 * HALF].rearrange("p t (h d) -> p t h d", d=HALF)
                          for k in (0, 8 * HALF))
                link(dve.tensor_tensor(t1, z1, cos, ALU.mult))
                link(dve.tensor_tensor(t2, z2, sin, ALU.mult))
                link(dve.tensor_tensor(rqk[:, :, :, 0:HALF], t1, t2, ALU.subtract))
                link(dve.tensor_tensor(t1, z1, sin, ALU.mult))
                link(dve.tensor_tensor(t2, z2, cos, ALU.mult))
                dve.tensor_tensor(rqk[:, :, :, HALF:B_DK], t1, t2, ALU.add).then_inc(sem["rotated"], 1)

            def mask_b():
                filled(dve, ("ao", TT - 1))
                for c in range(TT):
                    src, free = filled(dve, ("bs", c))
                    dve.tensor_tensor(sa[:, c, :].rearrange("p (h q) -> p h q", h=B_H),
                                      src[:].rearrange("p (h q) -> p h q", h=B_H), spread(cst("causal"), B_H),
                                      ALU.mult).then_inc(free, 1)

            def states_b():
                for c in range(TT - 1):
                    src, free = filled(dve, ("bU", c))
                    if c:
                        was_read(dve, ("bU", c - 1))
                    for h in range(B_H):
                        r, v = head_rows(h), slice(B_DV * h, B_DV * (h + 1))
                        if c == 0:
                            last = dve.tensor_copy(st_b[r, 0, v], src[r, v])
                        else:
                            last = dve.tensor_tensor(st_b[r, c, v], st_b[r, c - 1, v], src[r, v], ALU.add)
                    last.then_inc(free, 1)

            def norm_heads_b():
                for c in range(TT):
                    was_read(dve, ("bo", c))
                yb = y[:, :, AW:AW + BW].rearrange("p t (h d) -> p t h d", h=B_H)
                mu = b_mu[:].rearrange("p (t h o) -> p t h o", t=TT, o=1)
                sq = zqk.rearrange("p (a d) -> p a d", d=B_DV)
                link(dve.tensor_reduce(b_mu[:].rearrange("p (t h) -> p t h", t=TT), yb, AX.X, ALU.add))
                link(dve.tensor_scalar(b_mu[:], b_mu[:], 1.0 / B_DV, None, ALU.mult))
                link(dve.tensor_tensor(yb, yb, mu.broadcast_to([P, TT, B_H, B_DV]), ALU.subtract))
                link(dve.tensor_tensor(sq.rearrange("p (t h) d -> p t h d", t=TT), yb, yb, ALU.mult))
                link(dve.tensor_reduce(b_ms[:], sq, AX.X, ALU.add))
                dve.tensor_scalar(b_ms[:], b_ms[:], 1.0 / B_DV, EPS, ALU.mult, ALU.add).then_inc(sem["b_mean"], 1)

            def finish_b():
                dve.wait_ge(sem["b_root"], 1)
                link(dve.reciprocal(b_ms[:], b_ms[:]))
                yb = y[:, :, AW:AW + BW]
                rs = b_ms[:].rearrange("p (t h o) -> p t h o", t=TT, o=1)
                yh = yb.rearrange("p t (h d) -> p t h d", h=B_H)
                link(dve.tensor_tensor(yh, yh, rs.broadcast_to([P, TT, B_H, B_DV]), ALU.mult))
                link(dve.tensor_tensor(yb, yb, spread(norm_b[:], TT), ALU.mult))
                evacuated(dve, 7)
                dve.tensor_tensor(yb, yb, bg, ALU.mult).then_inc(sem["y_ready"], 1)

            def attend_max(i):
                t, h = C_ITEMS[i]
                n = P * (t + 1)
                src, free = filled(dve, ("cs", i))
                if i >= 2:
                    filled(dve, ("cT", i - 2))
                dve.tensor_tensor_reduce(pr[i % 2][:, 0:n], src[:, 0:n], bias[:, h, 512 - n:512], 1.0, 3.0e38,
                                         ALU.add, ALU.min, nmax[:, i:i + 1]).then_inc(free, 1)

            def finish_c(t):
                dve.wait_ge(sem["pv_done"], C_H * (t + 1))
                d = slice(C_H * t, C_H * t + C_H)
                link(dve.reciprocal(rden[:, d], den[:, d]))
                dve.tensor_tensor(y[:, t, AW + BW:D].rearrange("p (h d) -> p h d", h=C_H),
                                  side[3][:, 0:CW].rearrange("p (h d) -> p h d", h=C_H),
                                  each(rden[:, d], C_DH), ALU.mult).then_inc(sem["side_free3"], 1)

            def side_work(sl):
                if sl == 2:
                    gates()
                if sl == 4:
                    dve.wait_ge(sem["log_ready"], 1)
                    for c in range(2 * TT):
                        v = slice(P * c, P * c + P)
                        last = dve.tensor_tensor_scan(cum[:, v], ones, fa[:, v], 0.0, ALU.mult, ALU.add)
                    link(last)
                n = sl - LV0
                if 0 <= n - 1 <= LEVELS:
                    factors(n - 1)
                if 0 <= n <= LEVELS:
                    exponents(n)
                if 0 <= sl - A_LEVEL - 1 <= LEVELS:
                    if sl == A_LEVEL + 1:
                        dve.wait_ge(sem["zeroed"], 1)
                    place(sl - A_LEVEL - 1)
                if sl == A_STATE + 1:
                    states_a()
                if sl == A_OUT + 2:
                    dve.wait_ge(sem["a_squares"], 1)
                    dve.tensor_scalar(a_ms[:], a_ms[:], 1.0 / AW, EPS, ALU.mult, ALU.add).then_inc(sem["a_mean"], 1)
                if sl == A_OUT + 4:
                    finish_a()
                i = sl - C0
                if 0 <= i < len(C_ITEMS):
                    attend_max(i)
                if 0 <= i - 3 < len(C_ITEMS) and C_ITEMS[i - 3][1] == C_H - 1:
                    finish_c(C_ITEMS[i - 3][0])
                if sl == B_ROT:
                    rotate()
                if sl == B_SC:
                    mask_b()
                if sl == B_STATE:
                    states_b()
                if sl == B_OUT + 1:
                    norm_heads_b()
                if sl == N_SLOT + 3:
                    finish_b()

            dve.wait_ge(sem["small"], 64)
            link(dve.tensor_scalar(omlb[:], lb[:], -1.0, 1.0, ALU.mult, ALU.add))
            norm_scale(dve, link, x, y, norm_w, ssq, sem)
            for i in range(2 * TT):
                lo_rows("hT", i, i)
            for g in range(N_IN):
                for kt in range(KT):
                    split(g, kt)
                    if g:
                        side_work(slot(g, kt))
            for sl in range(N_SLOT, N_SLOT + N_TAIL):
                side_work(sl)
            for i in range(2 * TT):
                lo_rows("yT", i, 2 * TT + i)
            for g in range(N_IN, len(GROUPS)):
                for kt in range(KT):
                    split(g, kt)
                    if g > N_IN and kt == 2:
                        add_out(dve, g - 1)
            add_out(dve, len(GROUPS) - 1)


MIXER_SEMS = (["small", "raw0", "raw1", "trig", "lo_split", "hi_split", "unit_done", "zeroed", "factors",
               "squares_done", "mean_ready", "root_ready", "xn_ready", "aT_hi", "act_chain", 
               "dve_chain", "f_ready", "log_ready", "diff_ready", "decay_ready", "a_squares", "a_mean",
               "a_root", "b_mean", "b_root", "rotated", "y_ready", "exp_done", "pv_done"]
              + [f"pz_free{i}" for i in range(4)] + [f"side_full{i}" for i in range(4)]
              + [f"side_free{i}" for i in range(4)])


def router_block(nc, l, T, args, cst, sem):
    x, pz, side = T["x"], T["pz"], T["side"]
    with ExitStack() as ctx:
        def sb(name, shape, dt=F32):
            return ctx.enter_context(nc.sbuf_tensor(name, [P] + shape, dt))

        h = sb("h", [TT, D])
        hT = sb("hT", [KT, S])
        w_router = sb("w_router", [KT, NG + NE])
        ffn_w = sb("ffn_w", [D])
        ssq = sb("r_ssq", [TT])
        lg = sb("lg", [TT, 8])
        gtop = sb("gtop", [TT, 8])
        gtop_i = sb("gtop_i", [TT, 8], U32)
        gidx = sb("gidx", [TT])
        pgrp = sb("pgrp", [TT, NG])
        psum_ = sb("psum_", [TT])
        picked = sb("picked", [TT, NG])
        penalty = sb("penalty", [TT, NG])
        le = sb("le", [TT, NE])
        etop = sb("etop", [TT, 8])
        etop_i = sb("etop_i", [TT, 8], U32)
        e2 = sb("e2", [TT])
        both = sb("both", [TT, NE])
        cumr = sb("cumr", [TT, NE])
        prod = sb("prod", [TT * 2, NE])
        over = sb("over", [MAX_ROUNDS])
        most = sb("most", [2])
        one, gate, rank = T["one"], T["gate"], T["rank"]
        e_f = T["expert"]
        block = ctx.enter_context(nc.Block())

        @block.sync
        def _(sp):
            sp.dma_start(ffn_w[:], args["norm_ffn"][l].partition_broadcast(P)).then_inc(sem["small"], 16)
            sp.dma_start(w_router[:, :, 0:NG],
                         args["router_group"].rearrange("l (p k) n -> l p k n", k=KT)[l]).then_inc(sem["small"], 16)
            sp.dma_start(w_router[:, :, NG:NG + NE],
                         args["router_expert"].rearrange("l (p k) n -> l p k n", k=KT)[l]).then_inc(sem["small"], 16)
            for t in range(TT):
                sp.wait_ge(sem["xn_ready"], t + 1)
                sp.dma_start(T["h_dram"][P * t:P * t + P, :], h[:, t, :]).then_inc(sem["h_stored"], 16)
            sp.wait_ge(sem["h_stored"], 16 * TT)

        @block.tensor
        def _(pe):
            ident = cst("ident")
            for i in range(2 * TT):
                t, half = i // 2, i % 2
                pe.wait_ge(sem["xn_ready"], t + 1)
                if i >= 4:
                    pe.wait_ge(sem["hT_ready"], i - 3)
                for k in range(4):
                    last = pe.transpose(side[i % 4][:, P * k:P * k + P],
                                        h[:, t, :].rearrange("p (f k) -> p k f", k=KT)[:, 4 * half + k, :], ident)
                last.then_inc(sem["hT_turned"], 1)
            pe.wait_ge(sem["small"], 48)
            for t in range(TT):
                pe.wait_ge(sem["hT_ready"], 2 * t + 2)
                for kt in range(KT):
                    last = pe.matmul(pz[t][:, 0:NG + NE], hT[:, kt, tile_cols(t)], w_router[:, kt, :],
                                     start=(kt == 0), stop=(kt == KT - 1))
                last.then_inc(sem["logits"], 1)
            pe.wait_ge(sem["both_ready"], 1)
            for t in range(TT):
                for n in range(t + 1):
                    last = pe.matmul(side[0][:, NE * t:NE * t + NE], cst("before") if n == 0 else cst("ones"),
                                     both[:, t if n == 0 else n - 1, :], start=(n == 0), stop=(n == t))
            for n in range(TT):
                last = pe.matmul(side[1][:, 0:NE], cst("ones"), both[:, n, :], start=(n == 0), stop=(n == TT - 1))
            last.then_inc(sem["counted"], 1)

        @block.scalar
        def _(act):
            norm_square(act, x, h, ssq, sem["squares_done"])
            norm_root(act, ssq, sem)
            for i in range(2 * TT):
                t, half = i // 2, i % 2
                act.wait_ge(sem["hT_turned"], i + 1)
                act.copy(hT[:, 4 * half:4 * half + 4, tile_cols(t)],
                         side[i % 4][:].rearrange("p (k t) -> p k t", k=4)).then_inc(sem["hT_ready"], 1)
            act.wait_ge(sem["exp_args"], 1)
            act.activation(pgrp[:], pgrp[:], ACT.Exp).then_inc(sem["exps"], 1)
            act.wait_ge(sem["exp_args"], 2)
            act.activation(e2[:], e2[:], ACT.Exp).then_inc(sem["exps"], 1)

        @block.vector
        def _(dve):
            link = chain(dve, sem["dve_chain"])
            dve.wait_ge(sem["small"], 48)
            link(dve.memset(lg[:], NEG))
            norm_scale(dve, link, x, h, ffn_w[:], ssq, sem)
            for t in range(TT):
                dve.wait_ge(sem["logits"], t + 1)
                dve.tensor_copy(lg[:, t, 0:NG], pz[t][:, 0:NG])
                last = dve.tensor_copy(le[:, t, :], pz[t][:, NG:NG + NE])
            link(last)
            for t in range(TT):
                link(dve.max(gtop[:, t, :], lg[:, t, :]))
                last = dve.max_index(gtop_i[:, t, :], gtop[:, t, :], lg[:, t, :])
            link(last)
            link(dve.tensor_copy(gidx[:], gtop_i[:, :, 0]))
            dve.tensor_tensor(pgrp[:], lg[:, :, 0:NG], gtop[:, :, 0:1].broadcast_to([P, TT, NG]),
                              ALU.subtract).then_inc(sem["exp_args"], 1)
            link(dve.tensor_tensor(picked[:], spread(cst("groups"), TT), each(gidx[:], NG), ALU.is_equal))
            link(dve.tensor_scalar(penalty[:], picked[:], -1.0, -NEG, ALU.add, ALU.mult))
            lev = le[:].rearrange("p t (g e) -> p (t g) e", g=NG)
            link(dve.tensor_tensor(lev, lev, each(picked[:].rearrange("p t g -> p (t g)"), EPG), ALU.mult))
            link(dve.tensor_tensor(lev, lev, each(penalty[:].rearrange("p t g -> p (t g)"), EPG), ALU.add))
            for t in range(TT):
                link(dve.max(etop[:, t, :], le[:, t, :]))
                last = dve.max_index(etop_i[:, t, :], etop[:, t, :], le[:, t, :])
            link(last)
            dve.tensor_tensor(e2[:], etop[:, :, 1], etop[:, :, 0], ALU.subtract).then_inc(sem["exp_args"], 1)
            link(dve.tensor_copy(e_f[:], etop_i[:, :, 0:2]))
            link(dve.tensor_tensor(one[:], spread(cst("experts"), 2 * TT),
                                   each(e_f[:].rearrange("p t k -> p (t k)"), NE), ALU.is_equal))
            ov = one[:].rearrange("p (t k) e -> p t k e", k=2)
            dve.tensor_tensor(both[:], ov[:, :, 0, :], ov[:, :, 1, :], ALU.add).then_inc(sem["both_ready"], 1)
            for t in range(TT):
                last = dve.tensor_scalar(T["token_at"][:, 2 * t:2 * t + 2, :], one[:, 2 * t:2 * t + 2, :],
                                         cst("token")[:, t:t + 1], None, ALU.mult)
            link(last)
            dve.wait_ge(sem["exps"], 2)
            link(dve.tensor_reduce(psum_[:], pgrp[:], AX.X, ALU.add))
            link(dve.tensor_scalar(gidx[:], e2[:], 1.0, None, ALU.add))
            link(dve.tensor_tensor(psum_[:], psum_[:], gidx[:], ALU.mult))
            link(dve.reciprocal(gate[:, :, 0], psum_[:]))
            link(dve.tensor_tensor(gate[:, :, 1], gate[:, :, 0], e2[:], ALU.mult))
            dve.wait_ge(sem["counted"], 1)
            link(dve.tensor_copy(cumr[:].rearrange("p t e -> p (t e)"), side[0][:, 0:TT * NE]))
            for k in range(2):
                last = dve.tensor_tensor(prod[:].rearrange("p (t k) e -> p t k e", k=2)[:, :, k, :], ov[:, :, k, :],
                                         cumr[:], ALU.mult)
            link(last)
            link(dve.tensor_reduce(rank[:].rearrange("p t k -> p (t k)"), prod[:], AX.X, ALU.add))
            link(dve.tensor_reduce(most[:, 0:1], side[1][:, 0:NE], AX.X, ALU.max))
            link(dve.tensor_scalar(over[:], cst("limits"), most[:, 0:1], None, ALU.is_lt))
            link(dve.tensor_reduce(most[:, 1:2], over[:], AX.X, ALU.add))
            link(dve.tensor_scalar(T["rounds"][:], most[:, 1:2], 1.0, None, ALU.add))


ROUTER_SEMS = ["small", "h_stored", "xn_ready", "hT_ready", "hT_turned", "logits", "both_ready", "counted",
               "squares_done", "mean_ready", "root_ready", "exp_args", "exps", "dve_chain"]

UW = 1024
HEAD, BODY = 8, 12
E_RING = 8
SLOTS = 6
ON_POOL = (3, 9)


def place_of(j):
    return ((HEAD + j) // 2) % SLOTS


def ring_of(par, j):
    return (HEAD + BODY * par + j) % E_RING


def low_done(j):
    own = [k for k in range(j + 1) if (k in ON_POOL) == (j in ON_POOL)]
    return j in ON_POOL, len(own)


def expert_block(nc, l, T, args, cst, sem):
    x, pz, pz_all, side = T["x"], T["pz"], T["pz_all"], T["side"]
    weights = [args["expert_w_gate"].rearrange("l e (p k) n -> l e p (k n)", k=KT),
               args["expert_w_up"].rearrange("l e (p k) n -> l e p (k n)", k=KT),
               args["expert_w_down"].rearrange("l e (p k) n -> l e p (k n)", k=FT)]
    rank, gate, e_f = T["rank"], T["gate"], T["expert"]
    with ExitStack() as ctx:
        def sb(name, shape, dt=F32):
            return ctx.enter_context(nc.sbuf_tensor(name, [P] + shape, dt))

        raw = sb("e_raw", [SLOTS, 2 * UW])
        w_hi = sb("e_hi", [E_RING, UW], F32R)
        w_lo = sb("e_lo", [E_RING, UW], F32R)
        xg = sb("xg", [D])
        xs = sb("xs", [2, KT, P], F32R)
        hit = sb("hit", [2 * TT, P])
        idx = sb("idx", [PAIRS], I32)
        idx1 = sb("idx1", [1], I32)
        g_sb = sb("g_sb", [DE])
        u_sb = sb("u_sb", [DE])
        act_g = sb("act_g", [FT * CAP])
        hid = sb("hid", [FT * CAP])
        hs = sb("hs", [FT, P], F32R)
        y_low = sb("y_low", [D])
        y_sb = sb("y_sb", [D])
        yg = sb("yg", [2, D])
        inr = sb("inr", [2 * TT])
        tmp = sb("tmp", [2 * TT])
        wgt = sb("wgt", [2 * TT])
        row = sb("row", [2 * TT], I32)
        block = ctx.enter_context(nc.Block())
        y_rows = T["y_dram"].rearrange("(p s) d -> p s d", s=P)

        def wait_split(eng, b, j):
            on_pool, n = low_done(j)
            if on_pool:
                eng.wait_ge(sem["lo_pool"], len(ON_POOL) * b + n)
            else:
                eng.wait_ge(sem["lo_split"], (BODY - len(ON_POOL)) * b + (HEAD + n))

        def wait_used(eng, n):
            eng.wait_ge(sem["unit_done"], n + E_RING)

        @block.sync
        def _(sp):
            def load(place, w, e, half):
                sp.dma_start(raw[:, place, :], weights[w][l, e][:, 2 * UW * half:2 * UW * (half + 1)]
                             ).then_inc(sem[f"w{place}"], 16)

            for j in range(0, HEAD, 2):
                load(j // 2, j // 4, 0, (j // 2) % 2)
            for j in range(0, BODY, 2):
                if j >= 4:
                    sp.wait_ge(sem["lo_split"], j - 2)
                load(place_of(j), j // 4, 1 if j < 8 else 0, (j // 2) % 2)
            with sp.Fori(1, NE - 1) as b:
                for j in range(0, BODY, 2):
                    for k in (j, j + 1):
                        wait_split(sp, b - 1, k)
                        sp.sem_inc(sem["sp_passed"], 1)
                    load(place_of(j), j // 4, b + 1 if j < 8 else b, (j // 2) % 2)
            for j in range(0, 4, 2):
                wait_split(sp, NE - 2, j)
                wait_split(sp, NE - 2, j + 1)
                load(place_of(j), 2, NE - 1, j // 2)

        @block.gpsimd
        def _(pool):
            def gather(pair):
                column = idx[:, pair:pair + 1] if isinstance(pair, int) else idx[:, bass.ds(pair, 1)]
                pool.tensor_copy(idx1[:], column).then_inc(sem["idx_copied"], 1)
                pool.wait_ge(sem["idx_copied"], pair + 1)
                if not isinstance(pair, int):
                    pool.sem_inc(sem["pool_passed"], 1)
                pool.indirect_dma_start(xg[:], None, T["h_dram"], bass.IndirectOffsetOnAxis(ap=idx1[:, 0:1], axis=0)
                                        ).then_inc(sem["gathered"], 16)

            def body(b, par, pair=None):
                for j in ON_POOL:
                    pool.wait_ge(sem["hi_split"], BODY * b + (HEAD + j + 1))
                    place, cols, r = place_of(j), slice(UW * (j % 2), UW * (j % 2) + UW), ring_of(par, j)
                    pool.tensor_tensor(w_lo[:, r, :], raw[:, place, cols], w_hi[:, r, :],
                                       ALU.subtract).then_inc(sem["lo_pool"], 1)
                if pair is not None:
                    pool.wait_ge(sem["xg_turned"], 2 * pair)
                    gather(pair)

            pool.wait_ge(sem["idx_ready"], 1)
            gather(0)
            pool.wait_ge(sem["xg_turned"], 2)
            gather(1)
            body(0, 0)
            with pool.Fori(0, (NE - 4) // 2) as p:
                body(2 * p + 1, 1, p + 2)
                body(2 * p + 2, 0)
            body(NE - 3, 1)
            body(NE - 2, 0)
            pool.wait_ge(sem["hi_split"], BODY * (NE - 1) + HEAD + 4)
            pool.tensor_tensor(w_lo[:, ring_of(1, 3), :], raw[:, place_of(3), UW:2 * UW], w_hi[:, ring_of(1, 3), :],
                               ALU.subtract).then_inc(sem["lo_pool"], 1)
            pool.wait_ge(sem["y_stored"], 16 * (PAIRS + 1))
            for n in range(2 * TT):
                if n >= 2:
                    pool.wait_ge(sem["combined"], n - 1)
                pool.indirect_dma_start(yg[:, n % 2, :], None, T["y_dram"],
                                        bass.IndirectOffsetOnAxis(ap=row[:, n:n + 1], axis=0)
                                        ).then_inc(sem[f"fetched{n % 2}"], 16)
            pool.wait_ge(sem["combined"], 2 * TT)
            nums = sorted(sem[k].num for k in ("gathered", "fetched0", "fetched1"))
            pool.dma_reset(range(nums[0], nums[-1] + 1))

        @block.tensor
        def _(pe):
            ident = cst("ident")

            def into(bank, par_x, j, r):
                for k in range(2):
                    kt = 2 * j + k
                    for n, w in enumerate((w_hi, w_lo)):
                        last = pe.matmul(pz[bank][:], xs[:, par_x, kt, :], w[:, r, 512 * k:512 * k + 512],
                                         start=(kt == 0 and n == 0), stop=(kt == KT - 1 and n == 1))
                last.then_inc(sem["unit_done"], 1)

            def down(f, r):
                for n, w in enumerate((w_hi, w_lo)):
                    for c in range(2):
                        last = pe.matmul(pz[2 + c][:], hs[:, f, :], w[:, r, 512 * c:512 * c + 512],
                                         start=(f == 0 and n == 0), stop=(f == FT - 1 and n == 1))
                last.then_inc(sem["unit_done"], 1)

            def sum_turn(b):
                pe.wait_ge(sem["g_copied"], b + 1)
                pe.wait_ge(sem["u_copied"], b + 1)
                for n, src in enumerate((g_sb, u_sb)):
                    for f in range(FT):
                        c = CAP * (FT * n + f)
                        last = pe.matmul(side[2][:, c:c + CAP], src[:].rearrange("p (f k) -> p k f", k=FT)[:, f, :],
                                         cst("stack"), start=True, stop=True)
                last.then_inc(sem["gu_turned"], 1)

            def body(b, par, pair=None):
                pe.wait_ge(sem["xs_ready"], b + 2)
                pe.wait_ge(sem["g_copied"], b + 1)
                for j in range(8):
                    if j == 2:
                        sum_turn(b)
                    if j == 5 and pair is not None:
                        pe.wait_ge(sem["gathered"], 16 * pair + 16)
                    if j == 6 and pair is not None:
                        turn(par)
                    wait_split(pe, b, j)
                    into(j // 4, 1 - par, j % 4, ring_of(par, j))
                pe.wait_ge(sem["hs_ready"], b + 1)
                pe.wait_ge(sem["y_read"], b + 1)
                for j in range(8, BODY):
                    wait_split(pe, b, j)
                    down(j - 8, ring_of(par, j))

            def turn(par):
                rows = slice(CAP * par, CAP * par + CAP)
                for kt in range(KT):
                    last = pe.transpose(side[par][:, CAP * kt:CAP * kt + CAP],
                                        xg[rows, :].rearrange("p (f k) -> p k f", k=KT)[:, kt, :], ident[rows, rows])
                last.then_inc(sem["xg_turned"], 1)

            pe.sem_inc(sem["unit_done"], E_RING)
            pe.wait_ge(sem["hit_ready"], 1)
            for n in range(2 * TT):
                last = pe.matmul(side[3][:, 0:NE], hit[:, n, :], T["token_at"][:, n, :], start=(n == 0),
                                 stop=(n == 2 * TT - 1))
            last.then_inc(sem["tokens_found"], 1)
            pe.wait_ge(sem["gathered"], 16)
            turn(0)
            turn(1)
            pe.wait_ge(sem["xs_ready"], 1)
            for j in range(HEAD):
                pe.wait_ge(sem["lo_split"], j + 1)
                into(j // 4, 0, j % 4, j)
            body(0, 0, 1)
            with pe.Fori(0, (NE - 4) // 2) as p:
                body(2 * p + 1, 1, p + 1)
                body(2 * p + 2, 0, p + 2)
            body(NE - 3, 1, PAIRS - 1)
            body(NE - 2, 0)
            sum_turn(NE - 1)
            pe.wait_ge(sem["hs_ready"], NE)
            pe.wait_ge(sem["y_read"], NE)
            for j in range(FT):
                wait_split(pe, NE - 1, j)
                down(j, ring_of(1, j))

        @block.scalar
        def _(act):
            def split(b, par, j):
                place, r = place_of(j), ring_of(par, j)
                if j % 2 == 0:
                    act.wait_ge(sem[f"w{place}"], 16 * b + (16 if j < 4 else 32))
                wait_used(act, BODY * b + (HEAD + j + 1 - E_RING))
                act.copy(w_hi[:, r, :], raw[:, place, UW * (j % 2):UW * (j % 2) + UW]).then_inc(sem["hi_split"], 1)

            def tokens_high(e, par):
                act.wait_ge(sem["xg_turned"], e + 1)
                act.copy(xs[:, par, :, 0:CAP], side[par][:].rearrange("p (k s) -> p k s", k=KT)
                         ).then_inc(sem["xs_hi"], 1)

            def gate_out(e, n):
                wait_used(act, n)
                act.copy(g_sb[:], pz[0][:]).then_inc(sem["g_copied"], 1)

            def silu(e):
                act.wait_ge(sem["gu_turned"], e + 1)
                act.activation(act_g[:], side[2][:, 0:FT * CAP], ACT.Silu).then_inc(sem["silu_done"], 1)

            def low_rows(n):
                wait_used(act, n)
                act.copy(y_low[0:CAP, :], pz_all[CAP:P, 2:4, :].rearrange("p a b -> p (a b)")
                         ).then_inc(sem["low_copied"], 1)

            def store(pair):
                act.wait_ge(sem["y_read"], 2 * pair + 3)
                act.dma_start(y_rows[pair], y_sb[:]).then_inc(sem["y_stored"], 16)

            def body(b, par, turns=True, results=True):
                for j in range(BODY):
                    split(b, par, j)
                    if j == 2 and results:
                        low_rows(BODY * b + HEAD)
                    if j == 4:
                        silu(b)
                    if j == 7:
                        gate_out(b + 1, BODY * b + (HEAD + 4))
                    if j == 8 and turns:
                        tokens_high(b + 2, par)

            act.sem_inc(sem["y_stored"], 16)
            act.preload_act_table(ACT.Silu)
            tokens_high(0, 0)
            tokens_high(1, 1)
            for j in range(HEAD):
                if j % 2 == 0:
                    act.wait_ge(sem[f"w{j // 2}"], 16)
                act.copy(w_hi[:, j, :], raw[:, j // 2, UW * (j % 2):UW * (j % 2) + UW]).then_inc(sem["hi_split"], 1)
            gate_out(0, 4)
            body(0, 0, results=False)
            with act.Fori(0, (NE - 4) // 2) as p:
                body(2 * p + 1, 1)
                body(2 * p + 2, 0)
                store(p)
            body(NE - 3, 1)
            body(NE - 2, 0, turns=False)
            store(PAIRS - 2)
            for j in range(FT):
                split(NE - 1, 1, j)
            low_rows(BODY * (NE - 1) + HEAD)
            silu(NE - 1)
            low_rows(BODY * (NE - 1) + HEAD + FT)
            store(PAIRS - 1)

        @block.vector
        def _(dve):
            link = chain(dve, sem["dve_chain"])

            def split(b, par, j):
                r = ring_of(par, j)
                dve.wait_ge(sem["hi_split"], BODY * b + (HEAD + j + 1))
                dve.tensor_tensor(w_lo[:, r, :], raw[:, place_of(j), UW * (j % 2):UW * (j % 2) + UW], w_hi[:, r, :],
                                  ALU.subtract).then_inc(sem["lo_split"], 1)

            def tokens_low(e, par):
                dve.wait_ge(sem["xs_hi"], e + 1)
                dve.tensor_tensor(xs[:, par, :, CAP:P], side[par][:].rearrange("p (k s) -> p k s", k=KT),
                                  xs[:, par, :, 0:CAP], ALU.subtract).then_inc(sem["xs_ready"], 1)

            def up_out(n):
                wait_used(dve, n)
                dve.tensor_copy(u_sb[:], pz[1][:]).then_inc(sem["u_copied"], 1)

            def hidden(e):
                dve.wait_ge(sem["silu_done"], e + 1)
                dve.tensor_tensor(hid[:], act_g[:], side[2][:, FT * CAP:2 * FT * CAP], ALU.mult
                                  ).then_inc(sem["hid_chain"], 1)
                h3 = hid[:].rearrange("p (f s) -> p f s", f=FT)
                dve.wait_ge(sem["hid_chain"], 2 * e + 1)
                dve.tensor_copy(hs[:, :, 0:CAP], h3).then_inc(sem["hid_chain"], 1)
                dve.wait_ge(sem["hid_chain"], 2 * e + 2)
                dve.tensor_tensor(hs[:, :, CAP:P], h3, hs[:, :, 0:CAP], ALU.subtract).then_inc(sem["hs_ready"], 1)

            def result(e, pair, par):
                if par == 0:
                    dve.wait_ge(sem["y_stored"], 16 * pair + 16)
                dve.wait_ge(sem["low_copied"], e + 1)
                dve.tensor_tensor(y_sb[CAP * par:CAP * par + CAP, :],
                                  pz_all[0:CAP, 2:4, :].rearrange("p a b -> p (a b)"), y_low[0:CAP, :],
                                  ALU.add).then_inc(sem["y_read"], 1)

            def body(b, par, pair=None, turns=True):
                for j in range(BODY):
                    if j not in ON_POOL:
                        split(b, par, j)
                    if j == 4 and pair is not None:
                        result(b - 1, pair, 1 - par)
                    if j == 6:
                        hidden(b)
                    if j == 8 and turns:
                        tokens_low(b + 2, par)
                    if j == 10:
                        up_out(BODY * b + (HEAD + 8))

            dve.sem_inc(sem["y_read"], 1)
            rk = rank[:].rearrange("p t k -> p (t k)")
            dve.tensor_tensor(hit[:], spread(cst("rows"), 2 * TT), each(rk, P), ALU.is_equal).then_inc(sem["hit_ready"], 1)
            dve.wait_ge(sem["tokens_found"], 1)
            pairs = side[3][:, 0:NE].rearrange("p (e two) -> p two e", two=2)
            dve.tensor_copy(idx[0:CAP, :], pairs[0:CAP, 0, :])
            dve.tensor_copy(idx[CAP:P, :], pairs[CAP:P, 1, :]).then_inc(sem["idx_ready"], 1)
            tokens_low(0, 0)
            tokens_low(1, 1)
            for j in range(HEAD):
                dve.wait_ge(sem["hi_split"], j + 1)
                dve.tensor_tensor(w_lo[:, j, :], raw[:, j // 2, UW * (j % 2):UW * (j % 2) + UW], w_hi[:, j, :],
                                  ALU.subtract).then_inc(sem["lo_split"], 1)
            link(dve.tensor_scalar(inr[:], rk, 0.0, None, ALU.is_ge))
            link(dve.tensor_scalar(tmp[:], rk, float(CAP), None, ALU.is_lt))
            link(dve.tensor_tensor(inr[:], inr[:], tmp[:], ALU.mult))
            link(dve.tensor_tensor(wgt[:], gate[:].rearrange("p t k -> p (t k)"), inr[:], ALU.mult))
            link(dve.scalar_tensor_tensor(tmp[:], e_f[:].rearrange("p t k -> p (t k)"), float(CAP), rk,
                                          ALU.mult, ALU.add))
            link(dve.tensor_tensor(tmp[:], tmp[:], inr[:], ALU.mult))
            link(dve.tensor_copy(row[:], tmp[:]))
            link(dve.tensor_scalar(rk, rk, -float(CAP), None, ALU.add))
            up_out(HEAD)
            body(0, 0)
            with dve.Fori(0, (NE - 4) // 2) as p:
                body(2 * p + 1, 1, p)
                body(2 * p + 2, 0, p)
            body(NE - 3, 1, PAIRS - 2)
            body(NE - 2, 0, PAIRS - 2, turns=False)
            for j in range(FT):
                if j not in ON_POOL:
                    split(NE - 1, 1, j)
            result(NE - 2, PAIRS - 1, 0)
            hidden(NE - 1)
            result(NE - 1, PAIRS - 1, 1)
            for n in range(2 * TT):
                dve.wait_ge(sem[f"fetched{n % 2}"], 16 * (n // 2 + 1))
                if n % 2:
                    dve.wait_ge(sem["combined"], n)
                xt = x[:, n // 2, :]
                dve.scalar_tensor_tensor(xt, yg[:, n % 2, :], wgt[:, n:n + 1], xt, ALU.mult,
                                         ALU.add).then_inc(sem["combined"], 1)


EXPERT_SEMS = (["lo_split", "lo_pool", "hi_split", "unit_done", "idx_ready", "idx_copied", "xg_turned", "gathered",
                "y_stored", "combined", "fetched0", "fetched1", "hit_ready", "tokens_found", "xs_ready", "xs_hi",
                "g_copied", "u_copied", "gu_turned", "hs_ready", "y_read", "silu_done", "low_copied", "hid_chain",
                "dve_chain", "sp_passed", "pool_passed"] + [f"w{k}" for k in range(SLOTS)])


def trunk(nc, args, out):
    with ExitStack() as ctx:
        T = {}

        def sb(name, shape, dt=F32):
            T[name] = ctx.enter_context(nc.sbuf_tensor(name, [P] + shape, dt))
            return T[name]

        x = sb("x", [TT, D])
        bias = sb("bias", [C_H, S])
        const = sb("const", [N_CONST])
        sb("masks", [(LEVELS + 1) * P], U8)
        sb("one", [2 * TT, NE])
        sb("token_at", [2 * TT, NE])
        sb("expert", [TT, 2])
        sb("gate", [TT, 2])
        sb("rank", [TT, 2])
        sb("rounds", [1], I32)
        lbs = sb("lbs", [DEPTH, 2])
        lt = sb("lt", [3, 2])
        T["h_dram"] = nc.dram_tensor("h_rows", [S, D], F32, kind="Internal").ap()
        T["y_dram"] = nc.dram_tensor("expert_rows", [NE * CAP, D], F32, kind="Internal").ap()
        T["lb_dram"] = nc.dram_tensor("lower_bounds", [DEPTH, P, 2], F32, kind="Internal").ap()
        T["pz_all"] = ctx.enter_context(nc.psum_tensor("pz", [P, 4, 512], F32))
        side = ctx.enter_context(nc.psum_tensor("side", [P, 4, 512], F32))
        T["pz"] = [T["pz_all"][:, i, :] for i in range(4)]
        T["side"] = [side[:, i, :] for i in range(4)]

        def cst(name):
            a, b = CONST[name]
            return const[:, a:b]

        pool_sems = ["gathered", "fetched0", "fetched1"]
        names = pool_sems + sorted((set(MIXER_SEMS) | set(ROUTER_SEMS) | set(EXPERT_SEMS) | {"ready"})
                                   - set(pool_sems))
        sem = {n: ctx.enter_context(nc.semaphore(n)) for n in names}
        numbers = range(min(s.num for s in sem.values()), max(s.num for s in sem.values()) + 1)

        def restart():
            nc.all_engine_barrier(sems_to_clear=numbers)

        xv = args["x"].rearrange("b (t p) d -> p (b t) d", p=P)
        ov = out.rearrange("b (t p) d -> p (b t) d", p=P)

        with nc.sbuf_tensor("masks_in", [P, (LEVELS + 1) * P], F32) as masks_in, nc.Block() as block:
            @block.sync
            def _(sp):
                sp.dma_start(lbs[:], args["hgrn_lb"]).then_inc(sem["ready"], 16)
                sp.dma_start(x[:], xv).then_inc(sem["small"], 16)
                sp.dma_start(const[:], args["const"]).then_inc(sem["small"], 16)
                sp.dma_start(masks_in[:], args["masks"]).then_inc(sem["small"], 16)
                sp.dma_start(bias[:], args["rel_bias"]).then_inc(sem["raw0"], 16)
                sp.wait_ge(sem["f_ready"], 1)
                for n in range(DEPTH):
                    sp.dma_start(T["lb_dram"][n], lbs[:, n, :]).then_inc(sem["raw1"], 16)
                sp.wait_ge(sem["raw1"], 16 * DEPTH)
                sp.wait_ge(sem["small"], 48)

            @block.scalar
            def _(act):
                act.wait_ge(sem["exp_args"], 1)
                act.activation(lt[:, 0:2, :], lt[:, 0:2, :], ACT.Exp).then_inc(sem["exps"], 1)

            @block.vector
            def _(dve):
                link = chain(dve, sem["dve_chain"])
                dve.wait_ge(sem["ready"], 16)
                link(dve.tensor_tensor(lt[:, 2, :], lbs[:, 0, :], lbs[:, 1, :], ALU.max))
                dve.tensor_tensor(lt[:, 0, :], lbs[:, 0, :], lt[:, 2, :], ALU.subtract)
                dve.tensor_tensor(lt[:, 1, :], lbs[:, 1, :], lt[:, 2, :], ALU.subtract).then_inc(sem["exp_args"], 1)
                dve.wait_ge(sem["exps"], 1)
                link(dve.tensor_tensor(lt[:, 2, :], lt[:, 0, :], lt[:, 1, :], ALU.add))
                link(dve.reciprocal(lt[:, 2, :], lt[:, 2, :]))
                link(dve.memset(lbs[:, 0, :], 0.0))
                dve.tensor_tensor(lbs[:, 1, :], lt[:, 1, :], lt[:, 2, :], ALU.mult).then_inc(sem["f_ready"], 1)
                dve.wait_ge(sem["small"], 48)
                dve.tensor_copy(T["masks"][:], masks_in[:])
                dve.wait_ge(sem["raw0"], 16)
                link(dve.tensor_scalar(bias[:], bias[:], -1.0, None, ALU.mult))
                link(dve.memset(bias[0:CHUNK, :, S - CHUNK:S], -NEG))
        restart()
        with nc.Fori(0, DEPTH) as l:
            mixer_block(nc, l, T, args, cst, sem)
            restart()
            router_block(nc, l, T, args, cst, sem)
            restart()
            rounds = nc.values_load(T["rounds"][0:1, 0:1], min_val=1, max_val=MAX_ROUNDS)
            with nc.Fori(0, rounds):
                expert_block(nc, l, T, args, cst, sem)
                restart()

        with nc.sbuf_tensor("f_out", [P, TT, D], F32) as y, nc.sbuf_tensor("f_w", [P, D], F32) as fw, \
                nc.sbuf_tensor("f_ssq", [P, TT], F32) as ssq, nc.Block() as block:
            @block.sync
            def _(sp):
                sp.dma_start(fw[:], args["norm_final"].partition_broadcast(P)).then_inc(sem["small"], 16)
                for t in range(TT):
                    sp.wait_ge(sem["xn_ready"], t + 1)
                    sp.dma_start(ov[:, t, :], y[:, t, :]).then_inc(sem["y_stored"], 16)
                sp.wait_ge(sem["y_stored"], 16 * TT)

            @block.scalar
            def _(act):
                norm_square(act, x, y, ssq, sem["squares_done"])
                norm_root(act, ssq, sem)

            @block.vector
            def _(dve):
                link = chain(dve, sem["dve_chain"])
                dve.wait_ge(sem["small"], 16)
                norm_scale(dve, link, x, y, fw[:], ssq, sem)


_INPUTS = ["x", "w_in", "w_out", "norm_mix", "norm_ffn", "norm_final", "hgrn_lb", "hgrn_norm", "ret_norm",
           "rel_bias", "router_group", "router_expert", "expert_w_gate", "expert_w_up", "expert_w_down"]


def kernel(**inputs):
    import concourse.bacc as bacc
    from concourse.bass_utils import run_bass_kernel_spmd

    arrays = {n: np.ascontiguousarray(inputs[n]) for n in _INPUTS}
    arrays["hgrn_lb"] = np.ascontiguousarray(arrays["hgrn_lb"].reshape(DEPTH, 2, P).transpose(2, 0, 1))
    dist = (S - P) + np.arange(P)[:, None] - np.arange(S)[None, :]
    at = np.clip(dist, -MAX_REL, MAX_REL) + MAX_REL
    arrays["rel_bias"] = np.ascontiguousarray(arrays["rel_bias"][:, at].transpose(1, 0, 2))
    arrays["const"], arrays["trig"], arrays["masks"] = constants()

    nc = bacc.Bacc("TRN2", target_bir_lowering=False, num_devices=1)
    args = {n: nc.dram_tensor(f"in_{n}", a.shape, mybir.dt.from_np(a.dtype), kind="ExternalInput").ap()
            for n, a in arrays.items()}
    out = nc.dram_tensor("out", (1, S, D), F32, kind="ExternalOutput").ap()
    trunk(nc, args, out)
    r = run_bass_kernel_spmd(nc, [{f"in_{n}": a for n, a in arrays.items()}], core_ids=[0])
    return r.results[0]["out"]
```

```python
from contextlib import ExitStack

import numpy as np
import concourse.bass as bass
from concourse import mybir

F32 = mybir.dt.float32
F32R = mybir.dt.float32r
I32 = mybir.dt.int32
U32 = mybir.dt.uint32
U8 = mybir.dt.uint8
ALU = mybir.AluOpType
ACT = mybir.ActivationFunctionType
AX = mybir.AxisListType

P = 128
DEPTH, D, S = 2, 1024, 512
TT = S // P
KT = D // P
EPS = 1e-6
NEG = -1e30
MIN_FORGET = 1e-30

A_H, A_DK = 4, 64
AW = A_H * A_DK
B_H, B_DK, B_DV = 4, 48, 96
BW = B_H * B_DV
HALF = B_DK // 2
C_H, C_DH = 6, 64
CW = C_H * C_DH
CHUNK, MAX_REL = 64, 128
ROPE_BASE = 10000.0
D_IN = 4 * AW + 2 * B_H * B_DK + 2 * BW + 3 * CW

NG, EPG = 4, 8
NE = NG * EPG
DE = 512
FT = DE // P
CAP = 64
PAIRS = NE // 2
MAX_ROUNDS = S // CAP

LEVELS = 7
HQ = P // 2
N_MASKS = LEVELS * HQ + P

_o = np.cumsum([0, AW, AW, AW, AW, B_H * B_DK, B_H * B_DK, BW, BW, CW, CW, CW]).tolist()
GROUPS = [
    ("aq_af", _o[0], 2 * AW, True),
    ("ai_ag", _o[2], 2 * AW, False),
    ("cq", _o[8], CW, True),
    ("ck", _o[9], CW, True),
    ("cv", _o[10], CW, False),
    ("bq_bk", _o[4], 2 * B_H * B_DK, False),
    ("bv", _o[6], BW, False),
    ("bg", _o[7], BW, False),
    ("out_lo", 0, D // 2, False),
    ("out_hi", D // 2, D // 2, False),
]
N_IN = 8
RING = 4
AHEAD = 2
UNITS = KT * len(GROUPS)


def tiles_of(g):
    return GROUPS[g][2] // P if GROUPS[g][3] else TT


def bank_fills(g, i):
    return sum(1 for k in range(g) if tiles_of(k) > i)


CONST = {}
_n = 0
for _name, _w in [("ident", 128), ("stack", CAP), ("causal", 128), ("before", 128), ("ones", 128),
                  ("rows", 128), ("token", TT), ("experts", NE), ("groups", NG), ("limits", MAX_ROUNDS)]:
    CONST[_name] = (_n, _n + _w)
    _n += _w
N_CONST = _n


def constants():
    c = np.zeros((P, N_CONST), np.float32)

    def put(name, a):
        c[:, CONST[name][0]:CONST[name][1]] = a.reshape(P, -1)

    i = np.arange(P)
    put("ident", np.eye(P))
    put("stack", np.concatenate([np.eye(CAP)] * 2))
    put("causal", (i[None, :] >= i[:, None]))
    put("before", (i[:, None] < i[None, :]))
    put("ones", np.ones((P, P)))
    put("rows", np.tile(np.arange(CAP), (P, 2)))
    put("token", i[:, None] + P * np.arange(TT)[None, :])
    put("experts", np.tile(np.arange(NE), (P, 1)))
    put("groups", np.tile(np.arange(NG), (P, 1)))
    put("limits", np.tile(CAP * (1 + np.arange(MAX_ROUNDS)), (P, 1)))
    pos = np.arange(S, dtype=np.float32)
    inv = (np.float32(ROPE_BASE) ** (-np.arange(HALF, dtype=np.float32) / np.float32(HALF))).astype(np.float32)
    ang = (pos[:, None] * inv[None, :]).astype(np.float32).astype(np.float64)
    lg = np.log1p(-np.exp2(-5.0 - np.arange(B_H)))
    gq = np.exp(lg[None, :] * pos[:, None].astype(np.float64))
    gk = np.exp(-lg[None, :] * pos[:, None].astype(np.float64)) * B_DK ** -0.5
    f = np.concatenate([gq, gk], axis=1)[:, :, None]
    trig = [(f * tr[:, None, :]).reshape(TT, P, 8, HALF).transpose(1, 0, 2, 3).reshape(P, -1)
            for tr in (np.cos(ang), np.sin(ang))]
    masks = np.zeros((P, N_MASKS), np.float32)
    j, q = i[:, None], np.arange(HQ)[None, :]
    for n in range(LEVELS):
        h = 1 << n
        masks[:, HQ * n:HQ * n + HQ] = (j // (2 * h) == q // h) & (j % (2 * h) < h)
    masks[:, LEVELS * HQ:] = np.eye(P)
    return c, np.concatenate(trig, axis=1).astype(np.float32), masks


class Side:

    def __init__(self):
        self.at, self.fills, self.signals = {}, [0] * 4, [0] * 4

    def add(self, key, bank, signalled=True):
        self.fills[bank] += 1
        self.signals[bank] += signalled
        self.at[key] = (bank, self.fills[bank], self.signals[bank])


N_SLOT = UNITS - KT


def slot(g, kt):
    return (g - 1) * KT + kt


LV0 = 7
A_LEVEL = LV0 + 2
A_KEYS, A_STATE, A_OUT = LV0 + 10, LV0 + 12, LV0 + 14
C0 = slot(4, 7)
C_ITEMS = [(t, h) for t in range(TT) for h in range(C_H)]
B_ROT = slot(6, 1)
B_QKT, B_SC, B_STATE, B_OUT = slot(6, 3), slot(6, 5), slot(7, 1), slot(7, 3)
Y_TURN = [slot(7, 5)] * 2 + [slot(8, 1)] * 3 + [slot(8, 3)] * 3


def side_plan():
    s = Side()
    n = 0
    first = [("hT", i) for i in range(2 * TT)]
    first += [("level", lv, c) for lv in range(LEVELS + 1) for c in range(TT)]
    first += [("kdT", c) for c in range(TT - 1)] + [("aU", c) for c in range(TT - 1)]
    first += [("ao", c) for c in range(TT)]
    for n, key in enumerate(first):
        s.add(key, n % 4)
    n = 0
    for sl in range(C0, N_SLOT):
        i = sl - C0
        keys = [("cT", i - 1)] if 0 <= i - 1 < len(C_ITEMS) else []
        keys += [("cs", i)] if 0 <= i < len(C_ITEMS) else []
        keys += [("bT", k) for k in range(4)] if sl == B_QKT else []
        keys += [("bs", c) for c in range(TT)] if sl == B_SC else []
        keys += [("bU", c) for c in range(TT - 1)] if sl == B_STATE else []
        keys += [("bo", c) for c in range(TT)] if sl == B_OUT else []
        keys += [("yT", k) for k in range(KT) if sl == Y_TURN[k]]
        for k in keys:
            s.add(k, n % 3)
            n += 1
        if 0 <= i - 2 < len(C_ITEMS) and C_ITEMS[i - 2][1] == 0:
            s.add(("co", C_ITEMS[i - 2][0]), 3, signalled=False)
    return s.at


def norm_square(act, T, t, squares, sem):
    act.activation(squares, T["x"][:, t, :], ACT.Square,
                   accum_out=T["scale"][:, t:t + 1]).then_inc(sem["squares_done"], 1)


def norm_root(act, T, sem):
    act.wait_ge(sem["mean_ready"], 1)
    act.activation(T["scale"][:], T["scale"][:], ACT.Sqrt).then_inc(sem["root_ready"], 1)


def norm_inverse(dve, T, sem):
    scale = T["scale"]
    dve.wait_ge(sem["squares_done"], TT)
    dve.tensor_scalar(scale[:], scale[:], 1.0 / D, EPS, ALU.mult, ALU.add).then_inc(sem["mean_ready"], 1)
    dve.wait_ge(sem["root_ready"], 1)
    dve.reciprocal(scale[:], scale[:])


def norm_scale(dve, T, xn, weight, sem):
    x, ssq = T["x"], T["scale"]
    for t in range(TT):
        dve.scalar_tensor_tensor(xn[:, t, :], x[:, t, :], ssq[:, t:t + 1], weight, ALU.mult,
                                 ALU.mult).then_inc(sem["xn_ready"], 1)


def chain(eng, sem):
    n = [0]

    def link(ins):
        n[0] += 1
        ins.then_inc(sem, 1)
        eng.wait_ge(sem, n[0])
    return link


def spread(ap, n):
    return ap.rearrange("p (o a) -> p o a", o=1).broadcast_to([P, n, ap.shape[1]])


def each(ap, n):
    return ap.rearrange("p (a o) -> p a o", o=1).broadcast_to([P, ap.shape[1], n])


def head_rows(h, n=64):
    return slice(64 * (h % 2), 64 * (h % 2) + n)


def tile_cols(t, f=0):
    return slice(S * f + P * t, S * f + P * t + P)


def halves(ap, n, upper):
    h = 1 << n
    return ap.rearrange("p (b w) -> p b w", w=2 * h)[:, :, h:2 * h] if upper else \
        ap.rearrange("p (b w) -> p b w", w=2 * h)[:, :, 0:h]


def score_place(h, c):
    return 2 * (c // 2) + h % 2, slice(P * (2 * (c % 2) + h // 2), P * (2 * (c % 2) + h // 2) + P)


def mixer_block(nc, l, T, args, cst, sem):
    x, bias, pz, side = T["x"], T["bias"], T["pz"], T["side"]
    plan = side_plan()
    win = args["w_in"].rearrange("l (p k) n -> l p k n", k=KT)
    wout = args["w_out"].rearrange("l (k p) n -> l p k n", k=KT)
    with ExitStack() as ctx:
        def sb(name, shape, dt=F32):
            return ctx.enter_context(nc.sbuf_tensor(name, [P] + shape, dt))

        raw = sb("raw", [2, KT, 512])
        w_hi = sb("w_hi", [RING, 512], F32R)
        w_lo = sb("w_lo", [RING, 512], F32R)
        a_hi = sb("a_hi", [KT, S], F32R)
        a_lo = sb("a_lo", [KT, S], F32R)
        y = sb("y", [TT, D])
        junk = sb("junk", [AW])
        norm_a = sb("norm_a", [AW])
        norm_b = sb("norm_b", [BW])
        lb = sb("lb", [2])
        omlb = sb("omlb", [2])
        glast = sb("glast", [2, TT])
        a_ms = sb("a_ms", [TT])
        b_mu = sb("b_mu", [TT * B_H])
        b_ms = sb("b_ms", [TT * B_H])
        nmax = sb("nmax", [len(C_ITEMS)])
        den = sb("den", [len(C_ITEMS)])
        rden = sb("rden", [len(C_ITEMS)])
        sa = sb("sa", [TT, 4 * P])

        arena = sb("arena", [16512])
        used = [0]

        def early(n):
            used[0] += n
            return arena[:, used[0] - n:used[0]]

        fa = early(2 * S)
        cum = early(2 * S)
        diff = [early(2 * S), early(2 * S)]
        qf = [early(2 * S), early(2 * S)]
        kf = [early(2 * S), early(2 * S)]
        qa = early(2 * S)
        ka = early(2 * S)
        aig = early(TT * 2 * AW).rearrange("p (t c) -> p t c", t=TT)
        kd = early(3 * AW).rearrange("p (t c) -> p t c", t=3)
        st_a = early(3 * AW).rearrange("p (t c) -> p t c", t=3)
        norm_w = arena[:, 15360:15360 + D]
        used[0] = 0
        cq = early(3 * S).rearrange("p (f t) -> p f t", f=3)
        ck = early(3 * S).rearrange("p (f t) -> p f t", f=3)
        cv = early(TT * CW).rearrange("p (t c) -> p t c", t=TT)
        pr = [early(S), early(S)]
        prT = [early(S), early(S)]
        zqk = early(TT * 8 * B_DK)
        rqk = early(TT * 8 * 64).rearrange("p (t h d) -> p t h d", t=TT, h=8)
        qkT = early(4 * S).rearrange("p (f t) -> p f t", f=4)
        bv = early(TT * BW).rearrange("p (t c) -> p t c", t=TT)
        trig = early(2 * TT * 8 * HALF)
        bg = trig.rearrange("p (t c) -> p t c", t=TT)
        st_b = early(3 * BW).rearrange("p (t c) -> p t c", t=3)

        block = ctx.enter_context(nc.Block())

        def evacuated(eng, g):
            for i in range(tiles_of(g)):
                eng.wait_ge(sem[f"pz_free{i}"], bank_fills(g, i) + 1)

        def bank_ready(eng, g, i):
            if i < tiles_of(g) - 1:
                eng.wait_ge(sem["bank_done"], sum(tiles_of(k) - 1 for k in range(g)) + i + 1)
            else:
                eng.wait_ge(sem["unit_done"], KT * (g + 1))

        def was_read(eng, key):
            bank, nth, _ = plan[key]
            eng.wait_ge(sem[f"side_free{bank}"], nth)

        def filled(eng, key):
            bank, _, nth = plan[key]
            eng.wait_ge(sem[f"side_full{bank}"], nth)
            return side[bank], sem[f"side_free{bank}"]

        def add_out(dve, g):
            col = GROUPS[g][1]
            for i in range(TT):
                bank_ready(dve, g, i)
                xs = x[:, i, col:col + 512]
                dve.tensor_tensor(xs, xs, pz[i][:], ALU.add).then_inc(sem[f"pz_free{i}"], 1)

        @block.sync
        def _(sp):
            sp.dma_start(norm_w, args["norm_mix"][l].partition_broadcast(P)).then_inc(sem["small"], 16)
            sp.dma_start(norm_a[:], args["hgrn_norm"][l].partition_broadcast(P)).then_inc(sem["small"], 16)
            sp.dma_start(norm_b[:], args["ret_norm"][l].partition_broadcast(P)).then_inc(sem["small"], 16)
            sp.dma_start(lb[:], T["lb_dram"][l]).then_inc(sem["small"], 16)
            for g, (_, col, width, _) in enumerate(GROUPS):
                if g >= 2:
                    sp.wait_ge(sem["lo_split"], KT * (g - 1))
                src = win[l, :, :, col:col + width] if g < N_IN else wout[l, :, :, col:col + width]
                sp.dma_start(raw[:, g % 2, :, 0:width], src).then_inc(sem[f"raw{g % 2}"], 16)
                if g == 2:
                    sp.dma_start(trig, args["trig"]).then_inc(sem["trig"], 16)

        @block.gpsimd
        def _(pool):
            for buffer in kf:
                last = pool.memset(buffer, 0.0)
            last.then_inc(sem["zeroed"], 1)
            pool.memset(st_a, 0.0)
            pool.memset(sa[:], 0.0).then_inc(sem["zeroed"], 1)
            for c in range(TT):
                pool.wait_ge(sem[f"side_full{plan[('ao', c)][0]}"], plan[("ao", c)][2])
            pool.memset(st_b, 0.0)
            pool.memset(rqk, 0.0).then_inc(sem["zeroed"], 1)

        @block.tensor
        def _(pe):
            ident = cst("ident")

            def fill(key):
                bank, nth, _ = plan[key]
                if nth > 1:
                    pe.wait_ge(sem[f"side_free{bank}"], nth - 1)
                return side[bank], sem[f"side_full{bank}"]

            def turn_y(kt):
                if kt < 5:
                    pe.wait_ge(sem["y_ready"], 1 if kt < 2 else 2)
                else:
                    was_read(pe, ("co", TT - 1))
                out, full = fill(("yT", kt))
                for t in range(TT):
                    last = pe.transpose(out[:, P * t:P * t + P], y[:, t, P * kt:P * kt + P], ident)
                last.then_inc(full, 1)

            def turn_rows(i):
                t, half = i // 2, i % 2
                out, full = fill(("hT", i))
                for k in range(4):
                    last = pe.transpose(out[:, P * k:P * k + P],
                                        y[:, t, :].rearrange("p (f k) -> p k f", k=KT)[:, 4 * half + k, :], ident)
                last.then_inc(full, 1)

            def unit(g, kt):
                u = g * KT + kt
                _, _, width, feature_major = GROUPS[g]
                if g == N_IN:
                    was_read(pe, ("yT", kt))
                pe.wait_ge(sem["lo_split"], u + 1)
                wh, wl = w_hi[:, u % RING, :], w_lo[:, u % RING, :]
                ah, al = a_hi[:, kt, :], a_lo[:, kt, :]
                for i in range(tiles_of(g)):
                    if kt == 0 and bank_fills(g, i):
                        pe.wait_ge(sem[f"pz_free{i}"], bank_fills(g, i))
                    c = slice(P * i, P * i + P)
                    if feature_major:
                        parts = [(wh[:, c], ah), (wh[:, c], al), (wl[:, c], ah)]
                        out = pz[i][:]
                    else:
                        parts = [(ah[:, c], wh[:, 0:width]), (ah[:, c], wl[:, 0:width]), (al[:, c], wh[:, 0:width])]
                        out = pz[i][:, 0:width]
                    for n, (a, b) in enumerate(parts):
                        last = pe.matmul(out, a, b, start=(kt == 0 and n == 0), stop=(kt == KT - 1 and n == 2))
                    if kt == KT - 1 and i < tiles_of(g) - 1:
                        last.then_inc(sem["bank_done"], 1)
                last.then_inc(sem["unit_done"], 1)

            def level(n):
                if n < LEVELS:
                    pe.wait_ge(sem["factors"], n + 1)
                k_, q_ = (kf[n % 2], qf[n % 2]) if n < LEVELS else (ka, qa)
                for k in range(4):
                    out, full = fill(("level", n, k))
                    for c in (2 * (k // 2), 2 * (k // 2) + 1):
                        for h in range(k % 2, A_H, 2):
                            r, cols = head_rows(h), tile_cols(c, h // 2)
                            if n < LEVELS:
                                i = 2 * (c % 2) + h // 2
                                to = out[:, HQ * i:HQ * i + HQ].rearrange("p (b w) -> p b w", w=1 << n)
                                last = pe.matmul(to, k_[r, cols], halves(q_[r, cols], n, True), start=True, stop=True)
                            else:
                                last = pe.matmul(out[:, score_place(h, c)[1]], k_[r, cols], q_[r, cols],
                                                 start=True, stop=True)
                    last.then_inc(full, 1)

            def turn_keys():
                pe.wait_ge(sem["factors"], LEVELS + 1)
                for c in range(TT - 1):
                    out, full = fill(("kdT", c))
                    for f in range(2):
                        last = pe.transpose(out[:, P * f:P * f + P], kf[1][:, tile_cols(c, f)], ident)
                    last.then_inc(full, 1)

            def update_a():
                evacuated(pe, 1)
                for c in range(TT - 1):
                    was_read(pe, ("kdT", c))
                    out, full = fill(("aU", c))
                    for f in range(2):
                        v = slice(P * f, P * f + P)
                        last = pe.matmul(out[:, v], kd[:, c, v], aig[:, c, v], start=True, stop=True)
                    last.then_inc(full, 1)

            def out_a():
                for c in range(TT):
                    for h in range(2):
                        was_read(pe, ("level", LEVELS, score_place(h, c)[0]))
                    if c:
                        was_read(pe, ("aU", c - 1))
                    out, full = fill(("ao", c))
                    for h in range(A_H):
                        if c and h % 2 == 0:
                            v = slice(64 * h, 64 * h + P)
                            pe.matmul(out[:, v], qf[1][:, tile_cols(c, h // 2)], st_a[:, c - 1, v],
                                      start=True, stop=False)
                        v = slice(64 * h, 64 * h + 64)
                        k, cols = score_place(h, c)
                        last = pe.matmul(out[:, v], sa[:, k, cols], aig[:, c, v], start=(c == 0),
                                         stop=(c == 0 or h % 2 == 1))
                    last.then_inc(full, 1)

            def turn_b():
                pe.wait_ge(sem["rotated"], 1)
                for k in range(4):
                    out, full = fill(("bT", k))
                    for t in range(TT):
                        last = pe.transpose(out[:, P * t:P * t + P],
                                            rqk[:, t, 2 * k:2 * k + 2, :].rearrange("p a b -> p (a b)"), ident)
                    last.then_inc(full, 1)

            def scores_b():
                for k in range(4):
                    was_read(pe, ("bT", k))
                for k in range(4):
                    out, full = fill(("bs", k))
                    for c in (2 * (k // 2), 2 * (k // 2) + 1):
                        for h in range(k % 2, B_H, 2):
                            r = head_rows(h, B_DK)
                            last = pe.matmul(out[:, score_place(h, c)[1]], qkT[r, 2 + h // 2, tile_cols(c)],
                                             qkT[r, h // 2, tile_cols(c)], start=True, stop=True)
                    last.then_inc(full, 1)

            def update_b():
                evacuated(pe, 6)
                for c in range(TT - 1):
                    out, full = fill(("bU", c))
                    for k in range(2):
                        v = slice(2 * B_DV * k, 2 * B_DV * (k + 1))
                        last = pe.matmul(out[:, v], rqk[:, c, 4 + 2 * k:6 + 2 * k, :].rearrange("p a b -> p (a b)"),
                                         bv[:, c, v], start=True, stop=True)
                    last.then_inc(full, 1)

            def out_b():
                for c in range(TT):
                    for h in range(2):
                        was_read(pe, ("bs", score_place(h, c)[0]))
                    if c:
                        was_read(pe, ("bU", c - 1))
                    out, full = fill(("bo", c))
                    for h in range(B_H):
                        if c and h % 2 == 0:
                            v = slice(B_DV * h, B_DV * (h + 2))
                            pe.matmul(out[:, v], qkT[:, h // 2, tile_cols(c)], st_b[:, c - 1, v],
                                      start=True, stop=False)
                        v = slice(B_DV * h, B_DV * (h + 1))
                        k, cols = score_place(h, c)
                        last = pe.matmul(out[:, v], sa[:, k, cols], bv[:, c, v], start=(c == 0),
                                         stop=(c == 0 or h % 2 == 1))
                    last.then_inc(full, 1)

            def attend_turn(i):
                t, h = C_ITEMS[i]
                pe.wait_ge(sem["exp_done"], i + 1)
                out, full = fill(("cT", i))
                for j in range(t + 1):
                    last = pe.transpose(out[:, P * j:P * j + P], pr[i % 2][:, P * j:P * j + P], ident)
                last.then_inc(full, 1)

            def attend_scores(i):
                t, h = C_ITEMS[i]
                if i == 0:
                    evacuated(pe, 2)
                    evacuated(pe, 3)
                r = head_rows(h)
                out, full = fill(("cs", i))
                pe.matmul(out[:, 0:P * (t + 1)], cq[r, h // 2, tile_cols(t)], ck[r, h // 2, 0:P * (t + 1)],
                          start=True, stop=True).then_inc(full, 1)

            def attend_values(i):
                t, h = C_ITEMS[i]
                if i == 0:
                    evacuated(pe, 4)
                was_read(pe, ("cT", i))
                if h == 0:
                    fill(("co", t))
                for j in range(t + 1):
                    last = pe.matmul(side[3][:, 64 * h:64 * h + 64], prT[i % 2][:, P * j:P * j + P],
                                     cv[:, j, 64 * h:64 * h + 64], start=(j == 0), stop=(j == t))
                last.then_inc(sem["pv_done"], 1)

            def side_work(sl):
                if 0 <= sl - A_LEVEL <= LEVELS:
                    level(sl - A_LEVEL)
                if sl == A_KEYS:
                    turn_keys()
                if sl == A_STATE:
                    update_a()
                if sl == A_OUT:
                    out_a()
                i = sl - C0
                if 0 <= i - 1 < len(C_ITEMS):
                    attend_turn(i - 1)
                if 0 <= i < len(C_ITEMS):
                    attend_scores(i)
                if sl == B_QKT:
                    turn_b()
                if sl == B_SC:
                    scores_b()
                if sl == B_STATE:
                    update_b()
                if sl == B_OUT:
                    out_b()
                for kt in range(KT):
                    if sl == Y_TURN[kt]:
                        turn_y(kt)
                if 0 <= i - 2 < len(C_ITEMS):
                    attend_values(i - 2)

            for i in range(2 * TT):
                pe.wait_ge(sem["xn_ready"], i // 2 + 1)
                turn_rows(i)
            for i in range(2 * TT):
                was_read(pe, ("hT", i))
            for g in range(len(GROUPS)):
                for kt in range(KT):
                    unit(g, kt)
                    if g:
                        side_work(slot(g, kt))

        @block.scalar
        def _(act):
            link = chain(act, sem["act_chain"])

            def hi_y(kt):
                src, _ = filled(act, ("yT", kt))
                act.copy(a_hi[:, kt, :], src[:]).then_inc(sem["aT_hi"], 1)

            def hi_rows(i):
                t, half = i // 2, i % 2
                src, _ = filled(act, ("hT", i))
                act.copy(a_hi[:, 4 * half:4 * half + 4, tile_cols(t)],
                         src[:].rearrange("p (k t) -> p k t", k=4)).then_inc(sem["aT_hi"], 1)

            def split(u):
                g, kt, width = u // KT, u % KT, GROUPS[u // KT][2]
                if kt == 0:
                    act.wait_ge(sem[f"raw{g % 2}"], 16 * (g // 2 + 1))
                if u >= RING:
                    act.wait_ge(sem["unit_done"], u - RING + 1)
                act.copy(w_hi[:, u % RING, 0:width], raw[:, g % 2, kt, 0:width]).then_inc(sem["hi_split"], 1)

            def evacuate(g):
                name = GROUPS[g][0]
                free = [sem[f"pz_free{i}"] for i in range(4)]
                if name == "aq_af":
                    for i in range(2):
                        bank_ready(act, g, i)
                        act.activation(qa[:, S * i:S * i + S], pz[i][:], ACT.Silu).then_inc(free[i], 1)
                    for i in range(2):
                        bank_ready(act, g, 2 + i)
                        act.activation(ka[:, S * i:S * i + S], pz[2 + i][:], ACT.Sigmoid, scale=-1.0)
                        act.activation(fa[:, S * i:S * i + S], pz[2 + i][:], ACT.Sigmoid).then_inc(free[2 + i], 1)
                if name == "ai_ag":
                    for i in range(TT):
                        bank_ready(act, g, i)
                        act.copy(aig[:, i, 0:AW], pz[i][:, 0:AW])
                        act.activation(aig[:, i, AW:2 * AW], pz[i][:, AW:2 * AW], ACT.Silu).then_inc(free[i], 1)
                if name == "cq":
                    act.wait_ge(sem["factors"], LEVELS + 1)
                    for i in range(3):
                        bank_ready(act, g, i)
                        act.mul(cq[:, i, :], pz[i][:], -C_DH ** -0.5).then_inc(free[i], 1)
                if name == "ck":
                    for c in range(TT):
                        was_read(act, ("ao", c))
                    for i in range(3):
                        bank_ready(act, g, i)
                        act.copy(ck[:, i, :], pz[i][:]).then_inc(free[i], 1)
                if name == "cv":
                    for i in range(TT):
                        bank_ready(act, g, i)
                        act.copy(cv[:, i, :], pz[i][:, 0:CW]).then_inc(free[i], 1)
                if name == "bq_bk":
                    for i in range(TT):
                        bank_ready(act, g, i)
                        act.copy(zqk[:, 384 * i:384 * i + 384], pz[i][:, 0:384]).then_inc(free[i], 1)
                if name == "bv":
                    for i in range(TT):
                        bank_ready(act, g, i)
                        act.copy(bv[:, i, :], pz[i][:, 0:BW]).then_inc(free[i], 1)
                if name == "bg":
                    act.wait_ge(sem["rotated"], 1)
                    for i in range(TT):
                        bank_ready(act, g, i)
                        act.activation(bg[:, i, :], pz[i][:, 0:BW], ACT.Silu).then_inc(free[i], 1)

            def side_work(sl):
                if sl == 3:
                    act.wait_ge(sem["f_ready"], 1)
                    link(act.activation(fa, fa, ACT.Sqrt))
                    act.activation(fa, fa, ACT.Ln).then_inc(sem["log_ready"], 1)
                n = sl - LV0
                if 0 <= n <= LEVELS:
                    act.wait_ge(sem["diff_ready"], n + 1)
                    act.activation(diff[n % 2], diff[n % 2], ACT.Exp, scale=2.0).then_inc(sem["decay_ready"], 1)
                    if n == LEVELS:
                        act.wait_ge(sem["factors"], LEVELS)
                        act.activation(diff[0], cum, ACT.Exp, scale=2.0).then_inc(sem["decay_ready"], 1)
                        act.activation(glast[:], cum.rearrange("p (f c t) -> p f c t", f=2, c=TT)[:, :, :, P - 1],
                                       ACT.Exp, scale=2.0).then_inc(sem["decay_ready"], 1)
                if sl == A_KEYS + 1:
                    for c in range(TT - 1):
                        src, free = filled(act, ("kdT", c))
                        act.copy(kd[:, c, :], src[:, 0:AW]).then_inc(free, 1)
                if sl == A_OUT + 1:
                    for c in range(TT):
                        src, free = filled(act, ("ao", c))
                        act.copy(y[:, c, 0:AW], src[:, 0:AW]).then_inc(free, 1)
                    for c in range(TT):
                        was_read(act, ("ao", c))
                        link(act.activation(junk[:], y[:, c, 0:AW], ACT.Square, accum_out=a_ms[:, c:c + 1]))
                    act.sem_inc(sem["a_squares"], 1)
                if sl == A_OUT + 3:
                    act.wait_ge(sem["a_mean"], 1)
                    act.activation(a_ms[:], a_ms[:], ACT.Sqrt).then_inc(sem["a_root"], 1)
                i = sl - C0
                if 0 <= i - 1 < len(C_ITEMS):
                    n = P * (C_ITEMS[i - 1][0] + 1)
                    src, free = filled(act, ("cT", i - 1))
                    if i - 1 >= 2:
                        act.wait_ge(sem["pv_done"], i - 2)
                    act.copy(prT[(i - 1) % 2][:, 0:n], src[:, 0:n]).then_inc(free, 1)
                if 0 <= i < len(C_ITEMS):
                    n = P * (C_ITEMS[i][0] + 1)
                    was_read(act, ("cs", i))
                    act.activation(pr[i % 2][:, 0:n], pr[i % 2][:, 0:n], ACT.Exp, bias=nmax[:, i:i + 1],
                                   scale=-1.0, accum_out=den[:, i:i + 1]).then_inc(sem["exp_done"], 1)
                if sl == B_QKT:
                    act.wait_ge(sem["y_ready"], 1)
                    for k in range(4):
                        src, free = filled(act, ("bT", k))
                        act.copy(qkT[:, k, :], src[:]).then_inc(free, 1)
                if sl == B_OUT:
                    for c in range(TT):
                        src, free = filled(act, ("bo", c))
                        act.copy(y[:, c, AW:AW + BW], src[:, 0:BW]).then_inc(free, 1)
                for kt in range(KT):
                    if sl == Y_TURN[kt]:
                        hi_y(kt)
                if sl == B_OUT + 3:
                    act.wait_ge(sem["b_mean"], 1)
                    act.activation(b_ms[:], b_ms[:], ACT.Sqrt).then_inc(sem["b_root"], 1)

            act.preload_act_table(ACT.Silu)
            for i in range(2 * TT):
                hi_rows(i)
            for u in range(AHEAD):
                split(u)
            for u in range(UNITS):
                if u + AHEAD < UNITS:
                    split(u + AHEAD)
                if u % KT == KT - 1 and u // KT < N_IN:
                    evacuate(u // KT)
                if u >= KT:
                    side_work(u - KT)
            for t in range(TT):
                act.wait_ge(sem[f"pz_free{t}"], bank_fills(len(GROUPS), t))
                norm_square(act, T, t, y[:, t, :], sem)
            norm_root(act, T, sem)

        @block.vector
        def _(dve):
            link = chain(dve, sem["dve_chain"])
            ones = cst("ones")

            def lo_y(kt):
                src, free = filled(dve, ("yT", kt))
                dve.wait_ge(sem["aT_hi"], 2 * TT + kt + 1)
                dve.tensor_tensor(a_lo[:, kt, :], src[:], a_hi[:, kt, :], ALU.subtract).then_inc(free, 1)

            def lo_rows(i):
                t, half = i // 2, i % 2
                src, free = filled(dve, ("hT", i))
                dve.wait_ge(sem["aT_hi"], i + 1)
                cols = a_hi[:, 4 * half:4 * half + 4, tile_cols(t)]
                dve.tensor_tensor(a_lo[:, 4 * half:4 * half + 4, tile_cols(t)],
                                  src[:].rearrange("p (k t) -> p k t", k=4), cols, ALU.subtract).then_inc(free, 1)

            def split(u):
                g, kt, width = u // KT, u % KT, GROUPS[u // KT][2]
                dve.wait_ge(sem["hi_split"], u + 1)
                dve.tensor_tensor(w_lo[:, u % RING, 0:width], raw[:, g % 2, kt, 0:width],
                                  w_hi[:, u % RING, 0:width], ALU.subtract).then_inc(sem["lo_split"], 1)

            def gates():
                evacuated(dve, 0)
                link(dve.tensor_scalar(qa, qa, A_DK ** -0.5, None, ALU.mult))
                for i in range(2):
                    c = slice(S * i, S * i + S)
                    link(dve.tensor_scalar(ka[:, c], ka[:, c], omlb[:, i:i + 1], None, ALU.mult))
                    link(dve.tensor_scalar(fa[:, c], fa[:, c], omlb[:, i:i + 1], lb[:, i:i + 1], ALU.mult, ALU.add))
                dve.tensor_scalar(fa, fa, MIN_FORGET, None, ALU.max).then_inc(sem["f_ready"], 1)

            def factors(n):
                dve.wait_ge(sem["decay_ready"], n + 1 if n < LEVELS else n + 3)
                if n >= 2:
                    filled(dve, ("level", n - 2, TT - 1))
                    dve.wait_ge(sem["factors"], n - 1)
                if n == 0:
                    dve.wait_ge(sem["zeroed"], 1)
                if n < LEVELS:
                    to, q, decay = (halves(a, n, True) for a in (qf[n % 2], qa, diff[n % 2]))
                    link(dve.tensor_tensor(to, q, decay, ALU.mult))
                    to, k, decay = (halves(a, n, False) for a in (kf[n % 2], ka, diff[n % 2]))
                    dve.tensor_tensor(to, k, decay, ALU.mult).then_inc(sem["factors"], 1)
                else:
                    link(dve.tensor_tensor(qf[n % 2], qa, diff[0], ALU.mult))
                    dve.tensor_tensor(kf[n % 2], ka, diff[1], ALU.mult).then_inc(sem["factors"], 1)

            def exponents(n):
                if n >= 2:
                    dve.wait_ge(sem["factors"], n - 1)
                out = diff[n % 2]
                if n == LEVELS:
                    src = cum.rearrange("p (b h) -> p b h", h=P)
                    dve.tensor_tensor(out.rearrange("p (b h) -> p b h", h=P),
                                      src[:, :, P - 1:P].broadcast_to([P, 2 * TT, P]), src,
                                      ALU.subtract).then_inc(sem["diff_ready"], 1)
                    return
                h = 1 << n
                src = cum.rearrange("p (b h) -> p b h", h=2 * h)
                out = out.rearrange("p (b h) -> p b h", h=2 * h)
                ref = src[:, :, h - 1:h].broadcast_to([P, S // h, h])
                link(dve.tensor_tensor(out[:, :, h:2 * h], src[:, :, h:2 * h], ref, ALU.subtract))
                dve.tensor_tensor(out[:, :, 0:h], ref, src[:, :, 0:h], ALU.subtract).then_inc(sem["diff_ready"], 1)

            def place(n):
                heads = sa[:].rearrange("p c (h q) -> p c h q", h=A_H)
                for c in range(TT):
                    src, free = filled(dve, ("level", n, c))
                    if n:
                        was_read(dve, ("level", n - 1, c))
                    if n < LEVELS:
                        w = 1 << n
                        mask = T["masks"][:, HQ * n:HQ * n + HQ].rearrange("p (o b w) -> p o b w", o=1, w=w)
                        to = heads[:, c, :, :].rearrange("p h (b w) -> p h b w", w=2 * w)[:, :, :, w:2 * w]
                        dve.copy_predicated(to, mask.broadcast_to([P, A_H, HQ // w, w]),
                                            src[:, 0:A_H * HQ].rearrange("p (h b w) -> p h b w", h=A_H, w=w)
                                            ).then_inc(free, 1)
                    else:
                        dve.copy_predicated(heads[:, c, :, :], spread(T["masks"][:, LEVELS * HQ:N_MASKS], A_H),
                                            src[:].rearrange("p (h q) -> p h q", h=A_H)).then_inc(free, 1)

            def states_a():
                for c in range(TT - 1):
                    src, free = filled(dve, ("aU", c))
                    if c:
                        was_read(dve, ("aU", c - 1))
                    for h in range(A_H):
                        r, v = head_rows(h), slice(64 * h, 64 * h + 64)
                        if c == 0:
                            last = dve.tensor_copy(st_a[r, 0, v], src[r, v])
                        else:
                            last = dve.scalar_tensor_tensor(st_a[r, c, v], st_a[r, c - 1, v],
                                                            glast[r, h // 2, c:c + 1], src[r, v], ALU.mult, ALU.add)
                    last.then_inc(free, 1)

            def finish_a():
                dve.wait_ge(sem["a_root"], 1)
                link(dve.reciprocal(a_ms[:], a_ms[:]))
                for c in range(TT):
                    last = dve.scalar_tensor_tensor(y[:, c, 0:AW], y[:, c, 0:AW], a_ms[:, c:c + 1], norm_a[:],
                                                    ALU.mult, ALU.mult)
                link(last)
                dve.tensor_tensor(y[:, :, 0:AW], y[:, :, 0:AW], aig[:, :, AW:2 * AW],
                                  ALU.mult).then_inc(sem["y_ready"], 1)

            def rotate():
                evacuated(dve, 5)
                dve.wait_ge(sem["trig"], 16)
                dve.wait_ge(sem["zeroed"], 3)
                z = zqk.rearrange("p (t h d) -> p t h d", t=TT, d=B_DK)
                z1, z2 = z[:, :, :, 0:HALF], z[:, :, :, HALF:B_DK]
                n = TT * 8 * HALF
                cos = trig[:, 0:n].rearrange("p (t h d) -> p t h d", t=TT, d=HALF)
                sin = trig[:, n:2 * n].rearrange("p (t h d) -> p t h d", t=TT, d=HALF)
                t1, t2 = (y[:, :, AW + k:AW + k + 8 * HALF].rearrange("p t (h d) -> p t h d", d=HALF)
                          for k in (0, 8 * HALF))
                link(dve.tensor_tensor(t1, z1, cos, ALU.mult))
                link(dve.tensor_tensor(t2, z2, sin, ALU.mult))
                link(dve.tensor_tensor(rqk[:, :, :, 0:HALF], t1, t2, ALU.subtract))
                link(dve.tensor_tensor(t1, z1, sin, ALU.mult))
                link(dve.tensor_tensor(t2, z2, cos, ALU.mult))
                dve.tensor_tensor(rqk[:, :, :, HALF:B_DK], t1, t2, ALU.add).then_inc(sem["rotated"], 1)

            def mask_b():
                filled(dve, ("ao", TT - 1))
                for c in range(TT):
                    src, free = filled(dve, ("bs", c))
                    dve.tensor_tensor(sa[:, c, :].rearrange("p (h q) -> p h q", h=B_H),
                                      src[:].rearrange("p (h q) -> p h q", h=B_H), spread(cst("causal"), B_H),
                                      ALU.mult).then_inc(free, 1)

            def states_b():
                for c in range(TT - 1):
                    src, free = filled(dve, ("bU", c))
                    if c:
                        was_read(dve, ("bU", c - 1))
                    for h in range(B_H):
                        r, v = head_rows(h), slice(B_DV * h, B_DV * (h + 1))
                        if c == 0:
                            last = dve.tensor_copy(st_b[r, 0, v], src[r, v])
                        else:
                            last = dve.tensor_tensor(st_b[r, c, v], st_b[r, c - 1, v], src[r, v], ALU.add)
                    last.then_inc(free, 1)

            def norm_heads_b():
                for c in range(TT):
                    was_read(dve, ("bo", c))
                yb = y[:, :, AW:AW + BW].rearrange("p t (h d) -> p t h d", h=B_H)
                mu = b_mu[:].rearrange("p (t h o) -> p t h o", t=TT, o=1)
                link(dve.tensor_reduce(b_mu[:].rearrange("p (t h) -> p t h", t=TT), yb, AX.X, ALU.add))
                link(dve.tensor_scalar(b_mu[:], b_mu[:], 1.0 / B_DV, None, ALU.mult))
                link(dve.tensor_tensor(yb, yb, mu.broadcast_to([P, TT, B_H, B_DV]), ALU.subtract))

            def spread_b():
                yb = y[:, :, AW:AW + BW].rearrange("p t (h d) -> p t h d", h=B_H)
                sq = zqk.rearrange("p (a d) -> p a d", d=B_DV)
                link(dve.tensor_tensor(sq.rearrange("p (t h) d -> p t h d", t=TT), yb, yb, ALU.mult))
                link(dve.tensor_reduce(b_ms[:], sq, AX.X, ALU.add))
                dve.tensor_scalar(b_ms[:], b_ms[:], 1.0 / B_DV, EPS, ALU.mult, ALU.add).then_inc(sem["b_mean"], 1)

            def finish_b():
                dve.wait_ge(sem["b_root"], 1)
                link(dve.reciprocal(b_ms[:], b_ms[:]))
                yb = y[:, :, AW:AW + BW]
                rs = b_ms[:].rearrange("p (t h o) -> p t h o", t=TT, o=1)
                yh = yb.rearrange("p t (h d) -> p t h d", h=B_H)
                link(dve.tensor_tensor(yh, yh, rs.broadcast_to([P, TT, B_H, B_DV]), ALU.mult))
                link(dve.tensor_tensor(yb, yb, spread(norm_b[:], TT), ALU.mult))

            def gate_b():
                yb = y[:, :, AW:AW + BW]
                evacuated(dve, 7)
                dve.tensor_tensor(yb, yb, bg, ALU.mult).then_inc(sem["y_ready"], 1)

            def attend_max(i):
                t, h = C_ITEMS[i]
                n = P * (t + 1)
                src, free = filled(dve, ("cs", i))
                if i >= 2:
                    filled(dve, ("cT", i - 2))
                dve.tensor_tensor_reduce(pr[i % 2][:, 0:n], src[:, 0:n], bias[:, h, 512 - n:512], 1.0, 3.0e38,
                                         ALU.add, ALU.min, nmax[:, i:i + 1]).then_inc(free, 1)

            def finish_c(t):
                dve.wait_ge(sem["pv_done"], C_H * (t + 1))
                d = slice(C_H * t, C_H * t + C_H)
                link(dve.reciprocal(rden[:, d], den[:, d]))
                dve.tensor_tensor(y[:, t, AW + BW:D].rearrange("p (h d) -> p h d", h=C_H),
                                  side[3][:, 0:CW].rearrange("p (h d) -> p h d", h=C_H),
                                  each(rden[:, d], C_DH), ALU.mult).then_inc(sem["side_free3"], 1)

            def side_work(sl):
                if sl == 2:
                    gates()
                if sl == 4:
                    dve.wait_ge(sem["log_ready"], 1)
                    for c in range(2 * TT):
                        v = slice(P * c, P * c + P)
                        last = dve.tensor_tensor_scan(cum[:, v], ones, fa[:, v], 0.0, ALU.mult, ALU.add)
                    link(last)
                n = sl - LV0
                if 0 <= n - 1 <= LEVELS:
                    factors(n - 1)
                if 0 <= n <= LEVELS:
                    exponents(n)
                if 0 <= sl - A_LEVEL - 1 <= LEVELS:
                    if sl == A_LEVEL + 1:
                        dve.wait_ge(sem["zeroed"], 2)
                    place(sl - A_LEVEL - 1)
                if sl == A_STATE + 1:
                    states_a()
                if sl == A_OUT + 2:
                    dve.wait_ge(sem["a_squares"], 1)
                    dve.tensor_scalar(a_ms[:], a_ms[:], 1.0 / AW, EPS, ALU.mult, ALU.add).then_inc(sem["a_mean"], 1)
                if sl == A_OUT + 4:
                    finish_a()
                i = sl - C0
                if 0 <= i < len(C_ITEMS):
                    attend_max(i)
                if 0 <= i - 3 < len(C_ITEMS) and C_ITEMS[i - 3][1] == C_H - 1:
                    finish_c(C_ITEMS[i - 3][0])
                if sl == B_ROT:
                    rotate()
                if sl == B_SC:
                    mask_b()
                if sl == B_STATE:
                    states_b()
                if sl == B_OUT + 1:
                    norm_heads_b()
                if sl == B_OUT + 2:
                    spread_b()
                if sl == B_OUT + 4:
                    finish_b()
                if sl == slot(8, 0):
                    gate_b()
                for kt in range(KT):
                    if sl == Y_TURN[kt]:
                        lo_y(kt)

            dve.wait_ge(sem["small"], 64)
            link(dve.tensor_scalar(omlb[:], lb[:], -1.0, 1.0, ALU.mult, ALU.add))
            norm_scale(dve, T, y, norm_w, sem)
            for i in range(2 * TT):
                lo_rows(i)
            for u in range(AHEAD):
                split(u)
            for u in range(UNITS):
                if u + AHEAD < UNITS:
                    split(u + AHEAD)
                if u >= KT:
                    side_work(u - KT)
                if u == (N_IN + 1) * KT - 2:
                    add_out(dve, N_IN)
            add_out(dve, len(GROUPS) - 1)
            norm_inverse(dve, T, sem)


MIXER_SEMS = (["small", "raw0", "raw1", "trig", "lo_split", "hi_split", "unit_done", "bank_done", "zeroed", "factors",
               "squares_done", "mean_ready", "root_ready", "xn_ready", "aT_hi", "act_chain", 
               "dve_chain", "f_ready", "log_ready", "diff_ready", "decay_ready", "a_squares", "a_mean",
               "a_root", "b_mean", "b_root", "rotated", "y_ready", "exp_done", "pv_done"]
              + [f"pz_free{i}" for i in range(4)] + [f"side_full{i}" for i in range(4)]
              + [f"side_free{i}" for i in range(4)])


def router_block(nc, l, T, args, cst, sem):
    pz, side = T["pz"], T["side"]
    with ExitStack() as ctx:
        def sb(name, shape, dt=F32):
            return ctx.enter_context(nc.sbuf_tensor(name, [P] + shape, dt))

        h = sb("h", [TT, D])
        hT = sb("hT", [KT, S])
        w_router = sb("w_router", [KT, NG + NE])
        ffn_w = sb("ffn_w", [D])
        lg = sb("lg", [TT, 8])
        gtop = sb("gtop", [TT, 8])
        gtop_i = sb("gtop_i", [TT, 8], U32)
        gidx = sb("gidx", [TT])
        pgrp = sb("pgrp", [TT, NG])
        psum_ = sb("psum_", [TT])
        picked = sb("picked", [TT, NG])
        penalty = sb("penalty", [TT, NG])
        le = sb("le", [TT, NE])
        etop = sb("etop", [TT, 8])
        etop_i = sb("etop_i", [TT, 8], U32)
        e2 = sb("e2", [TT])
        both = sb("both", [TT, NE])
        cumr = sb("cumr", [TT, NE])
        prod = sb("prod", [TT * 2, NE])
        over = sb("over", [MAX_ROUNDS])
        most = sb("most", [2])
        one, gate, rank = T["one"], T["gate"], T["rank"]
        e_f = T["expert"]
        block = ctx.enter_context(nc.Block())

        @block.sync
        def _(sp):
            sp.dma_start(ffn_w[:], args["norm_ffn"][l].partition_broadcast(P)).then_inc(sem["small"], 16)
            sp.dma_start(w_router[:, :, 0:NG],
                         args["router_group"].rearrange("l (p k) n -> l p k n", k=KT)[l]).then_inc(sem["small"], 16)
            sp.dma_start(w_router[:, :, NG:NG + NE],
                         args["router_expert"].rearrange("l (p k) n -> l p k n", k=KT)[l]).then_inc(sem["small"], 16)
            for n in range(2):
                first_load(sp, l, T, args, sem, n)
            for t in range(TT):
                sp.wait_ge(sem["xn_ready"], t + 1)
                sp.dma_start(T["h_dram"][P * t:P * t + P, :], h[:, t, :]).then_inc(sem["h_stored"], 16)
            for n in range(2, SLOTS):
                first_load(sp, l, T, args, sem, n)
            sp.wait_ge(sem["h_stored"], 16 * TT)

        @block.tensor
        def _(pe):
            ident = cst("ident")
            for i in range(2 * TT):
                t, half = i // 2, i % 2
                pe.wait_ge(sem["xn_ready"], t + 1)
                if i >= 4:
                    pe.wait_ge(sem["hT_ready"], i - 3)
                for k in range(4):
                    last = pe.transpose(side[i % 4][:, P * k:P * k + P],
                                        h[:, t, :].rearrange("p (f k) -> p k f", k=KT)[:, 4 * half + k, :], ident)
                last.then_inc(sem["hT_turned"], 1)
            pe.wait_ge(sem["small"], 48)
            for t in range(TT):
                pe.wait_ge(sem["hT_ready"], 2 * t + 2)
                for kt in range(KT):
                    last = pe.matmul(pz[t][:, 0:NG + NE], hT[:, kt, tile_cols(t)], w_router[:, kt, :],
                                     start=(kt == 0), stop=(kt == KT - 1))
                last.then_inc(sem["logits"], 1)
            pe.wait_ge(sem["both_ready"], 1)
            for t in range(TT):
                for n in range(t + 1):
                    last = pe.matmul(side[0][:, NE * t:NE * t + NE], cst("before") if n == 0 else cst("ones"),
                                     both[:, t if n == 0 else n - 1, :], start=(n == 0), stop=(n == t))
            for n in range(TT):
                last = pe.matmul(side[1][:, 0:NE], cst("ones"), both[:, n, :], start=(n == 0), stop=(n == TT - 1))
            last.then_inc(sem["counted"], 1)

        @block.scalar
        def _(act):
            act.preload_act_table(ACT.Exp)
            for i in range(2 * TT):
                t, half = i // 2, i % 2
                act.wait_ge(sem["hT_turned"], i + 1)
                act.copy(hT[:, 4 * half:4 * half + 4, tile_cols(t)],
                         side[i % 4][:].rearrange("p (k t) -> p k t", k=4)).then_inc(sem["hT_ready"], 1)
            act.wait_ge(sem["exp_args"], 1)
            act.activation(pgrp[:], pgrp[:], ACT.Exp).then_inc(sem["exps"], 1)
            act.wait_ge(sem["exp_args"], 2)
            act.activation(e2[:], e2[:], ACT.Exp).then_inc(sem["exps"], 1)

        @block.vector
        def _(dve):
            link = chain(dve, sem["dve_chain"])
            dve.wait_ge(sem["small"], 48)
            link(dve.memset(lg[:], NEG))
            norm_scale(dve, T, h, ffn_w[:], sem)
            for t in range(TT):
                dve.wait_ge(sem["logits"], t + 1)
                dve.tensor_copy(lg[:, t, 0:NG], pz[t][:, 0:NG])
                last = dve.tensor_copy(le[:, t, :], pz[t][:, NG:NG + NE])
            link(last)
            for t in range(TT):
                link(dve.max(gtop[:, t, :], lg[:, t, :]))
                last = dve.max_index(gtop_i[:, t, :], gtop[:, t, :], lg[:, t, :])
            link(last)
            link(dve.tensor_copy(gidx[:], gtop_i[:, :, 0]))
            dve.tensor_tensor(pgrp[:], lg[:, :, 0:NG], gtop[:, :, 0:1].broadcast_to([P, TT, NG]),
                              ALU.subtract).then_inc(sem["exp_args"], 1)
            link(dve.tensor_tensor(picked[:], spread(cst("groups"), TT), each(gidx[:], NG), ALU.is_equal))
            link(dve.tensor_scalar(penalty[:], picked[:], -1.0, -NEG, ALU.add, ALU.mult))
            lev = le[:].rearrange("p t (g e) -> p (t g) e", g=NG)
            link(dve.tensor_tensor(lev, lev, each(picked[:].rearrange("p t g -> p (t g)"), EPG), ALU.mult))
            link(dve.tensor_tensor(lev, lev, each(penalty[:].rearrange("p t g -> p (t g)"), EPG), ALU.add))
            for t in range(TT):
                link(dve.max(etop[:, t, :], le[:, t, :]))
                last = dve.max_index(etop_i[:, t, :], etop[:, t, :], le[:, t, :])
            link(last)
            dve.tensor_tensor(e2[:], etop[:, :, 1], etop[:, :, 0], ALU.subtract).then_inc(sem["exp_args"], 1)
            link(dve.tensor_copy(e_f[:], etop_i[:, :, 0:2]))
            link(dve.tensor_tensor(one[:], spread(cst("experts"), 2 * TT),
                                   each(e_f[:].rearrange("p t k -> p (t k)"), NE), ALU.is_equal))
            ov = one[:].rearrange("p (t k) e -> p t k e", k=2)
            dve.tensor_tensor(both[:], ov[:, :, 0, :], ov[:, :, 1, :], ALU.add).then_inc(sem["both_ready"], 1)
            for t in range(TT):
                last = dve.tensor_scalar(T["token_at"][:, 2 * t:2 * t + 2, :], one[:, 2 * t:2 * t + 2, :],
                                         cst("token")[:, t:t + 1], None, ALU.mult)
            link(last)
            dve.wait_ge(sem["exps"], 2)
            link(dve.tensor_reduce(psum_[:], pgrp[:], AX.X, ALU.add))
            link(dve.tensor_scalar(gidx[:], e2[:], 1.0, None, ALU.add))
            link(dve.tensor_tensor(psum_[:], psum_[:], gidx[:], ALU.mult))
            link(dve.reciprocal(gate[:, :, 0], psum_[:]))
            link(dve.tensor_tensor(gate[:, :, 1], gate[:, :, 0], e2[:], ALU.mult))
            dve.wait_ge(sem["counted"], 1)
            link(dve.tensor_copy(cumr[:].rearrange("p t e -> p (t e)"), side[0][:, 0:TT * NE]))
            for k in range(2):
                last = dve.tensor_tensor(prod[:].rearrange("p (t k) e -> p t k e", k=2)[:, :, k, :], ov[:, :, k, :],
                                         cumr[:], ALU.mult)
            link(last)
            link(dve.tensor_reduce(rank[:].rearrange("p t k -> p (t k)"), prod[:], AX.X, ALU.add))
            link(dve.tensor_reduce(most[:, 0:1], side[1][:, 0:NE], AX.X, ALU.max))
            link(dve.tensor_scalar(over[:], cst("limits"), most[:, 0:1], None, ALU.is_lt))
            link(dve.tensor_reduce(most[:, 1:2], over[:], AX.X, ALU.add))
            link(dve.tensor_scalar(T["rounds"][:], most[:, 1:2], 1.0, None, ALU.add))


ROUTER_SEMS = ["small", "h_stored", "xn_ready", "hT_ready", "hT_turned", "logits", "both_ready", "counted",
               "squares_done", "mean_ready", "root_ready", "exp_args", "exps", "dve_chain"]

UW = 1024
HEAD, BODY = 8, 12
E_RING = 4
SLOTS = 12
ON_POOL = (3, 9)


def place_of(par, j):
    return ((HEAD + BODY * par + j) // 2) % SLOTS


def ring_of(par, j):
    return (HEAD + BODY * par + j) % E_RING


def turn_at(par):
    return 1 if par else 8


def low_done(j):
    own = [k for k in range(j + 1) if (k in ON_POOL) == (j in ON_POOL)]
    return j in ON_POOL, len(own)


def expert_weights(args):
    return [args["expert_w_gate"].rearrange("l e (p k) n -> l e p (k n)", k=KT),
            args["expert_w_up"].rearrange("l e (p k) n -> l e p (k n)", k=KT),
            args["expert_w_down"].rearrange("l e (p k) n -> l e p (k n)", k=FT)]


def load_units(sp, l, T, args, sem, place, w, e, half):
    sp.dma_start(T["e_raw"][:, place, :], expert_weights(args)[w][l, e][:, 2 * UW * half:2 * UW * (half + 1)]
                 ).then_inc(sem[f"w{place}"], 16)


def first_load(sp, l, T, args, sem, n):
    if n < HEAD // 2:
        w, e = n // 2, 0
    else:
        b, j = divmod(2 * n - HEAD, BODY)
        w, e = j // 4, b + 1 if j < 8 else b
    load_units(sp, l, T, args, sem, n, w, e, n % 2)


def expert_block(nc, l, r, T, args, cst, sem):
    x, pz, pz_all, side = T["x"], T["pz"], T["pz_all"], T["side"]
    rank, gate, e_f = T["rank"], T["gate"], T["expert"]
    with ExitStack() as ctx:
        def sb(name, shape, dt=F32):
            return ctx.enter_context(nc.sbuf_tensor(name, [P] + shape, dt))

        raw = T["e_raw"]
        w_hi = sb("e_hi", [E_RING, UW], F32R)
        w_lo = sb("e_lo", [E_RING, UW], F32R)
        xg = sb("xg", [D])
        xs = sb("xs", [2, KT, P], F32R)
        hit = sb("hit", [2 * TT, P])
        idx = sb("idx", [PAIRS], I32)
        idx1 = sb("idx1", [1], I32)
        g_sb = sb("g_sb", [DE])
        u_sb = sb("u_sb", [DE])
        act_g = sb("act_g", [FT * CAP])
        hid = sb("hid", [FT * CAP])
        hs = sb("hs", [FT, P], F32R)
        y_low = sb("y_low", [D])
        y_sb = sb("y_sb", [D])
        inr = sb("inr", [2 * TT])
        tmp = sb("tmp", [2 * TT])
        wgt = sb("wgt", [2 * TT])
        row = sb("row", [2 * TT], I32)
        spare = raw[:].rearrange("p a (b d) -> p (a b) d", d=D)
        block = ctx.enter_context(nc.Block())
        y_rows = T["y_dram"].rearrange("(p s) d -> p s d", s=P)

        def wait_split(eng, b, j):
            on_pool, n = low_done(j)
            if on_pool:
                eng.wait_ge(sem["lo_pool"], len(ON_POOL) * b + n)
            else:
                eng.wait_ge(sem["lo_split"], (BODY - len(ON_POOL)) * b + (HEAD + n))

        def wait_used(eng, n):
            eng.wait_ge(sem["unit_done"], n + E_RING)

        @block.sync
        def _(sp):
            def load(par, j, w, e):
                load_units(sp, l, T, args, sem, place_of(par, j), w, e, (j // 2) % 2)

            def body(b, par):
                for j in range(0, BODY, 2):
                    for k in (j, j + 1):
                        wait_split(sp, b - 2, k)
                        sp.sem_inc(sem["sp_passed"], 1)
                    load(par, j, j // 4, b + 1 if j < 8 else b)

            with sp.If(r > 0):
                for n in range(SLOTS):
                    first_load(sp, l, T, args, sem, n)
            for j in range(2 * SLOTS - HEAD - BODY, BODY, 2):
                sp.wait_ge(sem["lo_split"], j + HEAD + BODY - 2 * SLOTS + 2)
                load(1, j, j // 4, 2 if j < 8 else 1)
            with sp.Fori(0, (NE - 4) // 2) as p:
                body(2 * p + 2, 0)
                body(2 * p + 3, 1)
            body(NE - 2, 0)
            for j in range(0, 4, 2):
                wait_split(sp, NE - 3, j)
                wait_split(sp, NE - 3, j + 1)
                load(1, j, 2, NE - 1)

        @block.gpsimd
        def _(pool):
            def gather(pair):
                column = idx[:, pair:pair + 1] if isinstance(pair, int) else idx[:, bass.ds(pair, 1)]
                pool.tensor_copy(idx1[:], column).then_inc(sem["idx_copied"], 1)
                pool.wait_ge(sem["idx_copied"], pair + 1)
                if not isinstance(pair, int):
                    pool.sem_inc(sem["pool_passed"], 1)
                pool.indirect_dma_start(xg[:], None, T["h_dram"], bass.IndirectOffsetOnAxis(ap=idx1[:, 0:1], axis=0)
                                        ).then_inc(sem["gathered"], 16)

            def body(b, par, pair=None):
                if pair is not None:
                    pool.wait_ge(sem["xg_turned"], 2 * pair)
                    gather(pair)
                for j in ON_POOL:
                    pool.wait_ge(sem["hi_split"], BODY * b + (HEAD + j + 1))
                    place, cols, r = place_of(par, j), slice(UW * (j % 2), UW * (j % 2) + UW), ring_of(par, j)
                    pool.tensor_tensor(w_lo[:, r, :], raw[:, place, cols], w_hi[:, r, :],
                                       ALU.subtract).then_inc(sem["lo_pool"], 1)

            pool.wait_ge(sem["idx_ready"], 1)
            gather(0)
            pool.wait_ge(sem["xg_turned"], 2)
            gather(1)
            body(0, 0)
            with pool.Fori(0, (NE - 4) // 2) as p:
                body(2 * p + 1, 1, p + 2)
                body(2 * p + 2, 0)
            body(NE - 3, 1)
            body(NE - 2, 0)
            pool.wait_ge(sem["hi_split"], BODY * (NE - 1) + HEAD + 4)
            pool.tensor_tensor(w_lo[:, ring_of(1, 3), :], raw[:, place_of(1, 3), UW:2 * UW], w_hi[:, ring_of(1, 3), :],
                               ALU.subtract).then_inc(sem["lo_pool"], 1)
            for par in range(2):
                pool.wait_ge(sem[f"y_stored{par}"], 16 * (PAIRS + 1))
            for n in range(2 * TT):
                pool.indirect_dma_start(spare[:, n, :], None, T["y_dram"],
                                        bass.IndirectOffsetOnAxis(ap=row[:, n:n + 1], axis=0)
                                        ).then_inc(sem[f"fetched{n}"], 16)
            pool.wait_ge(sem["combined"], 2 * TT)
            nums = sorted(sem[k].num for k in ["gathered"] + [f"fetched{n}" for n in range(2 * TT)])
            pool.dma_reset(range(nums[0], nums[-1] + 1))

        @block.tensor
        def _(pe):
            ident = cst("ident")

            def into(bank, par_x, j, r):
                for k in range(2):
                    kt = 2 * j + k
                    for n, w in enumerate((w_hi, w_lo)):
                        last = pe.matmul(pz[bank][:], xs[:, par_x, kt, :], w[:, r, 512 * k:512 * k + 512],
                                         start=(kt == 0 and n == 0), stop=(kt == KT - 1 and n == 1))
                last.then_inc(sem["unit_done"], 1)

            def down(f, r):
                for n, w in enumerate((w_hi, w_lo)):
                    for c in range(2):
                        last = pe.matmul(pz[2 + c][:], hs[:, f, :], w[:, r, 512 * c:512 * c + 512],
                                         start=(f == 0 and n == 0), stop=(f == FT - 1 and n == 1))
                last.then_inc(sem["unit_done"], 1)

            def sum_turn(b):
                pe.wait_ge(sem["g_copied"], b + 1)
                pe.wait_ge(sem["u_copied"], b + 1)
                for n, src in enumerate((g_sb, u_sb)):
                    for f in range(FT):
                        c = CAP * (FT * n + f)
                        last = pe.matmul(side[2][:, c:c + CAP], src[:].rearrange("p (f k) -> p k f", k=FT)[:, f, :],
                                         cst("stack"), start=True, stop=True)
                last.then_inc(sem["gu_turned"], 1)

            def body(b, par, pair=None, turns=True, final=False):
                pe.wait_ge(sem["xs_ready"], b + 2)
                pe.wait_ge(sem["g_copied"], b + 1)
                for j in range(8):
                    if j == 2:
                        sum_turn(b)
                    if j == turn_at(par):
                        turn(par)
                    if j == 7 and pair is not None:
                        pe.wait_ge(sem["gathered"], 16 * pair + 16)
                    wait_split(pe, b, j)
                    into(j // 4, 1 - par, j % 4, ring_of(par, j))
                if turns and turn_at(par) == 8:
                    turn(par)
                pe.wait_ge(sem["hs_ready"], b + 1)
                pe.wait_ge(sem["y_read"], b + 1)
                for j in range(8, BODY):
                    if final and j == BODY - 1:
                        sum_turn(b + 1)
                    wait_split(pe, b, j)
                    down(j - 8, ring_of(par, j))

            def turn(par):
                rows = slice(CAP * par, CAP * par + CAP)
                for kt in range(KT):
                    last = pe.transpose(side[par][:, CAP * kt:CAP * kt + CAP],
                                        xg[rows, :].rearrange("p (f k) -> p k f", k=KT)[:, kt, :], ident[rows, rows])
                last.then_inc(sem["xg_turned"], 1)

            pe.sem_inc(sem["unit_done"], E_RING)
            pe.wait_ge(sem["hit_ready"], 1)
            for n in range(2 * TT):
                last = pe.matmul(side[3][:, 0:NE], hit[:, n, :], T["token_at"][:, n, :], start=(n == 0),
                                 stop=(n == 2 * TT - 1))
            last.then_inc(sem["tokens_found"], 1)
            pe.wait_ge(sem["gathered"], 16)
            turn(0)
            turn(1)
            pe.wait_ge(sem["xs_ready"], 1)
            for j in range(HEAD):
                pe.wait_ge(sem["lo_split"], j + 1)
                into(j // 4, 0, j % 4, j % E_RING)
            body(0, 0, 1)
            with pe.Fori(0, (NE - 4) // 2) as p:
                body(2 * p + 1, 1)
                body(2 * p + 2, 0, p + 2)
            body(NE - 3, 1)
            body(NE - 2, 0, turns=False, final=True)
            pe.wait_ge(sem["hs_ready"], NE)
            pe.wait_ge(sem["y_read"], NE)
            for j in range(FT):
                wait_split(pe, NE - 1, j)
                down(j, ring_of(1, j))

        @block.scalar
        def _(act):
            def split(b, par, j):
                place, r = place_of(par, j), ring_of(par, j)
                if j % 2 == 0:
                    turn = (HEAD + BODY * par + j) // 2 // SLOTS + 1
                    act.wait_ge(sem[f"w{place}"], 8 * (b - par) + 16 * turn)
                wait_used(act, BODY * b + (HEAD + j + 1 - E_RING))
                act.copy(w_hi[:, r, :], raw[:, place, UW * (j % 2):UW * (j % 2) + UW]).then_inc(sem["hi_split"], 1)

            def tokens_high(e, par):
                act.wait_ge(sem["xg_turned"], e + 1)
                act.copy(xs[:, par, :, 0:CAP], side[par][:].rearrange("p (k s) -> p k s", k=KT)
                         ).then_inc(sem["xs_hi"], 1)

            def gate_out(e, n):
                wait_used(act, n)
                act.copy(g_sb[:], pz[0][:]).then_inc(sem["g_copied"], 1)

            def silu(e):
                act.wait_ge(sem["gu_turned"], e + 1)
                act.activation(act_g[:], side[2][:, 0:FT * CAP], ACT.Silu).then_inc(sem["silu_done"], 1)

            def low_rows(n):
                wait_used(act, n)
                act.copy(y_low[0:CAP, :], pz_all[CAP:P, 2:4, :].rearrange("p a b -> p (a b)")
                         ).then_inc(sem["low_copied"], 1)

            def store(e, pair, par):
                act.wait_ge(sem["y_read"], e + 2)
                rows = slice(CAP * par, CAP * par + CAP)
                act.dma_start(y_rows[pair][rows, :], y_sb[rows, :]).then_inc(sem[f"y_stored{par}"], 16)

            def body(b, par, pair=None, turns=True):
                for j in range(BODY):
                    split(b, par, j)
                    if j == 2 and pair is not None:
                        low_rows(BODY * b + HEAD)
                    if j == 4:
                        silu(b)
                    if j == 6 and pair is not None:
                        store(b - 1, pair, 1 - par)
                    if j == 7:
                        gate_out(b + 1, BODY * b + (HEAD + 4))
                    if j == turn_at(par) + 2 and turns:
                        tokens_high(b + 2, par)

            for par in range(2):
                act.sem_inc(sem[f"y_stored{par}"], 16)
            act.preload_act_table(ACT.Silu)
            for j in range(HEAD):
                if j == E_RING:
                    tokens_high(0, 0)
                    tokens_high(1, 1)
                if j % 2 == 0:
                    act.wait_ge(sem[f"w{j // 2}"], 16)
                if j >= E_RING:
                    wait_used(act, j + 1 - E_RING)
                act.copy(w_hi[:, j % E_RING, :], raw[:, j // 2, UW * (j % 2):UW * (j % 2) + UW]
                         ).then_inc(sem["hi_split"], 1)
            gate_out(0, 4)
            body(0, 0)
            with act.Fori(0, (NE - 4) // 2) as p:
                body(2 * p + 1, 1, p)
                body(2 * p + 2, 0, p)
            body(NE - 3, 1, PAIRS - 2)
            body(NE - 2, 0, PAIRS - 2, turns=False)
            silu(NE - 1)
            low_rows(BODY * (NE - 1) + HEAD)
            for j in range(FT):
                split(NE - 1, 1, j)
            low_rows(BODY * (NE - 1) + HEAD + FT)
            store(NE - 2, PAIRS - 1, 0)
            store(NE - 1, PAIRS - 1, 1)
            act.preload_act_table(ACT.Sqrt)
            for t in range(TT):
                act.wait_ge(sem["combined"], 2 * t + 2)
                norm_square(act, T, t, spare[:, 2 * TT + t, :], sem)
            norm_root(act, T, sem)

        @block.vector
        def _(dve):
            link = chain(dve, sem["dve_chain"])

            def split(b, par, j):
                r = ring_of(par, j)
                dve.wait_ge(sem["hi_split"], BODY * b + (HEAD + j + 1))
                dve.tensor_tensor(w_lo[:, r, :], raw[:, place_of(par, j), UW * (j % 2):UW * (j % 2) + UW],
                                  w_hi[:, r, :],
                                  ALU.subtract).then_inc(sem["lo_split"], 1)

            def tokens_low(e, par):
                dve.wait_ge(sem["xs_hi"], e + 1)
                dve.tensor_tensor(xs[:, par, :, CAP:P], side[par][:].rearrange("p (k s) -> p k s", k=KT),
                                  xs[:, par, :, 0:CAP], ALU.subtract).then_inc(sem["xs_ready"], 1)

            def up_out(n):
                wait_used(dve, n)
                dve.tensor_copy(u_sb[:], pz[1][:]).then_inc(sem["u_copied"], 1)

            def hidden(e):
                dve.wait_ge(sem["silu_done"], e + 1)
                dve.tensor_tensor(hid[:], act_g[:], side[2][:, FT * CAP:2 * FT * CAP], ALU.mult
                                  ).then_inc(sem["hid_chain"], 1)
                h3 = hid[:].rearrange("p (f s) -> p f s", f=FT)
                dve.wait_ge(sem["hid_chain"], 2 * e + 1)
                dve.tensor_copy(hs[:, :, 0:CAP], h3).then_inc(sem["hid_chain"], 1)
                dve.wait_ge(sem["hid_chain"], 2 * e + 2)
                dve.tensor_tensor(hs[:, :, CAP:P], h3, hs[:, :, 0:CAP], ALU.subtract).then_inc(sem["hs_ready"], 1)

            def result(e, pair, par):
                dve.wait_ge(sem[f"y_stored{par}"], 16 * pair + 16)
                dve.wait_ge(sem["low_copied"], e + 1)
                dve.tensor_tensor(y_sb[CAP * par:CAP * par + CAP, :],
                                  pz_all[0:CAP, 2:4, :].rearrange("p a b -> p (a b)"), y_low[0:CAP, :],
                                  ALU.add).then_inc(sem["y_read"], 1)

            def body(b, par, pair=None, turns=True):
                for j in range(BODY):
                    if j not in ON_POOL:
                        split(b, par, j)
                    if j == 4 and pair is not None:
                        result(b - 1, pair, 1 - par)
                    if j == 6:
                        hidden(b)
                    if j == turn_at(par) + 2 and turns:
                        tokens_low(b + 2, par)
                    if j == 10:
                        up_out(BODY * b + (HEAD + 8))

            dve.sem_inc(sem["y_read"], 1)
            rk = rank[:].rearrange("p t k -> p (t k)")
            dve.tensor_tensor(hit[:], spread(cst("rows"), 2 * TT), each(rk, P), ALU.is_equal).then_inc(sem["hit_ready"], 1)
            dve.wait_ge(sem["tokens_found"], 1)
            pairs = side[3][:, 0:NE].rearrange("p (e two) -> p two e", two=2)
            dve.tensor_copy(idx[0:CAP, :], pairs[0:CAP, 0, :])
            dve.tensor_copy(idx[CAP:P, :], pairs[CAP:P, 1, :]).then_inc(sem["idx_ready"], 1)
            for j in range(HEAD):
                if j == E_RING:
                    tokens_low(0, 0)
                    tokens_low(1, 1)
                dve.wait_ge(sem["hi_split"], j + 1)
                dve.tensor_tensor(w_lo[:, j % E_RING, :], raw[:, j // 2, UW * (j % 2):UW * (j % 2) + UW],
                                  w_hi[:, j % E_RING, :], ALU.subtract).then_inc(sem["lo_split"], 1)
            link(dve.tensor_scalar(inr[:], rk, 0.0, None, ALU.is_ge))
            link(dve.tensor_scalar(tmp[:], rk, float(CAP), None, ALU.is_lt))
            link(dve.tensor_tensor(inr[:], inr[:], tmp[:], ALU.mult))
            link(dve.tensor_tensor(wgt[:], gate[:].rearrange("p t k -> p (t k)"), inr[:], ALU.mult))
            link(dve.scalar_tensor_tensor(tmp[:], e_f[:].rearrange("p t k -> p (t k)"), float(CAP), rk,
                                          ALU.mult, ALU.add))
            link(dve.tensor_tensor(tmp[:], tmp[:], inr[:], ALU.mult))
            link(dve.tensor_copy(row[:], tmp[:]))
            link(dve.tensor_scalar(rk, rk, -float(CAP), None, ALU.add))
            up_out(HEAD)
            body(0, 0)
            with dve.Fori(0, (NE - 4) // 2) as p:
                body(2 * p + 1, 1, p)
                body(2 * p + 2, 0, p)
            body(NE - 3, 1, PAIRS - 2)
            body(NE - 2, 0, PAIRS - 2, turns=False)
            wait_used(dve, BODY * (NE - 1) + HEAD)
            hidden(NE - 1)
            result(NE - 2, PAIRS - 1, 0)
            for j in range(FT):
                if j not in ON_POOL:
                    split(NE - 1, 1, j)
            result(NE - 1, PAIRS - 1, 1)
            for n in range(2 * TT):
                dve.wait_ge(sem[f"fetched{n}"], 16)
                if n % 2:
                    dve.wait_ge(sem["combined"], n)
                xt = x[:, n // 2, :]
                dve.scalar_tensor_tensor(xt, spare[:, n, :], wgt[:, n:n + 1], xt, ALU.mult,
                                         ALU.add).then_inc(sem["combined"], 1)
            norm_inverse(dve, T, sem)


EXPERT_SEMS = (["lo_split", "lo_pool", "hi_split", "unit_done", "idx_ready", "idx_copied", "xg_turned", "gathered",
                "y_stored", "y_stored0", "y_stored1", "combined", "squares_done", "mean_ready", "root_ready", "hit_ready", "tokens_found", "xs_ready", "xs_hi",
                "g_copied", "u_copied", "gu_turned", "hs_ready", "y_read", "silu_done", "low_copied", "hid_chain",
                "dve_chain", "sp_passed", "pool_passed"])
LOAD_SEMS = [f"w{k}" for k in range(SLOTS)]


def trunk(nc, args, out):
    with ExitStack() as ctx:
        T = {}

        def sb(name, shape, dt=F32):
            T[name] = ctx.enter_context(nc.sbuf_tensor(name, [P] + shape, dt))
            return T[name]

        x = sb("x", [TT, D])
        bias = sb("bias", [C_H, S])
        const = sb("const", [N_CONST])
        sb("masks", [N_MASKS], U8)
        sb("one", [2 * TT, NE])
        sb("token_at", [2 * TT, NE])
        sb("expert", [TT, 2])
        sb("gate", [TT, 2])
        sb("rank", [TT, 2])
        sb("rounds", [1], I32)
        sb("scale", [TT])
        lbs = sb("lbs", [DEPTH, 2])
        lt = sb("lt", [3, 2])
        T["h_dram"] = nc.dram_tensor("h_rows", [S, D], F32, kind="Internal").ap()
        T["y_dram"] = nc.dram_tensor("expert_rows", [NE * CAP, D], F32, kind="Internal").ap()
        T["lb_dram"] = nc.dram_tensor("lower_bounds", [DEPTH, P, 2], F32, kind="Internal").ap()
        T["pz_all"] = ctx.enter_context(nc.psum_tensor("pz", [P, 4, 512], F32))
        side = ctx.enter_context(nc.psum_tensor("side", [P, 4, 512], F32))
        T["pz"] = [T["pz_all"][:, i, :] for i in range(4)]
        T["side"] = [side[:, i, :] for i in range(4)]

        def cst(name):
            a, b = CONST[name]
            return const[:, a:b]

        pool_sems = ["gathered"] + [f"fetched{n}" for n in range(2 * TT)]
        names = pool_sems + sorted((set(MIXER_SEMS) | set(ROUTER_SEMS) | set(EXPERT_SEMS) | {"ready", "x_loaded"})
                                   - set(pool_sems)) + LOAD_SEMS
        sem = {n: ctx.enter_context(nc.semaphore(n)) for n in names}
        numbers = range(min(s.num for s in sem.values()), max(s.num for s in sem.values()) + 1)

        def restart(loading=False):
            nc.all_engine_barrier(sems_to_clear=range(numbers[0], sem["w0"].num) if loading else numbers)

        xv = args["x"].rearrange("b (t p) d -> p (b t) d", p=P)
        ov = out.rearrange("b (t p) d -> p (b t) d", p=P)

        with nc.sbuf_tensor("masks_in", [P, N_MASKS], F32) as masks_in, \
                nc.sbuf_tensor("squares", [P, TT, D], F32) as squares, nc.Block() as block:
            @block.sync
            def _(sp):
                sp.dma_start(lbs[:], args["hgrn_lb"]).then_inc(sem["ready"], 16)
                sp.dma_start(x[:], xv).then_inc(sem["x_loaded"], 16)
                sp.dma_start(const[:], args["const"]).then_inc(sem["small"], 16)
                sp.dma_start(masks_in[:], args["masks"]).then_inc(sem["small"], 16)
                sp.dma_start(bias[:], args["rel_bias"]).then_inc(sem["raw0"], 16)
                sp.wait_ge(sem["f_ready"], 1)
                for n in range(DEPTH):
                    sp.dma_start(T["lb_dram"][n], lbs[:, n, :]).then_inc(sem["raw1"], 16)
                sp.wait_ge(sem["raw1"], 16 * DEPTH)
                sp.wait_ge(sem["small"], 32)

            @block.scalar
            def _(act):
                act.wait_ge(sem["exp_args"], 1)
                act.activation(lt[:, 0:2, :], lt[:, 0:2, :], ACT.Exp).then_inc(sem["exps"], 1)
                act.preload_act_table(ACT.Sqrt)
                act.wait_ge(sem["x_loaded"], 16)
                for t in range(TT):
                    norm_square(act, T, t, squares[:, t, :], sem)
                norm_root(act, T, sem)

            @block.vector
            def _(dve):
                link = chain(dve, sem["dve_chain"])
                dve.wait_ge(sem["ready"], 16)
                link(dve.tensor_tensor(lt[:, 2, :], lbs[:, 0, :], lbs[:, 1, :], ALU.max))
                dve.tensor_tensor(lt[:, 0, :], lbs[:, 0, :], lt[:, 2, :], ALU.subtract)
                dve.tensor_tensor(lt[:, 1, :], lbs[:, 1, :], lt[:, 2, :], ALU.subtract).then_inc(sem["exp_args"], 1)
                dve.wait_ge(sem["exps"], 1)
                link(dve.tensor_tensor(lt[:, 2, :], lt[:, 0, :], lt[:, 1, :], ALU.add))
                link(dve.reciprocal(lt[:, 2, :], lt[:, 2, :]))
                link(dve.memset(lbs[:, 0, :], 0.0))
                dve.tensor_tensor(lbs[:, 1, :], lt[:, 1, :], lt[:, 2, :], ALU.mult).then_inc(sem["f_ready"], 1)
                dve.wait_ge(sem["small"], 32)
                dve.tensor_copy(T["masks"][:], masks_in[:])
                dve.wait_ge(sem["raw0"], 16)
                link(dve.tensor_scalar(bias[:], bias[:], -1.0, None, ALU.mult))
                link(dve.memset(bias[0:CHUNK, :, S - CHUNK:S], -NEG))
                norm_inverse(dve, T, sem)
        restart()
        with nc.Fori(0, DEPTH) as l:
            mixer_block(nc, l, T, args, cst, sem)
            restart()
            with nc.sbuf_tensor("e_raw", [P, SLOTS, 2 * UW], F32) as T["e_raw"]:
                router_block(nc, l, T, args, cst, sem)
                restart(loading=True)
                rounds = nc.values_load(T["rounds"][0:1, 0:1], min_val=1, max_val=MAX_ROUNDS)
                with nc.Fori(0, rounds) as r:
                    expert_block(nc, l, r, T, args, cst, sem)
                    restart()

        with nc.sbuf_tensor("f_out", [P, TT, D], F32) as y, nc.sbuf_tensor("f_w", [P, D], F32) as fw, \
                nc.Block() as block:
            @block.sync
            def _(sp):
                sp.dma_start(fw[:], args["norm_final"].partition_broadcast(P)).then_inc(sem["small"], 16)
                for t in range(TT):
                    sp.wait_ge(sem["xn_ready"], t + 1)
                    sp.dma_start(ov[:, t, :], y[:, t, :]).then_inc(sem["y_stored"], 16)
                sp.wait_ge(sem["y_stored"], 16 * TT)

            @block.vector
            def _(dve):
                dve.wait_ge(sem["small"], 16)
                norm_scale(dve, T, y, fw[:], sem)


_INPUTS = ["x", "w_in", "w_out", "norm_mix", "norm_ffn", "norm_final", "hgrn_lb", "hgrn_norm", "ret_norm",
           "rel_bias", "router_group", "router_expert", "expert_w_gate", "expert_w_up", "expert_w_down"]


def kernel(**inputs):
    import concourse.bacc as bacc
    from concourse.bass_utils import run_bass_kernel_spmd

    arrays = {n: np.ascontiguousarray(inputs[n]) for n in _INPUTS}
    arrays["hgrn_lb"] = np.ascontiguousarray(arrays["hgrn_lb"].reshape(DEPTH, 2, P).transpose(2, 0, 1))
    dist = (S - P) + np.arange(P)[:, None] - np.arange(S)[None, :]
    at = np.clip(dist, -MAX_REL, MAX_REL) + MAX_REL
    arrays["rel_bias"] = np.ascontiguousarray(arrays["rel_bias"][:, at].transpose(1, 0, 2))
    arrays["const"], arrays["trig"], arrays["masks"] = constants()

    nc = bacc.Bacc("TRN2", target_bir_lowering=False, num_devices=1)
    args = {n: nc.dram_tensor(f"in_{n}", a.shape, mybir.dt.from_np(a.dtype), kind="ExternalInput").ap()
            for n, a in arrays.items()}
    out = nc.dram_tensor("out", (1, S, D), F32, kind="ExternalOutput").ap()
    trunk(nc, args, out)
    r = run_bass_kernel_spmd(nc, [{f"in_{n}": a for n, a in arrays.items()}], core_ids=[0])
    return r.results[0]["out"]
```
